# Optimizing a Trainium2 kernel written in Bass

```python
import math
import jax, jax.numpy as jnp
from jax import lax
import numpy as np

D_MODEL = 1024
BATCH = 1
SEQ = 512
DEPTH = 1

D_MIX = D_MODEL
DIFF_WIDTH = D_MIX // 2
DIFF_HEADS = 4
DIFF_QK_DIM = 64
DIFF_V_DIM = DIFF_WIDTH // DIFF_HEADS
NSA_WIDTH = D_MIX - DIFF_WIDTH
NSA_HEADS = 8
NSA_HEAD_DIM = NSA_WIDTH // NSA_HEADS
NSA_KV_HEADS = 2
NSA_GROUP = NSA_HEADS // NSA_KV_HEADS
CMP_BLOCK = 32
CMP_STRIDE = 16
CMP_HIDDEN = 256
SEL_BLOCK = 64
SEL_TOPK = 8
N_LOCAL_BLOCKS = 2
FORCE_BONUS = 1000.0
WINDOW = 512
Q_BLOCK = 128
SEL_Q_BLOCK = 32
RMS_EPS = 1e-6
NEG_BIG = -1e30

COL_DIFF_Q = DIFF_HEADS * 2 * DIFF_QK_DIM
COL_DIFF_K = DIFF_HEADS * 2 * DIFF_QK_DIM
COL_DIFF_V = DIFF_WIDTH
COL_DIFF_Z = DIFF_WIDTH
COL_NSA_Q = NSA_WIDTH
COL_NSA_KV = 6 * NSA_KV_HEADS * NSA_HEAD_DIM
COL_NSA_Z = NSA_WIDTH
COL_NSA_GATE = 3 * NSA_HEADS
IN_COLS = COL_DIFF_Q + COL_DIFF_K + COL_DIFF_V + COL_DIFF_Z + COL_NSA_Q + COL_NSA_KV + COL_NSA_Z + COL_NSA_GATE
IN_SPLITS = [int(v) for v in np.cumsum([COL_DIFF_Q, COL_DIFF_K, COL_DIFF_V, COL_DIFF_Z, COL_NSA_Q, COL_NSA_KV, COL_NSA_Z])]


def rms_norm(x, g):
    xf = x.astype(jnp.float32)
    r = lax.rsqrt(jnp.mean(xf * xf, axis=-1, keepdims=True) + RMS_EPS)
    return (xf * r).astype(x.dtype) * g

def alibi_slopes(n):
    return jnp.asarray([2.0 ** (-8.0 * (h + 1) / n) for h in range(n)], dtype=jnp.float32)

def diff_attention(q, k, v, lam, slopes):
    B, H, _, T, _ = q.shape
    dv = v.shape[-1]
    scale = DIFF_QK_DIM ** -0.5
    kpos = jnp.arange(T)

    def block(start):
        qb = lax.dynamic_slice_in_dim(q, start, Q_BLOCK, axis=3)
        s = jnp.einsum('bhcqd,bhckd->bhcqk', qb, k).astype(jnp.float32) * scale
        qpos = start + jnp.arange(Q_BLOCK)
        dist = (qpos[:, None] - kpos[None, :]).astype(jnp.float32)
        s = s - slopes[None, :, None, None, None] * dist
        s = jnp.where(dist >= 0, s, -jnp.inf)
        p = jax.nn.softmax(s, axis=-1)
        p = p[:, :, 0] - lam * p[:, :, 1]
        return jnp.einsum('bhqk,bhkd->bhqd', p.astype(v.dtype), v)

    out = lax.map(block, jnp.arange(T // Q_BLOCK) * Q_BLOCK)
    return out.transpose(1, 2, 0, 3, 4).reshape(B, H, T, dv)

def compress(kv, pos, w1, b1, w2):
    B, KVH, T, d = kv.shape
    n_cmp = (T - CMP_BLOCK) // CMP_STRIDE + 1
    idx = jnp.arange(n_cmp)[:, None] * CMP_STRIDE + jnp.arange(CMP_BLOCK)[None, :]
    blocks = kv[:, :, idx] + pos
    flat = blocks.reshape(B, KVH, n_cmp, CMP_BLOCK * d)
    return jax.nn.silu(flat @ w1 + b1) @ w2

def compressed_attention(q, kc, vc):
    T = q.shape[3]
    n_cmp = kc.shape[2]
    scale = NSA_HEAD_DIM ** -0.5
    s = jnp.einsum('bhgtd,bhcd->bhgtc', q, kc).astype(jnp.float32) * scale
    cend = jnp.arange(n_cmp) * CMP_STRIDE + CMP_BLOCK - 1
    valid = cend[None, :] <= jnp.arange(T)[:, None]
    p = jax.nn.softmax(jnp.where(valid, s, NEG_BIG), axis=-1)
    p = jnp.where(valid, p, 0.0)
    o = jnp.einsum('bhgtc,bhcd->bhgtd', p.astype(vc.dtype), vc)
    return o, p

def select_blocks(p_cmp):
    T, n_cmp = p_cmp.shape[3], p_cmp.shape[4]
    n_sb = T // SEL_BLOCK
    cstart = jnp.arange(n_cmp) * CMP_STRIDE
    sstart = jnp.arange(n_sb) * SEL_BLOCK
    overlap = ((cstart[:, None] < sstart[None, :] + SEL_BLOCK)
               & (cstart[:, None] + CMP_BLOCK > sstart[None, :])).astype(jnp.float32)
    imp = jnp.einsum('bhgtc,cs->bhts', p_cmp, overlap)
    blk_t = jnp.arange(T)[:, None] // SEL_BLOCK
    j = jnp.arange(n_sb)[None, :]
    valid = j <= blk_t
    forced = valid & ((j == 0) | (j >= blk_t - (N_LOCAL_BLOCKS - 1)))
    score = jnp.where(valid, imp, -1.0) + jnp.where(forced, FORCE_BONUS, 0.0)
    _, idx = lax.top_k(score, min(SEL_TOPK, n_sb))
    return idx

def selected_attention(q, k, v, sel_idx, slopes):
    B, KVH, G, T, d = q.shape
    n = sel_idx.shape[-1]
    scale = NSA_HEAD_DIM ** -0.5
    kb = k.reshape(B, KVH, T // SEL_BLOCK, SEL_BLOCK, d)
    vb = v.reshape(B, KVH, T // SEL_BLOCK, SEL_BLOCK, d)
    bi = jnp.arange(B)[:, None, None, None]
    hi = jnp.arange(KVH)[None, :, None, None]
    offs = jnp.arange(SEL_BLOCK)
    n_keys = n * SEL_BLOCK

    def chunk(start):
        qc = lax.dynamic_slice_in_dim(q, start, SEL_Q_BLOCK, axis=3)
        ic = lax.dynamic_slice_in_dim(sel_idx, start, SEL_Q_BLOCK, axis=2)
        kg = kb[bi, hi, ic].reshape(B, KVH, SEL_Q_BLOCK, n_keys, d)
        vg = vb[bi, hi, ic].reshape(B, KVH, SEL_Q_BLOCK, n_keys, d)
        kpos = (ic[..., None] * SEL_BLOCK + offs).reshape(B, KVH, SEL_Q_BLOCK, n_keys)
        qpos = start + jnp.arange(SEL_Q_BLOCK)
        dist = (qpos[None, None, :, None] - kpos).astype(jnp.float32)[:, :, None]
        s = jnp.einsum('bhgqd,bhqkd->bhgqk', qc, kg).astype(jnp.float32) * scale
        s = s - slopes[None, :, :, None, None] * dist
        s = jnp.where(dist >= 0, s, -jnp.inf)
        p = jax.nn.softmax(s, axis=-1)
        return jnp.einsum('bhgqk,bhqkd->bhgqd', p.astype(vg.dtype), vg)

    out = lax.map(chunk, jnp.arange(T // SEL_Q_BLOCK) * SEL_Q_BLOCK)
    return out.transpose(1, 2, 3, 0, 4, 5).reshape(B, KVH, G, T, d)

def window_attention(q, k, v, slopes):
    B, KVH, G, T, d = q.shape
    scale = NSA_HEAD_DIM ** -0.5
    span = WINDOW + Q_BLOCK
    kp = jnp.pad(k, ((0, 0), (0, 0), (WINDOW, 0), (0, 0)))
    vp = jnp.pad(v, ((0, 0), (0, 0), (WINDOW, 0), (0, 0)))

    def block(start):
        qb = lax.dynamic_slice_in_dim(q, start, Q_BLOCK, axis=3)
        kbk = lax.dynamic_slice_in_dim(kp, start, span, axis=2)
        vbk = lax.dynamic_slice_in_dim(vp, start, span, axis=2)
        qpos = start + jnp.arange(Q_BLOCK)
        kpos = start - WINDOW + jnp.arange(span)
        dist = (qpos[:, None] - kpos[None, :]).astype(jnp.float32)
        valid = (dist >= 0) & (dist < WINDOW) & (kpos[None, :] >= 0)
        s = jnp.einsum('bhgqd,bhkd->bhgqk', qb, kbk).astype(jnp.float32) * scale
        s = s - slopes[None, :, :, None, None] * dist
        s = jnp.where(valid, s, -jnp.inf)
        p = jax.nn.softmax(s, axis=-1)
        return jnp.einsum('bhgqk,bhkd->bhgqd', p.astype(vbk.dtype), vbk)

    out = lax.map(block, jnp.arange(T // Q_BLOCK) * Q_BLOCK)
    return out.transpose(1, 2, 3, 0, 4, 5).reshape(B, KVH, G, T, d)

def first_inputs(seed: int = 0) -> dict:
    key = jax.random.key(seed)
    ks = jax.random.split(key, 20)
    f32 = jnp.float32
    nrm = lambda k, shape, s: jax.random.normal(k, shape, f32) * s
    return {
        'x': nrm(ks[0], (BATCH, SEQ, D_MODEL), 1.0),
        'norm_g': 1.0 + nrm(ks[1], (DEPTH, D_MODEL), 0.02),
        'w_in': nrm(ks[2], (DEPTH, D_MODEL, IN_COLS), D_MODEL ** -0.5),
        'diff_q_norm_g': 1.0 + nrm(ks[3], (DEPTH, DIFF_QK_DIM), 0.02),
        'diff_k_norm_g': 1.0 + nrm(ks[4], (DEPTH, DIFF_QK_DIM), 0.02),
        'diff_lambda_q1': nrm(ks[5], (DEPTH, DIFF_QK_DIM), 0.1),
        'diff_lambda_k1': nrm(ks[6], (DEPTH, DIFF_QK_DIM), 0.1),
        'diff_lambda_q2': nrm(ks[7], (DEPTH, DIFF_QK_DIM), 0.1),
        'diff_lambda_k2': nrm(ks[8], (DEPTH, DIFF_QK_DIM), 0.1),
        'diff_subln_g': 1.0 + nrm(ks[9], (DEPTH, DIFF_V_DIM), 0.02),
        'nsa_q_norm_g': 1.0 + nrm(ks[10], (DEPTH, NSA_HEAD_DIM), 0.02),
        'nsa_k_norm_g': 1.0 + nrm(ks[11], (DEPTH, 3, NSA_HEAD_DIM), 0.02),
        'cmp_pos': nrm(ks[12], (DEPTH, 2, CMP_BLOCK, NSA_HEAD_DIM), 0.1),
        'cmp_w1': nrm(ks[13], (DEPTH, 2, CMP_BLOCK * NSA_HEAD_DIM, CMP_HIDDEN), (CMP_BLOCK * NSA_HEAD_DIM) ** -0.5),
        'cmp_b1': nrm(ks[14], (DEPTH, 2, CMP_HIDDEN), 0.01),
        'cmp_w2': nrm(ks[15], (DEPTH, 2, CMP_HIDDEN, NSA_HEAD_DIM), CMP_HIDDEN ** -0.5),
        'w_out': nrm(ks[16], (DEPTH, D_MIX, D_MODEL), D_MIX ** -0.5),
    }

def first_block(x, norm_g, w_in, diff_q_norm_g, diff_k_norm_g, diff_lambda_q1, diff_lambda_k1,
              diff_lambda_q2, diff_lambda_k2, diff_subln_g, nsa_q_norm_g, nsa_k_norm_g,
              cmp_pos, cmp_w1, cmp_b1, cmp_w2, w_out):
    B, T, _ = x.shape
    f32 = jnp.float32
    diff_slopes = alibi_slopes(DIFF_HEADS)
    nsa_slopes = alibi_slopes(NSA_HEADS).reshape(NSA_KV_HEADS, NSA_GROUP)
    for layer in range(DEPTH):
        lam_init = 0.8 - 0.6 * math.exp(-0.3 * layer)
        h = rms_norm(x, norm_g[layer])
        proj = h @ w_in[layer]
        dq, dk, dv, dz, nq, nkv, nz, ng = jnp.split(proj, IN_SPLITS, axis=-1)

        dq = rms_norm(dq.reshape(B, T, DIFF_HEADS, 2, DIFF_QK_DIM).transpose(0, 2, 3, 1, 4), diff_q_norm_g[layer])
        dk = rms_norm(dk.reshape(B, T, DIFF_HEADS, 2, DIFF_QK_DIM).transpose(0, 2, 3, 1, 4), diff_k_norm_g[layer])
        dv = dv.reshape(B, T, DIFF_HEADS, DIFF_V_DIM).transpose(0, 2, 1, 3)
        lam = (jnp.exp(jnp.sum(diff_lambda_q1[layer].astype(f32) * diff_lambda_k1[layer].astype(f32)))
               - jnp.exp(jnp.sum(diff_lambda_q2[layer].astype(f32) * diff_lambda_k2[layer].astype(f32)))
               + lam_init)
        o_diff = diff_attention(dq, dk, dv, lam, diff_slopes)
        o_diff = rms_norm(o_diff, diff_subln_g[layer]) * (1.0 - lam_init)
        o_diff = o_diff.transpose(0, 2, 1, 3).reshape(B, T, DIFF_WIDTH) * jax.nn.silu(dz)

        nq = rms_norm(nq.reshape(B, T, NSA_KV_HEADS, NSA_GROUP, NSA_HEAD_DIM).transpose(0, 2, 3, 1, 4),
                      nsa_q_norm_g[layer])
        nkv = nkv.reshape(B, T, 6, NSA_KV_HEADS, NSA_HEAD_DIM).transpose(2, 0, 3, 1, 4)
        kc = compress(nkv[0], cmp_pos[layer, 0], cmp_w1[layer, 0], cmp_b1[layer, 0], cmp_w2[layer, 0])
        vc = compress(nkv[1], cmp_pos[layer, 1], cmp_w1[layer, 1], cmp_b1[layer, 1], cmp_w2[layer, 1])
        kc = rms_norm(kc, nsa_k_norm_g[layer, 0])
        k_slc = rms_norm(nkv[2], nsa_k_norm_g[layer, 1])
        k_win = rms_norm(nkv[4], nsa_k_norm_g[layer, 2])
        o_cmp, p_cmp = compressed_attention(nq, kc, vc)
        sel_idx = select_blocks(p_cmp)
        o_slc = selected_attention(nq, k_slc, nkv[3], sel_idx, nsa_slopes)
        o_win = window_attention(nq, k_win, nkv[5], nsa_slopes)
        g = jax.nn.sigmoid(ng.astype(f32)).astype(x.dtype)
        g = g.reshape(B, T, 3, NSA_KV_HEADS, NSA_GROUP).transpose(2, 0, 3, 4, 1)[..., None]
        o_nsa = g[0] * o_cmp + g[1] * o_slc + g[2] * o_win
        o_nsa = o_nsa.transpose(0, 3, 1, 2, 4).reshape(B, T, NSA_WIDTH) * jax.nn.silu(nz)

        x = x + jnp.concatenate([o_diff, o_nsa], axis=-1) @ w_out[layer]
    return x


D_CONV = 512
CONV_K = 3
N_HEADS = 8
HEAD_DIM = 64
D_ATTN = N_HEADS * HEAD_DIM
N_IDX_HEADS = 8
IDX_DIM = 64
TOPK_MAX = 256
N_BUCKETS = 32
MAX_EXACT = 16
MAX_DISTANCE = 128
D_FF = -(-8 * D_MODEL // (3 * 256)) * 256
EPS = 1e-6

PROJ_SIZES = (
    D_CONV, D_CONV, D_CONV,
    D_ATTN, HEAD_DIM, HEAD_DIM,
    N_IDX_HEADS * IDX_DIM, IDX_DIM,
    N_IDX_HEADS,
    D_MODEL, D_MODEL,
)
N_PROJ = int(sum(PROJ_SIZES))
PROJ_SPLITS = [int(v) for v in np.cumsum(PROJ_SIZES)[:-1]]


def rms_norm_2(x, g):
    xf = x.astype(jnp.float32)
    y = xf * lax.rsqrt(jnp.mean(xf * xf, axis=-1, keepdims=True) + EPS)
    return (y * g.astype(jnp.float32)).astype(x.dtype)

def rel_bucket(dist):
    n = jnp.maximum(dist, 0)
    large = MAX_EXACT + (jnp.log(jnp.maximum(n, 1).astype(jnp.float32) / MAX_EXACT)
                         / math.log(MAX_DISTANCE / MAX_EXACT)
                         * (N_BUCKETS - MAX_EXACT)).astype(jnp.int32)
    large = jnp.minimum(large, N_BUCKETS - 1)
    return jnp.where(n < MAX_EXACT, n, large)

def short_conv_mixer(gate_b, gate_c, x_a, conv_w):
    u = gate_c * x_a
    rhs = conv_w[:, None, :].astype(u.dtype)
    y = lax.conv_general_dilated(u, rhs, window_strides=(1,), padding=[(CONV_K - 1, 0)],
                                 dimension_numbers=("NWC", "WIO", "NWC"),
                                 feature_group_count=D_CONV)
    return gate_b * y

def dsa_attention(q, k, v, iq, ik, iw, rel_bias):
    bsz, seq_len = q.shape[0], q.shape[1]
    k_top = min(TOPK_MAX, seq_len // 4)
    n_blk = seq_len // Q_BLOCK
    iw = iw * (N_IDX_HEADS ** -0.5 * IDX_DIM ** -0.5)
    s_pos = jnp.arange(seq_len, dtype=jnp.int32)
    t_blocks = s_pos.reshape(n_blk, Q_BLOCK)

    def to_blocks(a):
        return jnp.moveaxis(a.reshape(bsz, n_blk, Q_BLOCK, *a.shape[2:]), 1, 0)

    gather = jax.vmap(lambda arr, ind: arr[ind])

    def block_fn(args):
        q_b, iq_b, iw_b, t_b = args
        dots = jnp.einsum("bthd,bsd->bths", iq_b, ik)
        score = jnp.einsum("bth,bths->bts", iw_b, jax.nn.relu(dots)).astype(jnp.float32)
        causal = s_pos[None, :] <= t_b[:, None]
        score = jnp.where(causal[None], score, -jnp.inf)
        _, idx = lax.top_k(score, k_top)
        valid = idx <= t_b[None, :, None]
        k_sel = gather(k, idx)
        v_sel = gather(v, idx)
        logits = jnp.einsum("bthd,btkd->bhtk", q_b, k_sel).astype(jnp.float32) * (HEAD_DIM ** -0.5)
        bias = rel_bias[rel_bucket(t_b[None, :, None] - idx)]
        logits = logits + jnp.moveaxis(bias, -1, 1).astype(jnp.float32)
        logits = jnp.where(valid[:, None], logits, -jnp.inf)
        p = jax.nn.softmax(logits, axis=-1).astype(v.dtype)
        o = jnp.einsum("bhtk,btkd->bthd", p, v_sel)
        return o.reshape(bsz, Q_BLOCK, D_ATTN)

    out = lax.map(block_fn, (to_blocks(q), to_blocks(iq), to_blocks(iw), t_blocks))
    return jnp.moveaxis(out, 0, 1).reshape(bsz, seq_len, D_ATTN)

def second_inputs(seed: int = 0) -> dict:
    key = jax.random.key(seed)
    ks = jax.random.split(key, 16)
    f32 = jnp.float32
    nrm = lambda k, shape, scale: jax.random.normal(k, shape, f32) * scale
    return {
        "x": nrm(ks[0], (BATCH, SEQ, D_MODEL), 1.0),
        "g_mix": 1.0 + nrm(ks[1], (DEPTH, D_MODEL), 0.02),
        "w_in": nrm(ks[2], (DEPTH, D_MODEL, N_PROJ), D_MODEL ** -0.5),
        "b_gate": nrm(ks[3], (DEPTH, 2 * D_MODEL), 0.02),
        "conv_w": nrm(ks[4], (DEPTH, CONV_K, D_CONV), CONV_K ** -0.5),
        "w_branch_a": nrm(ks[5], (DEPTH, D_CONV, D_MODEL), D_CONV ** -0.5),
        "w_branch_b": nrm(ks[6], (DEPTH, D_ATTN, D_MODEL), D_ATTN ** -0.5),
        "w_out": nrm(ks[7], (DEPTH, D_MODEL, D_MODEL), D_MODEL ** -0.5),
        "rel_bias": nrm(ks[8], (N_BUCKETS, N_HEADS), 0.5),
        "g_ffn": 1.0 + nrm(ks[9], (DEPTH, D_MODEL), 0.02),
        "w_ffn_gate": nrm(ks[10], (DEPTH, D_MODEL, D_FF), D_MODEL ** -0.5),
        "w_ffn_up": nrm(ks[11], (DEPTH, D_MODEL, D_FF), D_MODEL ** -0.5),
        "w_ffn_down": nrm(ks[12], (DEPTH, D_FF, D_MODEL), D_FF ** -0.5),
        "g_final": 1.0 + nrm(ks[13], (D_MODEL,), 0.02),
    }

def second_block(x, g_mix, w_in, b_gate, conv_w, w_branch_a, w_branch_b, w_out, rel_bias,
              g_ffn, w_ffn_gate, w_ffn_up, w_ffn_down, g_final):
    bsz, seq_len, _ = x.shape
    for layer in range(DEPTH):
        h = rms_norm_2(x, g_mix[layer])
        proj = h @ w_in[layer]
        (c_b, c_c, c_x, q, k, v, iq, ik, iw, g_a, g_b) = jnp.split(proj, PROJ_SPLITS, axis=-1)
        y_a = short_conv_mixer(c_b, c_c, c_x, conv_w[layer]) @ w_branch_a[layer]
        attn = dsa_attention(q.reshape(bsz, seq_len, N_HEADS, HEAD_DIM), k, v,
                             iq.reshape(bsz, seq_len, N_IDX_HEADS, IDX_DIM), ik, iw, rel_bias)
        y_b = attn @ w_branch_b[layer]
        gates = jax.nn.sigmoid(jnp.concatenate([g_a, g_b], axis=-1) + b_gate[layer])
        merged = gates[..., :D_MODEL] * y_a + gates[..., D_MODEL:] * y_b
        x = x + merged @ w_out[layer]
        h2 = rms_norm_2(x, g_ffn[layer])
        x = x + (jax.nn.silu(h2 @ w_ffn_gate[layer]) * (h2 @ w_ffn_up[layer])) @ w_ffn_down[layer]
    return rms_norm_2(x, g_final)


def setup_inputs(seed=0):
    out = dict(first_inputs(seed))
    for name, value in second_inputs(seed + 1).items():
        if name != "x":
            out[name + "_2"] = value
    return out


def reference(
    x, norm_g, w_in, diff_q_norm_g, diff_k_norm_g, diff_lambda_q1, diff_lambda_k1,
    diff_lambda_q2, diff_lambda_k2, diff_subln_g, nsa_q_norm_g, nsa_k_norm_g, cmp_pos, cmp_w1,
    cmp_b1, cmp_w2, w_out, g_mix_2, w_in_2, b_gate_2, conv_w_2, w_branch_a_2, w_branch_b_2,
    w_out_2, rel_bias_2, g_ffn_2, w_ffn_gate_2, w_ffn_up_2, w_ffn_down_2, g_final_2,
):
    x = first_block(
        x, norm_g, w_in, diff_q_norm_g, diff_k_norm_g, diff_lambda_q1, diff_lambda_k1,
        diff_lambda_q2, diff_lambda_k2, diff_subln_g, nsa_q_norm_g, nsa_k_norm_g, cmp_pos,
        cmp_w1, cmp_b1, cmp_w2, w_out,
    )
    return second_block(
        x, g_mix_2, w_in_2, b_gate_2, conv_w_2, w_branch_a_2, w_branch_b_2, w_out_2, rel_bias_2,
        g_ffn_2, w_ffn_gate_2, w_ffn_up_2, w_ffn_down_2, g_final_2,
    )


_drawn_inputs = setup_inputs


def setup_inputs(seed=0):
    import zlib

    import numpy as np

    out = dict(_drawn_inputs(seed))
    spreads = {}
    factors = {'norm_g': 2.673,
     'diff_q_norm_g': 4.71,
     'diff_k_norm_g': 5.756,
     'diff_lambda_q1': 34.09,
     'diff_lambda_k2': 3.112,
     'diff_subln_g': 4.824,
     'nsa_q_norm_g': 8.0,
     'nsa_k_norm_g': 8.0,
     'cmp_pos': 3.667,
     'cmp_b1': 8.0,
     'g_mix_2': 2.696,
     'b_gate_2': 8.0,
     'g_ffn_2': 11.792,
     'g_final_2': 7.745,
     'rel_bias_2': 3.434}
    for name, (base, spread) in spreads.items():
        noise = np.random.default_rng([zlib.crc32(name.encode()), seed]).standard_normal(out[name].shape)
        drawn = base * np.exp(spread * noise) if base else spread * noise
        out[name] = __import__('jax').numpy.asarray(drawn.astype(out[name].dtype))
    for name, factor in factors.items():
        out[name] = (out[name] * factor).astype(out[name].dtype)
    return out
```

```python
import math
from contextlib import ExitStack

import concourse.bass as bass
import numpy as np
from concourse import mybir

P = 128
T = 512
D = 1024
NT = T // P
ND = D // P
DH = 64
DIFF_HEADS = 4
NSA_HEADS = 8
KVH = 2
GROUP = NSA_HEADS // KVH
CMP_BLOCK, CMP_STRIDE, CMP_HIDDEN = 32, 16, 256
NCMP = (T - CMP_BLOCK) // CMP_STRIDE + 1
NPAIR = CMP_BLOCK // 2
DSA_HEADS = 8
TOPK = min(256, T // 4)
BUCKETS, MAX_EXACT, MAX_DISTANCE = 32, 16, 128
DFF = 2816
NFF = DFF // P
EPS = 1e-6
LAM_INIT = 0.8 - 0.6 * math.exp(0.0)
BIG = 1e30
TAKEN = -3e38
BIASW = 640

C_DQ, C_DK, C_DV, C_DZ, C_NQ, C_KV, C_NZ, C_NG = 0, 512, 1024, 1536, 2048, 2560, 3328, 3840
C_CB, C_CC, C_CX, C_Q, C_K, C_V, C_IQ, C_IK, C_IW, C_GA, C_GB = (
    0, 512, 1024, 1536, 2048, 2112, 2176, 2688, 2752, 2760, 3784)

R_NORM, R_MIX, R_FFN, R_BGATE, R_CONV, R_B1, R_POS = 0, 8, 16, 24, 40, 52, 56
R_GDQ, R_GDK, R_GNQ, R_GKC, R_GKS, R_GKW = 88, 89, 90, 91, 92, 93
NROWS = 94
N_SMALL = 25
K_IDENT, K_ONES, K_MASK, K_CMASK, K_CVALID, K_END = 0, 128, 256, 768, 896, 1024


def shape_constants():
    p = np.arange(P)[:, None]
    x = np.arange(T)[None, :]
    dist = (T - P) + p - x
    mask = np.where(dist < 0, BIG, 0.0)
    ones = np.kron(np.eye(2), np.ones((DH, DH)) / DH)
    c = np.arange(32)[None, None, :]
    t = np.arange(P)[:, None, None] + P * np.arange(NT)[None, :, None]
    ok = (c * CMP_STRIDE + CMP_BLOCK - 1 <= t) & (c < NCMP)
    const = np.concatenate([np.eye(P), ones, mask, np.where(ok, 0.0, BIG).reshape(P, -1),
                            np.where(ok, 1.0, 0.0).reshape(P, -1)], 1).astype(np.float32)
    distance = np.maximum(dist, 0).astype(np.float32)
    n = np.arange(BIASW) - (P - 1)
    large = MAX_EXACT + np.floor(np.log(np.maximum(n, 1) / MAX_EXACT) / math.log(MAX_DISTANCE / MAX_EXACT)
                                 * (BUCKETS - MAX_EXACT) + 1e-9).astype(np.int64)
    bucket = np.where(n < MAX_EXACT, n, np.minimum(large, BUCKETS - 1))
    onehot = ((np.arange(BUCKETS)[:, None] == bucket[None, :]) & ((n >= 0) & (n < T))[None, :]).astype(np.float32)
    return const, distance, onehot


class Unit:

    def __init__(self, name, parts, nk, width, tiles=None, k0=0, evac=None, first=True, last=True, raw=False,
                 aux=0, act=False):
        self.name, self.parts, self.nk, self.width = name, parts, nk, width
        self.tiles, self.k0, self.evac = tiles, k0, evac
        self.first, self.last, self.raw, self.aux, self.act = first, last, raw, aux, act


def build(nc, a, out):
    F32, F32R = mybir.dt.float32, mybir.dt.float32r
    ACT, ALU, AX = mybir.ActivationFunctionType, mybir.AluOpType, mybir.AxisListType

    def rows_of(w, r0, nk, c0, width):
        return w[r0 * P:(r0 + nk) * P, c0:c0 + width].rearrange("(k p) n -> p k n", p=P)

    steps = []

    def feature_units(name, w, c0, n, evac, aux=0, first_index=0):
        for j in range(n):
            steps.append(("unit", Unit(name, [(rows_of(w, 0, ND, c0 + 256 * j, 256), 0, 256)], ND, 256,
                                       tiles=[(0, P, evac, first_index + 2 * j), (P, P, evac, first_index + 2 * j + 1)],
                                       aux=aux)))

    def token_units(name, w, c0, evac, half, ktiles=ND, act=False):
        starts = list(range(0, ktiles, 4))
        for s in starts:
            nk = min(4, ktiles - s)
            steps.append(("unit", Unit(name, [(rows_of(w, s, nk, c0, 512), 0, 512)], nk, 512, k0=s,
                                       evac=(evac, half), first=s == 0, last=s == starts[-1], act=act)))

    w1in, w2in = a["w_in"][0], a["w_in_2"][0]
    steps.append(("transpose", dict(norm=True, gain=R_NORM, n=ND)))
    feature_units("diff_q", w1in, C_DQ, 2, "norm_dq", aux=2)
    feature_units("diff_k", w1in, C_DK, 2, "norm_dk", aux=2)
    feature_units("nsa_q", w1in, C_NQ, 2, "norm_nq", aux=2)
    steps.append(("unit", Unit("nsa_k", [(rows_of(w1in, 0, ND, C_KV + 256, 128), 0, 128),
                                         (rows_of(w1in, 0, ND, C_KV + 512, 128), 128, 128)], ND, 256,
                               tiles=[(0, P, "norm_kd", 0), (P, P, "norm_kd", 1)], aux=2)))
    steps.append(("unit", Unit("cmp_kv", [(rows_of(w1in, 0, ND, C_KV, 256), 0, 256)], ND, 256,
                               tiles=[(0, P, "cmp", 0), (P, P, "cmp", 1)])))
    steps.append(("unit", Unit("nsa_v", [(rows_of(w1in, 0, ND, C_KV + 384, 128), 0, 128),
                                         (rows_of(w1in, 0, ND, C_KV + 640, 128), 128, 128)], ND, 256,
                               tiles=[(0, P, "vd", 0), (P, P, "vd", 1)], aux=2)))
    steps.append(("unit", Unit("nsa_gate", [(rows_of(w1in, 0, ND, C_NG - 96, 120), 0, 120)], ND, 120,
                               tiles=[(0, 120, "ng", 0)], aux=1)))
    for kv in range(2):
        for half in range(2):
            w1 = a["cmp_w1"][0, kv].rearrange("(q p) n -> p q n", p=P)
            steps.append(("unit", Unit("cmp_w1", [(w1[:, 8 * half:8 * half + 8, :], 0, CMP_HIDDEN)], 8, CMP_HIDDEN,
                                       k0=8 * half, evac=("hidden", kv), first=half == 0, last=half == 1, raw=True)))
    token_units("diff_v", w1in, C_DV, "dv", 0)
    token_units("diff_z", w1in, C_DZ, "z", 0)
    token_units("nsa_z", w1in, C_NZ, "z", 1)
    steps.append(("attention_1", None))
    steps.append(("transpose", dict(norm=False, gain=None, n=ND)))
    token_units("out_1", a["w_out"][0], 0, "residual", 0)
    token_units("out_1", a["w_out"][0], 512, "residual", 1)
    steps.append(("bias_rows", None))
    steps.append(("transpose", dict(norm=True, gain=R_MIX, n=ND)))
    feature_units("index_q", w2in, C_IQ, 2, "iq")
    steps.append(("unit", Unit("k_ik_v_iw", [(rows_of(w2in, 0, ND, C_K, 64), 0, 64),
                                             (rows_of(w2in, 0, ND, C_IK, 64), 64, 64),
                                             (rows_of(w2in, 0, ND, C_V, 64), 128, 64),
                                             (rows_of(w2in, 0, ND, C_IW, 8), 192, 8)], ND, 200,
                               tiles=[(0, P, "kik", 0), (P, 72, "viw", 0)], aux=1)))
    steps.append(("index", None))
    feature_units("q", w2in, C_Q, 2, "q2")
    feature_units("conv_b", w2in, C_CB, 2, "cb")
    feature_units("conv_c", w2in, C_CC, 2, "cc")
    feature_units("conv_x", w2in, C_CX, 2, "cx")
    feature_units("gates_a", w2in, C_GA, 4, "gate", first_index=0)
    feature_units("gates_b", w2in, C_GB, 4, "gate", first_index=8)
    steps.append(("attention_2", None))
    steps.append(("transpose", dict(norm=False, gain=None, n=NT, branches=True)))
    for name, w, k0 in (("branch_a", a["w_branch_a_2"][0], 0), ("branch_b", a["w_branch_b_2"][0], 4)):
        for half in range(2):
            steps.append(("unit", Unit(name, [(rows_of(w, 0, 4, 512 * half, 512), 0, 512)], 4, 512, k0=k0,
                                       tiles=[(P * j, P, name, 4 * half + j) for j in range(4)])))
    steps.append(("merge", None))
    token_units("out_2", a["w_out_2"][0], 0, "residual", 0)
    token_units("out_2", a["w_out_2"][0], 512, "residual", 1)
    steps.append(("transpose", dict(norm=True, gain=R_FFN, n=ND)))
    steps.append(("ffn", None))
    FFN_STEPS = DFF // 256
    token_units("down", a["w_ffn_down_2"][0], 0, "residual", 0, ktiles=NFF, act=True)
    token_units("down", a["w_ffn_down_2"][0], 512, "residual", 1, ktiles=NFF, act=True)
    steps.append(("final", None))

    n_unit = n_split = n_tile = n_part = n_aux = n_h = n_act = n_res = n_sc = n_ve = n_branch = 0
    ring_in = [0, 0]
    plan = []
    released = []
    units = []
    for kind, body in steps:
        at = dict(unit=n_unit, split=n_split, tile=n_tile, part=n_part, aux=n_aux, h=n_h, act=n_act, res=n_res,
                  sc=n_sc, ve=n_ve)
        plan.append((kind, body, at))
        if kind == "unit":
            ntiles = len(body.tiles) if body.tiles else (0 if not body.last else (2 if body.raw else NT))
            body.n, body.tile, body.ntiles = n_unit, n_tile, ntiles
            ring_in[n_unit % 2] += 16 * len(body.parts)
            body.arrived = ring_in[n_unit % 2]
            n_unit += 1
            n_split += not body.raw
            body.split = n_split
            n_tile += ntiles
            if not body.tiles and not body.last:
                n_part += 1
            body.part = n_part
            body.tile_end = n_tile
            body.aux0 = n_aux
            n_aux += body.aux
            body.act0 = n_act
            n_act += body.act
            body.sc0, body.ve0, body.res0, body.branch0, x = n_sc, n_ve, n_res, n_branch, body.aux0
            for tile_kind in ([t[2] for t in body.tiles] if body.tiles else [body.evac[0]] * ntiles):
                if tile_kind.startswith("norm"):
                    x += 1
                    released.append(("aux_free", x))
                elif tile_kind in ("vd", "ng", "viw"):
                    x += 1
                    released.append(("aux_in", x))
                elif tile_kind in ("cmp", "kik"):
                    n_ve += 1
                    released.append(("ve_evac", n_ve))
                elif tile_kind == "residual":
                    n_res += 1
                    released.append(("res_done", n_res))
                elif tile_kind.startswith("branch"):
                    n_branch += 1
                    released.append(("branch_done", n_branch))
                else:
                    n_sc += 1
                    released.append(("sc_evac", n_sc))
            units.append(body)
        elif kind == "transpose":
            n_tile += body["n"]
            n_h += 4 if body.get("branches") else 0
            for _ in range(body["n"]):
                n_h += 1
                released.append(("h_lo_done", n_h))
        elif kind == "merge":
            n_h += ND
        elif kind == "bias_rows":
            n_tile += 2
            released += [("rows_done", 1), ("rows_done", 2)]
        elif kind == "ffn":
            ffn_slots = n_unit % 2, (n_unit + 1) % 2
            for _ in range(FFN_STEPS):
                for j in range(2):
                    ring_in[ffn_slots[j]] += 16
                    u = Unit("ffn", None, ND, 256)
                    n_tile += 2
                    n_split += 1
                    released += [("gsilu" if j == 0 else "act_done", 2 * _ + 1), ("gsilu" if j == 0 else "act_done", 2 * _ + 2)]
                    u.n, u.arrived, u.split, u.part, u.tile_end = n_unit, ring_in[ffn_slots[j]], n_split, n_part, n_tile
                    n_unit += 1
                    units.append(u)

    ctx = ExitStack()
    with ctx:
        def sb(name, shape, dt=F32):
            return ctx.enter_context(nc.sbuf_tensor(name, shape, dt))

        def sem(name):
            return ctx.enter_context(nc.semaphore(name))

        const = sb("const", [P, K_END])
        col = sb("col", [P, NROWS])
        onehot = sb("onehot", [BUCKETS, BIASW])
        relb = sb("relb", [BUCKETS, DSA_HEADS])
        lam_in = sb("lam_in", [P, 4, DH])
        gsub = sb("gsub", [P, P])
        cmp_w2 = sb("cmp_w2", [P, 2, 2, DH])
        raw = sb("raw", [P, 2, 2048])
        w_hi = sb("w_hi", [P, 2, 2048], F32R)
        w_lo = sb("w_lo", [P, 2, 2048], F32R)
        h_hi = sb("h_hi", [P, ND, T], F32R)
        h_lo = sb("h_lo", [P, ND, T], F32R)
        xres = sb("xres", [P, NT, D])
        zs = sb("zs", [P, NT, D])
        pool = sb("pool", [P, 18080])
        L = sb("L", [P, 4, T])
        PT = sb("PT", [P, 2, T])
        st = sb("st", [P, 256])
        hid = sb("hid", [P, 2, 2, 2 * NCMP])
        kc = sb("kc", [P, 2 * NCMP])
        kc_t = sb("kc_t", [P, 2 * NCMP])
        vc = sb("vc", [NCMP, KVH, DH])
        ngt = sb("ngt", [P, NT, 24])
        vec_rows = PT[0:NROWS, 0, 0:P]
        bias_row = L[0:DSA_HEADS, 0:2, :].rearrange("p a n -> p (a n)")

        ident = const[:, K_IDENT:K_IDENT + P]
        ones = const[:, K_ONES:K_ONES + P]
        mask = const[:, K_MASK:K_MASK + T]
        cmask = const[:, K_CMASK:K_CMASK + P].rearrange("p (i c) -> p i c", c=32)
        cvalid = const[:, K_CVALID:K_CVALID + P].rearrange("p (i c) -> p i c", c=32)

        def region(start, *shape):
            n = int(np.prod(shape))
            v = pool[:, start:start + n]
            if len(shape) == 2:
                v = v.rearrange("p (a b) -> p a b", b=shape[1])
            if len(shape) == 3:
                v = v.rearrange("p (a b c) -> p a b c", b=shape[1], c=shape[2])
            return v

        dq, dk, nq, dv = (region(2048 * j, 4, T) for j in range(4))
        kd = region(8192, 2, KVH, T)
        vd = region(10240, 2, NT, P)
        nsm = region(11264, 8, T)
        oacc = region(15360, NT, 512)
        flat = region(15360, 2, NPAIR, 2 * NCMP)
        zflat = zs[:, :, :].rearrange("p a b -> p (a b)")
        shifted = zflat[:, 0:2048].rearrange("p (a b c) -> p a b c", a=2, b=KVH)
        iq, q2 = region(0, 4, T), region(2048, 4, T)
        k2, ik2 = region(4096, T), region(4608, T)
        v2 = region(5120, NT, DH)
        iw = region(5376, NT, 8)
        work = region(5408, 1152)
        pm = region(6560, 1280)
        bh = region(7840, DSA_HEADS, T)
        cc, cx = region(11936, 4, T), region(13984, 4, T)
        osb = zflat[:, 0:2048].rearrange("p (i n) -> p i n", i=NT)
        ya = zflat[:, 2048:4096].rearrange("p (m n) -> p m n", m=4)

        def gate(j):
            o = 512 * j if j < 4 else 11936 + 512 * (j - 4)
            return pool[:, o:o + T]
        act = region(0, NFF, T)
        gfin = region(NFF * T, D)

        def causal_window(i):
            return slice(T - P - P * i, T)

        def work_of(i):
            o = {1: 0, 2: 256, 3: 640}[i]
            return work[:, o:o + P * (i + 1)]

        def pm_of(i):
            o = P * (i * (i + 1) // 2)
            return pm[:, o:o + P * (i + 1)]

        bank = [ctx.enter_context(nc.psum_tensor(f"bank{j}", [P, T], F32)) for j in range(8)]
        S_BANKS, T_BANKS, O_BANKS = [4, 5, 3], [6, 1], [7, 2]

        ST_MN, ST_SM, ST_R, ST_C = 0, 32, 64, 72
        ST_EPS, ST_NEGLAM, ST_SS, ST_RS, ST_RR, ST_LAM = 80, 81, 84, 88, 92, 96
        ST_CMN, ST_CSM, ST_TOP, ST_DSS = 100, 116, 132, 160
        eps = st[:, ST_EPS:ST_EPS + 1]
        neglam = st[:, ST_NEGLAM:ST_NEGLAM + 1]

        small_in = sem("small_in")
        x_in = [sem(f"x_in{i}") for i in range(NT)]
        raw_in = [sem("raw_in0"), sem("raw_in1")]
        hi_done, lo_done = sem("hi_done"), sem("lo_done")
        part_done, tile_done = sem("part_done"), sem("tile_done")
        sc_evac, ve_evac = sem("sc_evac"), sem("ve_evac")
        col_tr, col_done = sem("col_tr"), sem("col_done")
        setup_done, eps_done = sem("setup_done"), sem("eps_done")
        lam_dot, lam_exp, lam_done = sem("lam_dot"), sem("lam_exp"), sem("lam_done")
        squares, roots, recips, xn_done = sem("squares"), sem("roots"), sem("recips"), sem("xn_done")
        h_hi_done, h_lo_done = sem("h_hi_done"), sem("h_lo_done")
        aux_in, aux_done, aux_root, aux_free = sem("aux_in"), sem("aux_done"), sem("aux_root"), sem("aux_free")
        dve_step = sem("dve_step")
        s_done, lg_done, ex_done, p_done = sem("s_done"), sem("lg_done"), sem("ex_done"), sem("p_done")
        tr_done, pt_act, pt_dve = sem("tr_done"), sem("pt_act"), sem("pt_dve")
        pv_done, o_free = sem("pv_done"), sem("o_free")
        flat_done, hid_done, z_done = sem("flat_done"), sem("hid_done"), sem("z_done")
        epi_sq, epi_root, epi_done = sem("epi_sq"), sem("epi_root"), sem("epi_done")
        kc_mm, kc_sq, kc_avg, kc_root, kc_done = sem("kc_mm"), sem("kc_sq"), sem("kc_avg"), sem("kc_root"), sem("kc_done")
        c_s, c_lg, c_ex, c_p = sem("c_s"), sem("c_lg"), sem("c_ex"), sem("c_p")
        c_tr, c_pt, c_pv, c_o = sem("c_tr"), sem("c_pt"), sem("c_pv"), sem("c_o")
        attn_done = sem("attn_done")
        res_done = sem("res_done")
        rows_done, scratch_in, bias_in = sem("rows_done"), sem("scratch_in"), sem("bias_in")
        iq_done, ik_done = sem("iq_done"), sem("ik_done")
        ix_s, ix_relu, ix_acc, topk_done = sem("ix_s"), sem("ix_relu"), sem("ix_acc"), sem("topk_done")
        q2_done, conv_in, conv_done, gate_done = sem("q2_done"), sem("conv_in"), sem("conv_done"), sem("gate_done")
        branch_done = sem("branch_done")
        gsilu, act_done = sem("gsilu"), sem("act_done")
        a_hi_done, a_lo_done = sem("a_hi_done"), sem("a_lo_done")
        gfin_in, y_done, out_done = sem("gfin_in"), sem("y_done"), sem("out_done")

        bias_dram = nc.dram_tensor("bias_dram", [DSA_HEADS, BIASW], F32, kind="Internal").ap()

        def used(n):
            u = units[n]
            if u.name != "ffn" and not u.tiles and not u.last:
                return part_done, u.part
            return tile_done, u.tile_end

        frees = dict(aux_free=aux_free, aux_in=aux_in, ve_evac=ve_evac, res_done=res_done, branch_done=branch_done,
                     sc_evac=sc_evac, h_lo_done=h_lo_done, rows_done=rows_done, gsilu=gsilu, act_done=act_done)

        def slot(t, n, u):
            return t[:, n % 2, 0:u.nk * u.width].rearrange("p (k c) -> p k c", c=u.width)

        last_unit = len(units)
        down_units = [u for u in units if u.act]

        def jobs_1(which):
            jobs = []
            if which == "diff":
                for h in range(DIFF_HEADS):
                    for i in range(NT):
                        subs = [dict(q=dq[DH * c:DH * c + DH, h, P * i:P * i + P], k=dk[DH * c:DH * c + DH, h, :],
                                     bias=nsm[:, 2 * h + 1, :]) for c in range(2)]
                        jobs.append(dict(g=h, i=i, subs=subs, dv=P,
                                         v=[dv[:, j, P * h:P * h + P] for j in range(i + 1)]))
            if which == "nsa":
                for br in range(2):
                    for h in range(NSA_HEADS):
                        kv, r = h // GROUP, DH * (h % 2)
                        for i in range(NT):
                            subs = [dict(q=nq[r:r + DH, h // 2, P * i:P * i + P], k=kd[r:r + DH, br, kv, :],
                                         bias=nsm[:, h, :])]
                            jobs.append(dict(g=NSA_HEADS * br + h, i=i, subs=subs, dv=DH, h=h, br=br,
                                             v=[vd[:, br, j, DH * kv:DH * kv + DH] for j in range(i + 1)]))
            if which == "dsa":
                for h in range(DSA_HEADS):
                    r = DH * (h % 2)
                    for i in range(NT):
                        subs = [dict(q=q2[r:r + DH, h // 2, P * i:P * i + P], k=k2[r:r + DH, :],
                                     bias=bh[:, h, :], select=pm_of(i))]
                        jobs.append(dict(g=h, i=i, subs=subs, dv=DH, h=h, v=[v2[:, j, :] for j in range(i + 1)]))
            return jobs

        attention = {w: jobs_1(w) for w in ("diff", "nsa", "dsa")}
        sub_n = job_n = group_n = act_pt = dve_pt = 0
        for w in ("diff", "nsa", "dsa"):
            for j in attention[w]:
                j["r"], j["n"], j["G"] = sub_n, job_n, group_n + j["g"]
                j["by_act"] = j["i"] in (0, 3) or w == "diff"
                act_pt += j["by_act"]
                dve_pt += not j["by_act"]
                j["pt"] = (pt_act, act_pt) if j["by_act"] else (pt_dve, dve_pt)
                sub_n += len(j["subs"])
                job_n += 1
            group_n += attention[w][-1]["g"] + 1
        job_of_sub = [j for w in ("diff", "nsa", "dsa") for j in attention[w] for _ in j["subs"]]
        all_jobs = [j for w in ("diff", "nsa", "dsa") for j in attention[w]]
        GROUPS = {"diff": DIFF_HEADS, "nsa": 2 * NSA_HEADS, "dsa": DSA_HEADS}
        LAG = {"diff": 1, "nsa": 3, "dsa": 3}

        def stat(base, job, c):
            o = base + 8 * (job["G"] % 4) + 4 * c + job["i"]
            return st[:, o:o + 1]

        block = ctx.enter_context(nc.Block())

        @block.sync
        def _(sp):
            def load(u):
                if u.n >= 2:
                    before = units[u.n - 2]
                    if before.raw:
                        sp.wait_ge(*used(u.n - 2))
                    else:
                        sp.wait_ge(lo_done, before.split)
                for src, c0, width in u.parts:
                    sp.dma_start(slot(raw, u.n, u)[:, :, c0:c0 + width], src).then_inc(raw_in[u.n % 2], 16)

            for i in range(NT):
                sp.dma_start(xres[:, i, :], a["x"][0, P * i:P * i + P, :]).then_inc(x_in[i], 16)
            for kind, body, at in plan:
                if kind == "unit":
                    load(body)
                if kind == "ffn":
                    wg, wu = a["w_ffn_gate_2"][0], a["w_ffn_up_2"][0]
                    with sp.Fori(0, FFN_STEPS) as f:
                        for j, w in enumerate((wg, wu)):
                            sp.wait_ge(lo_done, f * 2 + (at["split"] - 1 + j))
                            sp.dma_start(raw[:, ffn_slots[j], :].rearrange("p (k c) -> p k c", c=256),
                                         w.rearrange("(k p) n -> p k n", p=P)[:, :, bass.ds(f * 256, 256)])\
                              .then_inc(raw_in[ffn_slots[j]], 16)
            sp.dma_start(gfin, a["g_final_2"].to_broadcast([P, D])).then_inc(gfin_in, 16)
            for i in range(NT):
                sp.wait_ge(y_done, i + 1)
                sp.dma_start(out[0, P * i:P * i + P, :], zs[:, i, :]).then_inc(out_done, 16)
            sp.wait_ge(out_done, 16 * NT)

        @block.gpsimd
        def _(pool_e):
            def split_lo(u):
                pool_e.wait_ge(hi_done, u.split)
                size = u.nk * u.width
                nc.gpsimd.tensor_tensor(w_lo[:, u.n % 2, 0:size], raw[:, u.n % 2, 0:size],
                                        w_hi[:, u.n % 2, 0:size].bitcast(F32), ALU.subtract).then_inc(lo_done, 1)

            for kind, body, at in plan:
                if kind == "unit" and not body.raw:
                    split_lo(body)
                if kind == "bias_rows":
                    pool_e.wait_ge(rows_done, 2)
                    pool_e.dma_start(bias_dram, bias_row[:, 0:BIASW]).then_inc(scratch_in, 16)
                    pool_e.wait_ge(scratch_in, 16)
                    pool_e.wait_ge(attn_done, 1)
                    pool_e.dma_start(bh, bass.AP(bias_dram.tensor, 0, [[1, P], [BIASW, DSA_HEADS], [1, T]]))\
                          .then_inc(bias_in, 16)
                if kind == "ffn":
                    with pool_e.Fori(0, FFN_STEPS) as f:
                        for j in range(2):
                            pool_e.wait_ge(hi_done, f * 2 + (at["split"] + 1 + j))
                            z = ffn_slots[j]
                            nc.gpsimd.tensor_tensor(w_lo[:, z, :], raw[:, z, :], w_hi[:, z, :].bitcast(F32),
                                                    ALU.subtract).then_inc(lo_done, 1)

        @block.scalar
        def _(sc):
            act_fn = nc.scalar.activation
            rows = [(R_NORM, a["norm_g"][0].rearrange("(r c) -> r c", c=P)),
                    (R_MIX, a["g_mix_2"][0].rearrange("(r c) -> r c", c=P)),
                    (R_FFN, a["g_ffn_2"][0].rearrange("(r c) -> r c", c=P)),
                    (R_BGATE, a["b_gate_2"][0].rearrange("(r c) -> r c", c=P)),
                    (R_CONV, a["conv_w_2"][0].rearrange("k (r c) -> (k r) c", c=P)),
                    (R_B1, a["cmp_b1"][0].rearrange("k (r c) -> (k r) c", c=P)),
                    (R_POS, a["cmp_pos"][0].rearrange("k (q b) d -> (k q) (b d)", b=2))]
            n_small = 0

            def small(dst, src):
                nonlocal n_small
                sc.dma_start(dst, src).then_inc(small_in, 16)
                n_small += 1

            small(const[:, :], a["const"])
            for r, src in rows:
                small(vec_rows[r:r + src.shape[0], :], src)
            for half in range(2):
                cols = slice(DH * half, DH * half + DH)
                small(vec_rows[R_GDQ:R_GDQ + 1, cols], a["diff_q_norm_g"])
                small(vec_rows[R_GDK:R_GDK + 1, cols], a["diff_k_norm_g"])
                small(vec_rows[R_GNQ:R_GNQ + 1, cols], a["nsa_q_norm_g"])
                small(vec_rows[R_GKC:R_GKC + 3, cols], a["nsa_k_norm_g"][0])
            for j, name in enumerate(("diff_lambda_q1", "diff_lambda_k1", "diff_lambda_q2", "diff_lambda_k2")):
                small(lam_in[:, j, :], a[name].to_broadcast([P, DH]))
            small(gsub[:, :], a["diff_subln_g"].to_broadcast([P, P]))
            small(relb[:, :], a["rel_bias_2"])
            small(onehot[:, :], a["onehot"])
            small(cmp_w2[:, :, :, :], a["cmp_w2"][0].rearrange("k (h p) d -> p k h d", p=P))
            small(L[:, 0, :], a["distance"])
            assert n_small == N_SMALL

            def split_hi(n):
                if n >= last_unit or units[n].raw:
                    return
                u = units[n]
                sc.wait_ge(raw_in[n % 2], u.arrived)
                if n >= 2:
                    sc.wait_ge(*used(n - 2))
                size = u.nk * u.width
                act_fn(w_hi[:, n % 2, 0:size], raw[:, n % 2, 0:size], ACT.Copy).then_inc(hi_done, 1)

            def split_act_hi(u):
                if u.act0 >= 2:
                    sc.wait_ge(*used(u.n - 2))
                o = 4 * (u.act0 % 2)
                act_fn(h_hi[:, o:o + u.nk, :], act[:, u.k0:u.k0 + u.nk, :], ACT.Copy).then_inc(a_hi_done, 1)

            def evacuate(u):
                if u.tiles is None:
                    if not u.last:
                        return
                    kind, arg = u.evac
                    for j in range(u.ntiles):
                        t = u.tile + j
                        if kind == "hidden":
                            sc.wait_ge(tile_done, t + 1)
                            act_fn(hid[:, arg, j, :], bank[t % 4][:, 0:2 * NCMP], ACT.Silu,
                                   bias=col[:, R_B1 + 2 * arg + j:R_B1 + 2 * arg + j + 1])\
                                .then_inc(sc_evac, 1)
                        if kind == "z":
                            sc.wait_ge(tile_done, t + 1)
                            act_fn(zs[:, j, 512 * arg:512 * arg + 512], bank[t % 4][:, :], ACT.Silu)\
                                .then_inc(sc_evac, 1)
                        if kind == "dv":
                            sc.wait_ge(tile_done, t + 1)
                            act_fn(dv[:, j, :], bank[t % 4][:, :], ACT.Copy).then_inc(sc_evac, 1)
                    return
                x = u.aux0
                for j, (c0, m, kind, idx) in enumerate(u.tiles):
                    t = u.tile + j
                    src = bank[t % 4][0:m, :]
                    if kind.startswith("norm") or kind in ("vd", "ng", "viw"):
                        sc.wait_ge(tile_done, t + 1)
                        if x == 0:
                            sc.wait_ge(setup_done, 1)
                        if kind == "viw":
                            sc.wait_ge(scratch_in, 16)
                        if x >= 4:
                            sc.wait_ge(aux_free, x - 3)
                        fn = ACT.Square if kind.startswith("norm") else ACT.Sigmoid if kind == "ng" else ACT.Copy
                        act_fn(L[0:m, x % 4, :], src, fn).then_inc(aux_in, 1)
                        x += 1
                    if kind == "iq":
                        sc.wait_ge(tile_done, t + 1)
                        act_fn(iq[:, idx, :], src, ACT.Copy).then_inc(sc_evac, 1)
                    if kind == "q2":
                        sc.wait_ge(tile_done, t + 1)
                        act_fn(q2[:, idx, :], src, ACT.Copy, scale=-(DH ** -0.5)).then_inc(sc_evac, 1)
                    if kind in ("cb", "cc", "cx"):
                        sc.wait_ge(tile_done, t + 1)
                        dst = dict(cb=ya, cc=cc, cx=cx)[kind][:, idx, :]
                        act_fn(dst, src, ACT.Copy).then_inc(sc_evac, 1)
                    if kind == "gate":
                        sc.wait_ge(tile_done, t + 1)
                        if idx == 0:
                            sc.wait_ge(ix_acc, 3 * DSA_HEADS)
                        if idx == 4:
                            sc.wait_ge(conv_done, 4)
                        act_fn(gate(idx), src, ACT.Sigmoid, bias=col[:, R_BGATE + idx:R_BGATE + idx + 1])\
                            .then_inc(sc_evac, 1)

            def roots_of(u):
                for j, (c0, m, kind, idx) in enumerate(u.tiles or []):
                    if kind.startswith("norm"):
                        x = u.aux0 + j
                        sc.wait_ge(aux_done, x + 1)
                        act_fn(L[:, x % 4, :], bank[4 + x % 2][:, :], ACT.Sqrt, bias=eps).then_inc(aux_root, 1)

            def row_norm(nth, junk):
                for i in range(NT):
                    if nth == 0:
                        sc.wait_ge(x_in[i], 16)
                    act_fn(junk[:, i, :], xres[:, i, :], ACT.Square, accum_out=st[:, ST_SS + i:ST_SS + i + 1])\
                        .then_inc(squares, 1)
                sc.wait_ge(squares, NT * (nth + 1))
                act_fn(st[:, ST_RS:ST_RS + NT], st[:, ST_SS:ST_SS + NT], ACT.Sqrt, scale=1.0 / D, bias=eps)\
                    .then_inc(roots, 1)

            def attend(which):
                jobs, lag = attention[which], LAG[which]
                for k in range(len(jobs) + lag + 1):
                    if k < len(jobs):
                        job = jobs[k]
                        for c in range(len(job["subs"])):
                            r = job["r"] + c
                            n = P * (job["i"] + 1)
                            sc.wait_ge(lg_done, r + 1)
                            act_fn(L[:, r % 4, 0:n], L[:, r % 4, 0:n], ACT.Exp, scale=-1.0, bias=stat(ST_MN, job, c),
                                   accum_out=stat(ST_SM, job, c)).then_inc(ex_done, 1)
                    if 0 <= k - lag < len(jobs) and jobs[k - lag]["by_act"]:
                        job = jobs[k - lag]
                        copy_pt(sc, act_fn, job)

            def copy_pt(eng, fn, job):
                n, w = job["n"], P * (job["i"] + 1)
                eng.wait_ge(tr_done, n + 1)
                if n >= 2:
                    eng.wait_ge(pv_done, n - 1)
                fn(PT[:, n % 2, 0:w], bank[T_BANKS[n % 2]][:, 0:w], ACT.Copy).then_inc(pt_act, 1)

            nth_norm = 0
            pending = None
            for at_step, (kind, body, at) in enumerate(plan):
                if kind == "unit":
                    split_hi(body.n + 1)
                    if body.act and body.act0 + 1 < len(down_units):
                        split_act_hi(down_units[body.act0 + 1])
                    evacuate(body)
                    if pending is not None:
                        roots_of(pending)
                    pending = body
                    continue
                if pending is not None:
                    roots_of(pending)
                    pending = None
                if kind == "transpose":
                    if body["norm"]:
                        if nth_norm == 0:
                            sc.wait_ge(eps_done, 1)
                        else:
                            sc.wait_ge(res_done, at["res"])
                        row_norm(nth_norm, zs)
                        nth_norm += 1
                    if at["unit"] == 0:
                        sc.wait_ge(lam_dot, 2)
                        act_fn(st[:, ST_LAM + 2:ST_LAM + 4], st[:, ST_LAM:ST_LAM + 2], ACT.Exp).then_inc(lam_exp, 1)
                        sc.wait_ge(col_done, 3)
                        split_hi(0)
                    k0 = 0
                    if body.get("branches"):
                        k0 = 4
                        sc.wait_ge(tile_done, at["tile"])
                        for m in range(4):
                            act_fn(h_hi[:, m, :], ya[:, m, :], ACT.Copy).then_inc(h_hi_done, 1)
                    for k in range(body["n"]):
                        t = at["tile"] + k
                        sc.wait_ge(tile_done, t + 1)
                        if body["gain"] is None:
                            ins = act_fn(h_hi[:, k0 + k, :], bank[t % 4][:, :], ACT.Copy)
                        else:
                            ins = act_fn(h_hi[:, k, :], bank[t % 4][:, :], ACT.Copy,
                                         scale=col[:, body["gain"] + k:body["gain"] + k + 1])
                        ins.then_inc(h_hi_done, 1)
                if kind == "attention_1":
                    attend("diff")
                    sc.wait_ge(o_free, GROUPS["diff"])
                    act_fn(L[:, :, :], oacc[:, :, :], ACT.Square).then_inc(epi_sq, 1)
                    sc.wait_ge(epi_root, 1)
                    act_fn(st[:, ST_DSS + 16:ST_DSS + 32], st[:, ST_DSS:ST_DSS + 16], ACT.Sqrt, scale=1.0 / P,
                           bias=eps).then_inc(epi_sq, 1)
                    sc.wait_ge(kc_mm, 2)
                    act_fn(kc[:, :], bank[4][:, 0:2 * NCMP], ACT.Square).then_inc(kc_sq, 1)
                    sc.wait_ge(kc_mm, 3)
                    act_fn(vc[:, :, :].rearrange("p a b -> p (a b)"), bank[5][0:NCMP, 0:2 * DH], ACT.Copy)\
                        .then_inc(kc_sq, 1)
                    sc.wait_ge(kc_avg, 1)
                    act_fn(kc[:, :], bank[6][:, 0:2 * NCMP], ACT.Sqrt, bias=eps).then_inc(kc_root, 1)
                    for b in range(KVH):
                        sc.wait_ge(c_lg, b + 1)
                        act_fn(L[:, b, :].rearrange("p (j c) -> p j c", c=32)[:, :, 0:NCMP],
                               L[:, b, :].rearrange("p (j c) -> p j c", c=32)[:, :, 0:NCMP],
                               ACT.Exp, scale=-1.0).then_inc(c_ex, 1)
                        for g in range(GROUP):
                            h = GROUP * b + g
                            sc.wait_ge(c_tr, h + 1)
                            if h >= 2:
                                sc.wait_ge(c_pv, h - 1)
                            act_fn(PT[0:NCMP, h % 2, :], bank[T_BANKS[h % 2]][0:NCMP, :], ACT.Copy).then_inc(c_pt, 1)
                    attend("nsa")
                if kind == "bias_rows":
                    for j in range(2):
                        t = at["tile"] + j
                        w = T if j == 0 else BIASW - T
                        sc.wait_ge(tile_done, t + 1)
                        act_fn(bias_row[:, T * j:T * j + w], bank[t % 4][0:DSA_HEADS, 0:w], ACT.Copy, scale=-1.0)\
                            .then_inc(rows_done, 1)
                if kind == "index":
                    r = 0
                    for i in range(1, NT):
                        for h in range(DSA_HEADS):
                            w = P * (i + 1)
                            sc.wait_ge(ix_s, r + 1)
                            if r >= 4:
                                sc.wait_ge(ix_acc, r - 3)
                            act_fn(L[:, r % 4, 0:w], bank[4 + r % 3][:, 0:w], ACT.Relu).then_inc(ix_relu, 1)
                            r += 1
                if kind == "attention_2":
                    attend("dsa")
                if kind == "merge":
                    for m in range(ND):
                        sc.wait_ge(branch_done, ND + m + 1)
                        sc.wait_ge(tile_done, at["tile"])
                        act_fn(h_hi[:, m, :], gate(m), ACT.Copy).then_inc(h_hi_done, 1)
                if kind == "ffn":
                    n0, t0 = at["unit"], at["tile"]
                    z0, z1 = ffn_slots

                    def ffn_step(f, first=False):
                        sc.wait_ge(raw_in[z1], f * 16 + units[n0 + 1].arrived)
                        sc.wait_ge(tile_done, f * 4 + t0)
                        act_fn(w_hi[:, z1, :], raw[:, z1, :], ACT.Copy).then_inc(hi_done, 1)
                        for j in range(2):
                            sc.wait_ge(tile_done, f * 4 + (t0 + j + 1))
                            if not first:
                                sc.wait_ge(act_done, f * 2)
                            act_fn(L[:, j, :], bank[(t0 + j) % 4][:, :], ACT.Silu).then_inc(gsilu, 1)
                        sc.wait_ge(raw_in[z0], f * 16 + (units[n0].arrived + 16))
                        sc.wait_ge(tile_done, f * 4 + (t0 + 2))
                        act_fn(w_hi[:, z0, :], raw[:, z0, :], ACT.Copy).then_inc(hi_done, 1)

                    ffn_step(0, first=True)
                    with sc.Fori(1, FFN_STEPS) as f:
                        ffn_step(f)
                    sc.wait_ge(act_done, NFF)
                    sc.wait_ge(tile_done, t0 + 4 * FFN_STEPS)
                    split_act_hi(down_units[0])
                if kind == "final":
                    sc.wait_ge(res_done, at["res"])
                    row_norm(nth_norm, zs)

        @block.vector
        def _(ve):
            v = nc.vector
            count = [0]

            def chain(ins):
                ins.then_inc(dve_step, 1)
                count[0] += 1
                ve.wait_ge(dve_step, count[0])

            def spread(x, *dims):
                return bass.AP(x.tensor, x.offset, [list(x.ap[0])] + [list(d) for d in dims])

            v.memset(eps, EPS).then_inc(eps_done, 1)
            ve.wait_ge(small_in, 16 * N_SMALL)
            ve.wait_ge(col_tr, 1)
            v.tensor_copy(col[:, :], bank[4][:, 0:NROWS]).then_inc(col_done, 1)
            ve.wait_ge(col_done, 1)
            for r in (R_GDQ, R_GNQ):
                v.tensor_scalar(col[:, r:r + 1], col[:, r:r + 1], -(DH ** -0.5), None, ALU.mult).then_inc(col_done, 1)
            for j in range(2):
                v.tensor_tensor_reduce(out=lam_in[:, 2 * j, :], in0=lam_in[:, 2 * j, :], in1=lam_in[:, 2 * j + 1, :],
                                       scale=1.0, scalar=0.0, op0=ALU.mult, op1=ALU.add,
                                       accum_out=st[:, ST_LAM + j:ST_LAM + j + 1]).then_inc(lam_dot, 1)
            chain(v.tensor_scalar(gsub[:, :], gsub[:, :], 1.0 - LAM_INIT, None, ALU.mult))
            for m in range(8):
                ins = v.scalar_tensor_tensor(nsm[:, m, :], L[:, 0, :], 2.0 ** -(m + 1), mask, ALU.mult, ALU.add)
            ins.then_inc(setup_done, 1)
            ve.wait_ge(lam_exp, 1)
            chain(v.tensor_tensor(st[:, ST_LAM:ST_LAM + 1], st[:, ST_LAM + 3:ST_LAM + 4],
                                  st[:, ST_LAM + 2:ST_LAM + 3], ALU.subtract))
            v.tensor_scalar(neglam, st[:, ST_LAM:ST_LAM + 1], -LAM_INIT, None, ALU.add).then_inc(lam_done, 1)

            def evacuate(u):
                if u.tiles is None:
                    if not u.last:
                        return
                    kind, half = u.evac
                    if kind == "residual":
                        for i in range(NT):
                            t = u.tile + i
                            x = xres[:, i, 512 * half:512 * half + 512]
                            ve.wait_ge(tile_done, t + 1)
                            v.tensor_tensor(x, bank[t % 4][:, :], x, ALU.add).then_inc(res_done, 1)
                    return
                for j, (c0, m, kind, idx) in enumerate(u.tiles):
                    t = u.tile + j
                    src = bank[t % 4]
                    if kind == "cmp":
                        ve.wait_ge(tile_done, t + 1)
                        for kv in range(KVH):
                            half = slice(DH * kv, DH * kv + DH)
                            v.tensor_copy(shifted[0:DH, idx, kv, :], src[half, :])
                            ins = v.tensor_copy(shifted[DH:P, idx, kv, 0:T - 1], src[half, 1:T])
                        ins.then_inc(ve_evac, 1)
                        ve.wait_ge(ve_evac, u.ve0 + j + 1)
                        for s in range(2):
                            first = shifted[:, idx, 0, CMP_STRIDE * s:CMP_STRIDE * s + 1]
                            g = col[:, R_POS + NPAIR * idx + 8 * s:R_POS + NPAIR * idx + 8 * s + 1]
                            o = flat[:, idx, 8 * s, 0:1]
                            v.tensor_tensor(spread(o, [2 * NCMP, 8], [NCMP, KVH], [1, NCMP]),
                                            spread(first, [2, 8], [T, KVH], [CMP_STRIDE, NCMP]),
                                            spread(g, [1, 8], [0, KVH], [0, NCMP]), ALU.add).then_inc(flat_done, 1)
                    if kind == "kik":
                        ve.wait_ge(tile_done, t + 1)
                        for r in range(2):
                            rows = slice(DH * r, DH * r + DH)
                            v.tensor_copy(k2[rows, :], src[0:DH, :])
                            ins = v.tensor_copy(ik2[rows, :], src[DH:P, :])
                        ins.then_inc(ve_evac, 1)
                    if kind == "branch_a":
                        ve.wait_ge(tile_done, t + 1)
                        ve.wait_ge(sc_evac, u.sc0)
                        v.tensor_tensor(gate(idx), src[:, :], gate(idx), ALU.mult).then_inc(branch_done, 1)
                    if kind == "branch_b":
                        ve.wait_ge(tile_done, t + 1)
                        chain(v.tensor_tensor(gate(8 + idx), src[:, :], gate(8 + idx), ALU.mult))
                        v.tensor_tensor(gate(idx), gate(idx), gate(8 + idx), ALU.add).then_inc(branch_done, 1)

            def finish(u):
                x = u.aux0
                for j, (c0, m, kind, idx) in enumerate(u.tiles or []):
                    t = u.tile + j
                    aux = bank[4 + x % 2]
                    blocks = aux[:, :].rearrange("p (i c) -> p i c", c=P)
                    if kind.startswith("norm"):
                        ve.wait_ge(aux_root, x + 1)
                        chain(v.reciprocal(L[:, x % 4, :], L[:, x % 4, :]))
                        if kind != "norm_kd":
                            dst, g = {"norm_dq": (dq, R_GDQ), "norm_dk": (dk, R_GDK), "norm_nq": (nq, R_GNQ)}[kind]
                            v.scalar_tensor_tensor(dst[:, idx, :], bank[t % 4][:, :], col[:, g:g + 1], L[:, x % 4, :],
                                                   ALU.mult, ALU.mult).then_inc(aux_free, 1)
                        else:
                            g = R_GKS + idx
                            for r in range(2):
                                rows = slice(DH * r, DH * r + DH)
                                ins = v.scalar_tensor_tensor(kd[rows, idx, r, :], bank[t % 4][rows, :],
                                                             col[rows, g:g + 1], L[rows, x % 4, :],
                                                             ALU.mult, ALU.mult)
                            chain(ins)
                            v.tensor_copy(kd[DH:P, idx, 0, :], kd[0:DH, idx, 0, :])
                            v.tensor_copy(kd[0:DH, idx, 1, :], kd[DH:P, idx, 1, :]).then_inc(aux_free, 1)
                    elif kind == "vd":
                        ve.wait_ge(aux_done, x + 1)
                        v.tensor_copy(vd[:, idx, :, :], blocks).then_inc(aux_free, 1)
                    elif kind == "ng":
                        ve.wait_ge(aux_done, x + 1)
                        v.tensor_copy(ngt[:, :, :], blocks[:, :, 96:120]).then_inc(aux_free, 1)
                    elif kind == "viw":
                        ve.wait_ge(aux_done, x + 1)
                        v.tensor_copy(v2, blocks[:, :, 0:DH])
                        v.tensor_scalar(iw, blocks[:, :, DH:DH + 8], 8 ** -0.5 * DH ** -0.5, None, ALU.mult)\
                            .then_inc(aux_free, 1)
                    else:
                        continue
                    x += 1

            def convolve():
                for m in range(4):
                    w = [col[:, R_CONV + 4 * k + m:R_CONV + 4 * k + m + 1] for k in range(3)]
                    u_, y_ = cc[:, m, :], cx[:, m, :]
                    chain(v.tensor_tensor(u_, u_, y_, ALU.mult))
                    chain(v.tensor_scalar(y_, u_, w[2], None, ALU.mult))
                    chain(v.scalar_tensor_tensor(y_[:, 1:T], u_[:, 0:T - 1], w[1], y_[:, 1:T], ALU.mult, ALU.add))
                    chain(v.scalar_tensor_tensor(y_[:, 2:T], u_[:, 0:T - 2], w[0], y_[:, 2:T], ALU.mult, ALU.add))
                    v.tensor_tensor(ya[:, m, :], ya[:, m, :], y_, ALU.mult).then_inc(conv_done, 1)

            def logits(job):
                n, i = P * (job["i"] + 1), job["i"]
                for c, s in enumerate(job["subs"]):
                    r = job["r"] + c
                    ve.wait_ge(s_done, r + 1)
                    if r >= 4:
                        ve.wait_ge(tr_done, job_of_sub[r - 4]["n"] + 1)
                    src, bias = bank[S_BANKS[r % 3]][:, 0:n], s["bias"][:, causal_window(i)]
                    if "select" in s:
                        bias = spread(s["bias"][:, n - 1:n], [-1, n])
                        chain(v.tensor_tensor(L[:, r % 4, 0:n], src, bias, ALU.add))
                        src, bias = L[:, r % 4, 0:n], s["select"]
                    v.tensor_tensor_reduce(out=L[:, r % 4, 0:n], in0=src, in1=bias, scale=1.0, scalar=3e38,
                                           op0=ALU.add, op1=ALU.min, accum_out=stat(ST_MN, job, c))\
                        .then_inc(lg_done, 1)

            def combine(job):
                r, n = job["r"], P * (job["i"] + 1)
                ve.wait_ge(ex_done, r + 2)
                c = st[:, ST_C + job["n"] % 4:ST_C + job["n"] % 4 + 1]
                if job["n"] >= 4:
                    ve.wait_ge(p_done, job["n"] - 3)
                chain(v.reciprocal(c, stat(ST_SM, job, 1)))
                chain(v.tensor_scalar(c, c, stat(ST_SM, job, 0), neglam, ALU.mult, ALU.mult))
                v.scalar_tensor_tensor(L[:, r % 4, 0:n], L[:, (r + 1) % 4, 0:n], c, L[:, r % 4, 0:n],
                                       ALU.mult, ALU.add).then_inc(p_done, 1)

            def group_out(which, job):
                G, base = job["G"], ST_SM + 8 * (job["G"] % 4)
                O = bank[O_BANKS[G % 2]]
                ve.wait_ge(pv_done, job["n"] + 1)
                rec = st[:, ST_R + NT * (G % 2):ST_R + NT * (G % 2) + NT]
                if G >= 2:
                    ve.wait_ge(o_free, G - 1)
                chain(v.reciprocal(rec, st[:, base:base + NT]))
                if which == "nsa":
                    g = 8 * (1 + job["br"]) + job["h"]
                    chain(v.tensor_tensor(rec, rec, ngt[:, :, g], ALU.mult))
                    ve.wait_ge(o_free, G)
                for i in range(NT):
                    r = rec[:, i:i + 1]
                    if which == "diff":
                        ins = v.tensor_scalar(oacc[:, i, P * G:P * G + P], O[:, P * i:P * i + P], r, None, ALU.mult)
                    elif which == "nsa":
                        o = oacc[:, i, DH * job["h"]:DH * job["h"] + DH]
                        ins = v.scalar_tensor_tensor(o, O[:, DH * i:DH * i + DH], r, o, ALU.mult, ALU.add)
                    else:
                        ins = v.tensor_scalar(osb[:, i, DH * job["h"]:DH * job["h"] + DH], O[:, DH * i:DH * i + DH],
                                              r, None, ALU.mult)
                ins.then_inc(o_free, 1)

            def attend(which):
                jobs, lag = attention[which], LAG[which]
                for k in range(len(jobs) + lag + 1):
                    if k < len(jobs):
                        logits(jobs[k])
                    if which == "diff" and 1 <= k <= len(jobs):
                        combine(jobs[k - 1])
                    if 0 <= k - lag < len(jobs) and not jobs[k - lag]["by_act"]:
                        job = jobs[k - lag]
                        n, w = job["n"], P * (job["i"] + 1)
                        ve.wait_ge(tr_done, n + 1)
                        ve.wait_ge(pv_done, n - 1)
                        v.tensor_copy(PT[:, n % 2, 0:w], bank[T_BANKS[n % 2]][:, 0:w]).then_inc(pt_dve, 1)
                    if 0 <= k - lag - 1 and jobs[k - lag - 1]["i"] == NT - 1:
                        group_out(which, jobs[k - lag - 1])

            def split_act_lo(u):
                ve.wait_ge(a_hi_done, u.act0 + 1)
                o = 4 * (u.act0 % 2)
                v.tensor_tensor(h_lo[:, o:o + u.nk, :], act[:, u.k0:u.k0 + u.nk, :],
                                h_hi[:, o:o + u.nk, :].bitcast(F32), ALU.subtract).then_inc(a_lo_done, 1)

            nth_norm, pending = 0, None
            for kind, body, at in plan:
                if kind == "unit":
                    if body.act and body.act0 + 1 < len(down_units):
                        split_act_lo(down_units[body.act0 + 1])
                    evacuate(body)
                    if pending is not None:
                        finish(pending)
                    pending = body
                    if body.name == "conv_x" and body.tiles[1][3] == 3:
                        ve.wait_ge(sc_evac, body.sc0 + 2)
                        convolve()
                    continue
                if pending is not None:
                    finish(pending)
                    pending = None
                if kind in ("transpose", "final") and (kind == "final" or body["norm"]):
                    ve.wait_ge(roots, nth_norm + 1)
                    nth_norm += 1
                    chain(v.reciprocal(st[:, ST_RR:ST_RR + NT], st[:, ST_RS:ST_RS + NT]))
                    for i in range(NT):
                        r = st[:, ST_RR + i:ST_RR + i + 1]
                        if kind == "transpose":
                            v.tensor_scalar(zs[:, i, :], xres[:, i, :], r, None, ALU.mult).then_inc(xn_done, 1)
                        else:
                            ve.wait_ge(gfin_in, 16)
                            v.scalar_tensor_tensor(zs[:, i, :], xres[:, i, :], r, gfin, ALU.mult, ALU.mult)\
                                .then_inc(y_done, 1)
                if kind == "transpose":
                    h0, k0 = at["h"], 0
                    if body.get("branches"):
                        k0 = 4
                        for m in range(4):
                            ve.wait_ge(h_hi_done, h0 + m + 1)
                            v.tensor_tensor(h_lo[:, m, :], ya[:, m, :], h_hi[:, m, :].bitcast(F32), ALU.subtract)\
                                .then_inc(h_lo_done, 1)
                        h0 += 4
                    for k in range(body["n"]):
                        g = 1.0 if body["gain"] is None else col[:, body["gain"] + k:body["gain"] + k + 1]
                        ve.wait_ge(h_hi_done, h0 + k + 1)
                        v.scalar_tensor_tensor(h_lo[:, k0 + k, :], bank[(at["tile"] + k) % 4][:, :], g,
                                               h_hi[:, k0 + k, :].bitcast(F32), ALU.mult, ALU.subtract)\
                            .then_inc(h_lo_done, 1)
                if kind == "attention_1":
                    attend("diff")
                    z_d = zs[:, :, 0:512]
                    heads = lambda x: x.rearrange("p i (h d) -> p i h d", d=P)
                    ve.wait_ge(epi_sq, 1)
                    v.tensor_reduce(out=st[:, ST_DSS:ST_DSS + 16].rearrange("p (i h) -> p i h", h=4),
                                    in_=L[:, :, :].rearrange("p i (h d) -> p i h d", d=P), axis=AX.X, op=ALU.add)\
                        .then_inc(epi_root, 1)
                    ve.wait_ge(sc_evac, at["sc"])
                    chain(v.tensor_tensor(heads(z_d), heads(z_d), spread(gsub[:, 0:1], [0, 4], [0, 4], [1, P]), ALU.mult))
                    ve.wait_ge(epi_sq, 2)
                    rr = st[:, ST_DSS + 16:ST_DSS + 32]
                    chain(v.reciprocal(rr, rr))
                    chain(v.tensor_tensor(heads(oacc), heads(oacc), spread(rr[:, 0:1], [4, 4], [1, 4], [0, P]), ALU.mult))
                    v.tensor_tensor(z_d, z_d, oacc, ALU.mult).then_inc(epi_done, 1)
                    ve.wait_ge(kc_root, 1)
                    chain(v.reciprocal(kc[:, :], kc[:, :]))
                    v.scalar_tensor_tensor(kc_t[:, :], bank[4][:, 0:2 * NCMP], col[:, R_GKC:R_GKC + 1], kc[:, :],
                                           ALU.mult, ALU.mult).then_inc(kc_done, 1)
                    for b in range(2):
                        s_ = bank[(3, 0)[b]]
                        view = lambda x: spread(x, [P, GROUP], [32, NT], [1, NCMP])
                        lc, sc_ = view(L[:, b, 0:1]), view(s_[:, 0:1])
                        cmn, csm = st[:, ST_CMN:ST_CMN + 16], st[:, ST_CSM:ST_CSM + 16]
                        ve.wait_ge(c_s, b + 1)
                        chain(v.tensor_tensor(lc, sc_, spread(cmask[:, 0, 0:1], [0, GROUP], [32, NT], [1, NCMP]), ALU.add))
                        l3 = L[:, b, :].rearrange("p (j c) -> p j c", c=32)[:, :, 0:NCMP]
                        chain(v.tensor_reduce(out=cmn, in_=l3, axis=AX.X, op=ALU.min))
                        v.tensor_tensor(l3, l3, spread(cmn[:, 0:1], [1, 16], [0, NCMP]), ALU.subtract).then_inc(c_lg, 1)
                        ve.wait_ge(c_ex, b + 1)
                        chain(v.tensor_reduce(out=csm, in_=l3, axis=AX.X, op=ALU.add))
                        chain(v.reciprocal(csm, csm))
                        v.tensor_tensor(lc, lc, spread(cvalid[:, 0, 0:1], [0, GROUP], [32, NT], [1, NCMP]), ALU.mult)\
                            .then_inc(c_p, 1)
                        for g in range(GROUP):
                            h, head = GROUP * b + g, 2 * g + b
                            coef = st[:, ST_R + NT * (h % 2):ST_R + NT * (h % 2) + NT]
                            if h >= 2:
                                ve.wait_ge(c_o, h - 1)
                            chain(v.tensor_tensor(coef, csm[:, NT * g:NT * g + NT], ngt[:, :, head], ALU.mult))
                            ve.wait_ge(c_pv, h + 1)
                            for i in range(NT):
                                ins = v.tensor_scalar(oacc[:, i, DH * head:DH * head + DH],
                                                      bank[O_BANKS[h % 2]][:, DH * i:DH * i + DH],
                                                      coef[:, i:i + 1], None, ALU.mult)
                            ins.then_inc(c_o, 1)
                    ve.wait_ge(c_o, NSA_HEADS)
                    ve.wait_ge(c_tr, NSA_HEADS)
                    ve.wait_ge(c_pv, NSA_HEADS)
                    attend("nsa")
                    ve.wait_ge(o_free, GROUPS["diff"] + GROUPS["nsa"])
                    v.tensor_tensor(zs[:, :, 512:1024], zs[:, :, 512:1024], oacc, ALU.mult).then_inc(attn_done, 1)
                if kind == "index":
                    ve.wait_ge(aux_free, at["aux"])
                    r = 0
                    for i in range(1, NT):
                        for h in range(DSA_HEADS):
                            w = P * (i + 1)
                            ve.wait_ge(ix_relu, r + 1)
                            src = L[:, r % 4, 0:w]
                            if h == 0:
                                v.scalar_tensor_tensor(work_of(i), src, iw[:, i, h:h + 1], mask[:, causal_window(i)],
                                                       ALU.mult, ALU.subtract).then_inc(ix_acc, 1)
                            else:
                                ve.wait_ge(ix_acc, r)
                                v.scalar_tensor_tensor(work_of(i), src, iw[:, i, h:h + 1], work_of(i),
                                                       ALU.mult, ALU.add).then_inc(ix_acc, 1)
                            r += 1
                    ve.wait_ge(ix_acc, r)
                    v.tensor_copy(pm_of(0), mask[:, causal_window(0)])
                    for _ in range(TOPK // 8):
                        for i in range(1, NT):
                            ins = v.max(st[:, ST_TOP + 8 * (i - 1):ST_TOP + 8 * i], work_of(i))
                        chain(ins)
                        for i in range(1, NT):
                            ins = v.match_replace(work_of(i), st[:, ST_TOP + 8 * (i - 1):ST_TOP + 8 * i], work_of(i), TAKEN)
                        chain(ins)
                    for i in range(1, NT):
                        ins = v.tensor_scalar(pm_of(i), work_of(i), TAKEN / 2, BIG, ALU.is_gt, ALU.mult)
                    ins.then_inc(topk_done, 1)
                if kind == "attention_2":
                    ve.wait_ge(topk_done, 1)
                    ve.wait_ge(bias_in, 16)
                    attend("dsa")
                    ve.wait_ge(o_free, sum(GROUPS.values()))
                    v.tensor_copy(st[:, ST_C:ST_C + 1], eps).then_inc(attn_done, 1)
                if kind == "merge":
                    for m in range(ND):
                        ve.wait_ge(h_hi_done, at["h"] + m + 1)
                        v.tensor_tensor(h_lo[:, m, :], gate(m), h_hi[:, m, :].bitcast(F32), ALU.subtract)\
                            .then_inc(h_lo_done, 1)
                if kind == "ffn":
                    t0 = at["tile"]

                    def ffn_step(f, tile):
                        for j in range(2):
                            ve.wait_ge(tile_done, f * 4 + (t0 + j + 3))
                            ve.wait_ge(gsilu, f * 2 + (j + 1))
                            v.tensor_tensor(tile(j), bank[(t0 + 2 + j) % 4][:, :], L[:, j, :], ALU.mult).then_inc(act_done, 1)

                    with ve.Fori(0, FFN_STEPS) as f:
                        ffn_step(f, lambda j: pool[:, bass.ds(f * (2 * T) + T * j, T)])
                    split_act_lo(down_units[0])

        @block.tensor
        def _(pe):
            mm = nc.tensor.matmul

            def free_bank(t):
                if t >= 4:
                    name, value = released[t - 4]
                    pe.wait_ge(frees[name], value)

            def three(dst, w_pair, h_pair, start, stop):
                for p, (w, h) in enumerate(((0, 0), (0, 1), (1, 0))):
                    ins = mm(dst, w_pair[w], h_pair[h], start=start and p == 0, stop=stop and p == 2)
                return ins

            fresh = [None]

            def main(u):
                n = u.n
                if u.raw:
                    pe.wait_ge(raw_in[n % 2], u.arrived)
                    w, kv = slot(raw, n, u), u.evac[1]
                    pe.wait_ge(flat_done, 2 * kv + 2)
                    tile = u.tile if u.last else n_tile_of_next(u)
                    for j in range(2):
                        if u.first:
                            free_bank(tile + j)
                        for q in range(u.nk):
                            ins = mm(bank[(tile + j) % 4][:, 0:2 * NCMP], w[:, q, P * j:P * j + P],
                                     flat[:, kv, u.k0 + q, :], start=u.first and q == 0, stop=u.last and q == u.nk - 1,
                                     skip_group_check=True)
                        if u.last:
                            ins.then_inc(tile_done, 1)
                    if not u.last:
                        ins.then_inc(part_done, 1)
                    return
                pe.wait_ge(lo_done, u.split)
                hi, lo = slot(w_hi, n, u), slot(w_lo, n, u)
                if u.tiles:
                    for j, (c0, m, kind, idx) in enumerate(u.tiles):
                        t = u.tile + j
                        free_bank(t)
                        for k in range(u.nk):
                            if j == 0 and fresh[0] is not None:
                                pe.wait_ge(h_lo_done, fresh[0] + u.k0 + k + 1)
                            h = u.k0 + k
                            ins = three(bank[t % 4][0:m, :], (hi[:, k, c0:c0 + m], lo[:, k, c0:c0 + m]),
                                        (h_hi[:, h, :], h_lo[:, h, :]), k == 0, k == u.nk - 1)
                        ins.then_inc(tile_done, 1)
                    fresh[0] = None
                    return
                tile = u.tile
                if u.act:
                    pe.wait_ge(a_lo_done, u.act0 + 1)
                for i in range(NT):
                    if u.first:
                        free_bank(tile + i)
                    for k in range(u.nk):
                        h = 4 * (u.act0 % 2) + k if u.act else u.k0 + k
                        if i == 0 and fresh[0] is not None:
                            pe.wait_ge(h_lo_done, fresh[0] + u.k0 + k + 1)
                        cols = slice(P * i, P * i + P)
                        s, e = u.first and k == 0, u.last and k == u.nk - 1
                        for p, (x, w) in enumerate(((h_hi, hi), (h_lo, hi), (h_hi, lo))):
                            ins = mm(bank[(tile + i) % 4][:, :], x[:, h, cols], w[:, k, :],
                                     start=s and p == 0, stop=e and p == 2, skip_group_check=True)
                    if u.last:
                        ins.then_inc(tile_done, 1)
                if not u.last:
                    ins.then_inc(part_done, 1)
                if u.last:
                    fresh[0] = None

            def n_tile_of_next(u):
                return u.tile

            def second(u):
                x = u.aux0
                for j, (c0, m, kind, idx) in enumerate(u.tiles or []):
                    if not (kind.startswith("norm") or kind in ("vd", "ng", "viw")):
                        continue
                    pe.wait_ge(aux_in, x + 1)
                    if x >= 2:
                        pe.wait_ge(aux_free, x - 1)
                    else:
                        pe.wait_ge(col_done, 1)
                    dst = bank[4 + x % 2]
                    if kind.startswith("norm"):
                        mm(dst[:, :], ones, L[:, x % 4, :], start=True, stop=True).then_inc(aux_done, 1)
                    else:
                        for i in range(NT):
                            ins = nc.tensor.transpose(dst[:, P * i:P * i + m], L[0:m, x % 4, P * i:P * i + P],
                                                      ident[0:m, 0:m])
                        ins.then_inc(aux_done, 1)
                    x += 1

            def attend(which):
                jobs, lag = attention[which], LAG[which]
                for k in range(len(jobs) + lag + 1):
                    if k < len(jobs):
                        job = jobs[k]
                        for c, s in enumerate(job["subs"]):
                            r = job["r"] + c
                            if r >= 3:
                                pe.wait_ge(lg_done, r - 2)
                            n = P * (job["i"] + 1)
                            mm(bank[S_BANKS[r % 3]][:, 0:n], s["q"], s["k"][:, 0:n], start=True, stop=True)\
                                .then_inc(s_done, 1)
                    if 0 <= k - lag < len(jobs):
                        job = jobs[k - lag]
                        if which == "diff":
                            pe.wait_ge(p_done, job["n"] + 1)
                        else:
                            pe.wait_ge(ex_done, job["r"] + 1)
                        if job["n"] >= 2:
                            pe.wait_ge(*all_jobs[job["n"] - 2]["pt"])
                        for j in range(job["i"] + 1):
                            ins = nc.tensor.transpose(bank[T_BANKS[job["n"] % 2]][:, P * j:P * j + P],
                                                      L[:, job["r"] % 4, P * j:P * j + P], ident)
                        ins.then_inc(tr_done, 1)
                    if 0 <= k - lag - 1:
                        job = jobs[k - lag - 1]
                        i, G, w = job["i"], job["G"], job["dv"]
                        pe.wait_ge(*job["pt"])
                        if i == 0 and G >= 2:
                            pe.wait_ge(o_free, G - 1)
                        for j in range(i + 1):
                            ins = mm(bank[O_BANKS[G % 2]][:, w * i:w * i + w], PT[:, job["n"] % 2, P * j:P * j + P],
                                     job["v"][j], start=j == 0, stop=j == i)
                        ins.then_inc(pv_done, 1)

            pe.wait_ge(small_in, 16 * N_SMALL)
            nc.tensor.transpose(bank[4][:, 0:NROWS], vec_rows[:, :], ident[0:NROWS, 0:NROWS]).then_inc(col_tr, 1)
            nth_norm = n_attn = 0
            pending = None
            for kind, body, at in plan:
                if kind == "unit":
                    main(body)
                    if pending is not None:
                        second(pending)
                    pending = body
                    continue
                if pending is not None:
                    second(pending)
                    pending = None
                if kind == "transpose":
                    src = osb if body.get("branches") else zs
                    if not body["norm"]:
                        pe.wait_ge(attn_done, n_attn)
                    for k in range(body["n"]):
                        t = at["tile"] + k
                        free_bank(t)
                        for i in range(NT):
                            if body["norm"] and k == 0:
                                pe.wait_ge(xn_done, NT * nth_norm + i + 1)
                            ins = nc.tensor.transpose(bank[t % 4][:, P * i:P * i + P], src[:, i, P * k:P * k + P], ident)
                        ins.then_inc(tile_done, 1)
                    nth_norm += body["norm"]
                    fresh[0] = at["h"]
                if kind == "merge":
                    fresh[0] = at["h"]
                if kind == "bias_rows":
                    for j in range(2):
                        t, w = at["tile"] + j, (T, BIASW - T)[j]
                        free_bank(t)
                        mm(bank[t % 4][0:DSA_HEADS, 0:w], relb[:, :], onehot[:, T * j:T * j + w], start=True, stop=True)\
                            .then_inc(tile_done, 1)
                if kind == "attention_1":
                    n_attn += 1
                    for j in range(4):
                        free_bank(at["tile"] + j)
                    pe.wait_ge(aux_free, at["aux"])
                    pe.wait_ge(lam_done, 1)
                    attend("diff")
                    pe.wait_ge(o_free, GROUPS["diff"])
                    for r in range(2):
                        for hh in range(2):
                            ins = mm(bank[4][DH * r:DH * r + DH, 0:2 * NCMP], cmp_w2[:, 0, hh, :], hid[:, 0, hh, :],
                                     start=hh == 0, stop=hh == 1)
                        ins.then_inc(kc_mm, 1)
                    for kv in range(KVH):
                        for hh in range(2):
                            ins = mm(bank[5][0:NCMP, DH * kv:DH * kv + DH],
                                     hid[:, 1, hh, NCMP * kv:NCMP * kv + NCMP], cmp_w2[:, 1, hh, :],
                                     start=hh == 0, stop=hh == 1)
                    ins.then_inc(kc_mm, 1)
                    pe.wait_ge(kc_sq, 1)
                    mm(bank[6][:, 0:2 * NCMP], ones, kc[:, :], start=True, stop=True).then_inc(kc_avg, 1)
                    pe.wait_ge(kc_done, 1)
                    pe.wait_ge(kc_sq, 2)
                    for b in range(KVH):
                        for g in range(GROUP):
                            h, r = 2 * g + b, DH * b
                            kv = h // GROUP
                            for i in range(NT):
                                o = P * g + 32 * i
                                ins = mm(bank[(3, 0)[b]][:, o:o + NCMP], nq[r:r + DH, h // 2, P * i:P * i + P],
                                         kc_t[r:r + DH, NCMP * kv:NCMP * kv + NCMP], start=True, stop=True)
                        ins.then_inc(c_s, 1)
                    for b in range(KVH):
                        pe.wait_ge(c_p, b + 1)
                        for g in range(GROUP):
                            h = GROUP * b + g
                            if h >= 2:
                                pe.wait_ge(c_pt, h - 1)
                                pe.wait_ge(c_o, h - 1)
                            for i in range(NT):
                                o = P * g + 32 * i
                                ins = nc.tensor.transpose(bank[T_BANKS[h % 2]][0:NCMP, P * i:P * i + P],
                                                          L[:, b, o:o + NCMP], ident)
                            ins.then_inc(c_tr, 1)
                            pe.wait_ge(c_pt, h + 1)
                            for i in range(NT):
                                ins = mm(bank[O_BANKS[h % 2]][:, DH * i:DH * i + DH], PT[0:NCMP, h % 2, P * i:P * i + P],
                                         vc[:, (2 * g + b) // GROUP, :], start=True, stop=True)
                            ins.then_inc(c_pv, 1)
                    pe.wait_ge(c_o, NSA_HEADS)
                    attend("nsa")
                if kind == "index":
                    pe.wait_ge(aux_free, at["aux"])
                    pe.wait_ge(sc_evac, at["sc"])
                    pe.wait_ge(ve_evac, at["ve"])
                    r = 0
                    for i in range(1, NT):
                        for h in range(DSA_HEADS):
                            w, o = P * (i + 1), DH * (h % 2)
                            if r >= 3:
                                pe.wait_ge(ix_relu, r - 2)
                            mm(bank[4 + r % 3][:, 0:w], iq[o:o + DH, h // 2, P * i:P * i + P], ik2[o:o + DH, 0:w],
                               start=True, stop=True).then_inc(ix_s, 1)
                            r += 1
                if kind == "attention_2":
                    n_attn += 1
                    for j in range(4):
                        free_bank(at["tile"] + j)
                    pe.wait_ge(ix_relu, 3 * DSA_HEADS)
                    attend("dsa")
                if kind == "ffn":
                    n0, t0, s0 = at["unit"], at["tile"], at["split"]

                    def ffn_step(f, first=False):
                        for j in range(2):
                            pe.wait_ge(lo_done, f * 2 + (s0 + j + 1))
                            hi = w_hi[:, ffn_slots[j], :].rearrange("p (k c) -> p k c", c=256)
                            lo = w_lo[:, ffn_slots[j], :].rearrange("p (k c) -> p k c", c=256)
                            for m in range(2):
                                if first:
                                    free_bank(t0 + 2 * j + m)
                                else:
                                    pe.wait_ge((gsilu, act_done)[j], f * 2 + (m - 1))
                                for k in range(ND):
                                    if first and j == 0 and m == 0:
                                        pe.wait_ge(h_lo_done, at["h"] - ND + k + 1)
                                    ins = three(bank[(t0 + 2 * j + m) % 4][:, :],
                                                (hi[:, k, P * m:P * m + P], lo[:, k, P * m:P * m + P]),
                                                (h_hi[:, k, :], h_lo[:, k, :]), k == 0, k == ND - 1)
                                ins.then_inc(tile_done, 1)

                    ffn_step(0, first=True)
                    with pe.Fori(1, FFN_STEPS) as f:
                        ffn_step(f)
                    fresh[0] = None


_INS = ["x", "norm_g", "w_in", "diff_q_norm_g", "diff_k_norm_g", "diff_lambda_q1", "diff_lambda_k1",
        "diff_lambda_q2", "diff_lambda_k2", "diff_subln_g", "nsa_q_norm_g", "nsa_k_norm_g", "cmp_pos", "cmp_w1",
        "cmp_b1", "cmp_w2", "w_out", "g_mix_2", "w_in_2", "b_gate_2", "conv_w_2", "w_branch_a_2", "w_branch_b_2",
        "w_out_2", "rel_bias_2", "g_ffn_2", "w_ffn_gate_2", "w_ffn_up_2", "w_ffn_down_2", "g_final_2"]


def kernel(**inputs):
    import concourse.bacc as bacc
    from concourse.bass_utils import run_bass_kernel_spmd

    nc = bacc.Bacc("TRN2", target_bir_lowering=False, num_devices=1)
    arrays = {name: np.ascontiguousarray(inputs[name]) for name in _INS}
    arrays["g_final_2"] = arrays["g_final_2"].reshape(1, D)
    arrays["const"], arrays["distance"], arrays["onehot"] = shape_constants()
    ins = {name: nc.dram_tensor(f"in_{name}", x.shape, mybir.dt.from_np(x.dtype), kind="ExternalInput").ap()
           for name, x in arrays.items()}
    out = nc.dram_tensor("out_0", (1, T, D), mybir.dt.float32, kind="ExternalOutput").ap()
    build(nc, ins, out)
    r = run_bass_kernel_spmd(nc, [{f"in_{name}": x for name, x in arrays.items()}], core_ids=[0])
    return r.results[0]["out_0"]
```

```python
import math
from contextlib import ExitStack

import concourse.bass as bass
import numpy as np
from concourse import mybir

P = 128
T = 512
D = 1024
NT = T // P
ND = D // P
DH = 64
DIFF_HEADS = 4
NSA_HEADS = 8
KVH = 2
GROUP = NSA_HEADS // KVH
CMP_BLOCK, CMP_STRIDE, CMP_HIDDEN = 32, 16, 256
NCMP = (T - CMP_BLOCK) // CMP_STRIDE + 1
NPAIR = CMP_BLOCK // 2
DSA_HEADS = 8
TOPK = min(256, T // 4)
BUCKETS, MAX_EXACT, MAX_DISTANCE = 32, 16, 128
DFF = 2816
NFF = DFF // P
EPS = 1e-6
LAM_INIT = 0.8 - 0.6 * math.exp(0.0)
BIG = 1e30
TAKEN = -3e38
BIASW = 640

C_DQ, C_DK, C_DV, C_DZ, C_NQ, C_KV, C_NZ, C_NG = 0, 512, 1024, 1536, 2048, 2560, 3328, 3840
C_CB, C_CC, C_CX, C_Q, C_K, C_V, C_IQ, C_IK, C_IW, C_GA, C_GB = (
    0, 512, 1024, 1536, 2048, 2112, 2176, 2688, 2752, 2760, 3784)

R_NORM, R_MIX, R_FFN, R_BGATE, R_CONV, R_B1, R_POS = 0, 8, 16, 24, 40, 52, 56
R_GDQ, R_GDK, R_GNQ, R_GKC, R_GKS, R_GKW = 88, 89, 90, 91, 92, 93
NROWS = 94
N_SMALL = 23
K_IDENT, K_ONES, K_MASK, K_CMASK, K_CVALID, K_END = 0, 128, 256, 768, 896, 1024


def shape_constants():
    p = np.arange(P)[:, None]
    x = np.arange(T)[None, :]
    dist = (T - P) + p - x
    mask = np.where(dist < 0, BIG, 0.0)
    ones = np.kron(np.eye(2), np.ones((DH, DH)) / DH)
    c = np.arange(32)[None, None, :]
    t = np.arange(P)[:, None, None] + P * np.arange(NT)[None, :, None]
    ok = (c * CMP_STRIDE + CMP_BLOCK - 1 <= t) & (c < NCMP)
    const = np.concatenate([np.eye(P), ones, mask, np.where(ok, 0.0, BIG).reshape(P, -1),
                            np.where(ok, 1.0, 0.0).reshape(P, -1)], 1).astype(np.float32)
    distance = np.maximum(dist, 0).astype(np.float32)
    n = np.arange(BIASW) - (P - 1)
    large = MAX_EXACT + np.floor(np.log(np.maximum(n, 1) / MAX_EXACT) / math.log(MAX_DISTANCE / MAX_EXACT)
                                 * (BUCKETS - MAX_EXACT) + 1e-9).astype(np.int64)
    bucket = np.where(n < MAX_EXACT, n, np.minimum(large, BUCKETS - 1))
    onehot = ((np.arange(BUCKETS)[:, None] == bucket[None, :]) & ((n >= 0) & (n < T))[None, :]).astype(np.float32)
    return const, distance, onehot


class Unit:

    def __init__(self, name, parts, nk, width, tiles=None, k0=0, evac=None, first=True, last=True, raw=False,
                 aux=0, act=False):
        self.name, self.parts, self.nk, self.width = name, parts, nk, width
        self.tiles, self.k0, self.evac = tiles, k0, evac
        self.first, self.last, self.raw, self.aux, self.act = first, last, raw, aux, act


def build(nc, a, out):
    F32, F32R, F16 = mybir.dt.float32, mybir.dt.float32r, mybir.dt.float16
    ACT, ALU, AX = mybir.ActivationFunctionType, mybir.AluOpType, mybir.AxisListType

    def rows_of(w, r0, nk, c0, width):
        return w[r0 * P:(r0 + nk) * P, c0:c0 + width].rearrange("(k p) n -> p k n", p=P)

    steps = []

    def feature_units(name, w, c0, n, evac, aux=0, first_index=0):
        for j in range(n):
            steps.append(("unit", Unit(name, [(rows_of(w, 0, ND, c0 + 256 * j, 256), 0, 256)], ND, 256,
                                       tiles=[(0, P, evac, first_index + 2 * j), (P, P, evac, first_index + 2 * j + 1)],
                                       aux=aux)))

    def token_units(name, w, c0, evac, half, ktiles=ND, act=False):
        starts = list(range(0, ktiles, 4))
        for s in starts:
            nk = min(4, ktiles - s)
            steps.append(("unit", Unit(name, [(rows_of(w, s, nk, c0, 512), 0, 512)], nk, 512, k0=s,
                                       evac=(evac, half), first=s == 0, last=s == starts[-1], act=act)))

    w1in, w2in = a["w_in"][0], a["w_in_2"][0]

    def cmp_unit(kv, half):
        w1 = a["cmp_w1"][0, kv].rearrange("(q p) n -> p q n", p=P)
        steps.append(("unit", Unit("cmp_w1", [(w1[:, 8 * half:8 * half + 8, :], 0, CMP_HIDDEN)], 8, CMP_HIDDEN,
                                   k0=8 * half, evac=("hidden", kv), first=half == 0, last=half == 1, raw=True)))

    steps.append(("transpose", dict(norm=True, gain=R_NORM, n=ND)))
    steps.append(("small_arrays", None))
    feature_units("diff_q", w1in, C_DQ, 2, "norm_dq", aux=2)
    steps.append(("unit", Unit("cmp_kv", [(rows_of(w1in, 0, ND, C_KV, 256), 0, 256)], ND, 256,
                               tiles=[(0, P, "cmp", 0), (P, P, "cmp", 1)])))
    feature_units("diff_k", w1in, C_DK, 1, "norm_dk", aux=2)
    cmp_unit(0, 0)
    feature_units("diff_k", w1in, C_DK + 256, 1, "norm_dk", aux=2, first_index=2)
    cmp_unit(0, 1)
    feature_units("nsa_q", w1in, C_NQ, 1, "norm_nq", aux=2)
    cmp_unit(1, 0)
    feature_units("nsa_q", w1in, C_NQ + 256, 1, "norm_nq", aux=2, first_index=2)
    cmp_unit(1, 1)
    steps.append(("unit", Unit("nsa_k", [(rows_of(w1in, 0, ND, C_KV + 256, 128), 0, 128),
                                         (rows_of(w1in, 0, ND, C_KV + 512, 128), 128, 128)], ND, 256,
                               tiles=[(0, P, "norm_kd", 0), (P, P, "norm_kd", 1)], aux=2)))
    steps.append(("unit", Unit("nsa_v", [(rows_of(w1in, 0, ND, C_KV + 384, 128), 0, 128),
                                         (rows_of(w1in, 0, ND, C_KV + 640, 128), 128, 128)], ND, 256,
                               tiles=[(0, P, "vd", 0), (P, P, "vd", 1)], aux=2)))
    steps.append(("unit", Unit("nsa_gate", [(rows_of(w1in, 0, ND, C_NG - 96, 120), 0, 120)], ND, 120,
                               tiles=[(0, 120, "ng", 0)], aux=1)))
    token_units("diff_z", w1in, C_DZ, "z", 0)
    feature_units("nsa_z", w1in, C_NZ, 2, "nz")
    token_units("diff_v", w1in, C_DV, "dv", 0)
    steps.append(("attention_1", None))
    steps.append(("transpose", dict(norm=False, gain=None, n=DIFF_HEADS)))
    steps.append(("split", "nsa"))
    token_units("out_1", a["w_out"][0], 0, "residual", 0)
    token_units("out_1", a["w_out"][0], 512, "residual", 1)
    steps.append(("transpose", dict(norm=True, gain=R_MIX, n=ND)))
    feature_units("index_q", w2in, C_IQ, 2, "iq")
    steps.append(("unit", Unit("k_ik_v_iw", [(rows_of(w2in, 0, ND, C_K, 64), 0, 64),
                                             (rows_of(w2in, 0, ND, C_IK, 64), 64, 64),
                                             (rows_of(w2in, 0, ND, C_V, 64), 128, 64),
                                             (rows_of(w2in, 0, ND, C_IW, 8), 192, 8)], ND, 200,
                               tiles=[(0, P, "kik", 0), (P, 72, "viw", 0)], aux=1)))
    steps.append(("index", None))
    feature_units("q", w2in, C_Q, 2, "q2")
    feature_units("conv_b", w2in, C_CB, 2, "cb")
    feature_units("conv_c", w2in, C_CC, 2, "cc")
    feature_units("conv_x", w2in, C_CX, 2, "cx")
    feature_units("gates_a", w2in, C_GA, 4, "gate", first_index=0)
    feature_units("gates_b", w2in, C_GB, 4, "gate", first_index=8)
    steps.append(("attention_2", None))
    steps.append(("split", "branches"))
    for name, w, k0 in (("branch_a", a["w_branch_a_2"][0], 0), ("branch_b", a["w_branch_b_2"][0], 4)):
        for half in range(2):
            steps.append(("unit", Unit(name, [(rows_of(w, 0, 4, 512 * half, 512), 0, 512)], 4, 512, k0=k0,
                                       tiles=[(P * j, P, name, 4 * half + j) for j in range(4)])))
    steps.append(("split", "merged"))
    token_units("out_2", a["w_out_2"][0], 0, "residual", 0)
    token_units("out_2", a["w_out_2"][0], 512, "residual", 1)
    steps.append(("transpose", dict(norm=True, gain=R_FFN, n=ND)))
    steps.append(("ffn", None))
    FFN_STEPS = DFF // 256
    token_units("down", a["w_ffn_down_2"][0], 0, "residual", 0, ktiles=NFF, act=True)
    token_units("down", a["w_ffn_down_2"][0], 512, "residual", 1, ktiles=NFF, act=True)
    steps.append(("final", None))

    n_unit = n_split = n_tile = n_part = n_aux = n_h = n_act = n_res = n_sc = n_ve = n_branch = n_hid = 0
    ring_in = [0, 0]
    plan = []
    released = []
    units = []
    for kind, body in steps:
        at = dict(unit=n_unit, split=n_split, tile=n_tile, part=n_part, aux=n_aux, h=n_h, act=n_act, res=n_res,
                  sc=n_sc, ve=n_ve)
        plan.append((kind, body, at))
        if kind == "unit":
            ntiles = len(body.tiles) if body.tiles else (NT if body.last and not body.raw else 0)
            body.n, body.tile, body.ntiles = n_unit, n_tile, ntiles
            ring_in[n_unit % 2] += 16 * len(body.parts)
            body.arrived = ring_in[n_unit % 2]
            n_unit += 1
            n_split += not body.raw
            body.split = n_split
            n_tile += ntiles
            if not body.tiles and not body.last:
                n_part += 1
            elif body.raw:
                n_hid += 2
            body.part, body.hid = n_part, n_hid
            body.tile_end = n_tile
            body.aux0 = n_aux
            n_aux += body.aux
            body.act0 = n_act
            n_act += body.act
            body.sc0, body.ve0, body.res0, body.branch0, x = n_sc, n_ve, n_res, n_branch, body.aux0
            for tile_kind in ([t[2] for t in body.tiles] if body.tiles else [body.evac[0]] * ntiles):
                if tile_kind.startswith("norm"):
                    x += 1
                    released.append(("aux_free", x))
                elif tile_kind in ("vd", "ng", "viw"):
                    x += 1
                    released.append(("aux_in", x))
                elif tile_kind in ("cmp", "kik"):
                    n_ve += 1
                    released.append(("ve_evac", n_ve))
                elif tile_kind == "residual":
                    n_res += 1
                    released.append(("res_done", n_res))
                elif tile_kind.startswith("branch"):
                    n_branch += 1
                    released.append(("branch_done", n_branch))
                else:
                    n_sc += 1
                    released.append(("sc_evac", n_sc))
            units.append(body)
        elif kind == "transpose":
            n_tile += body["n"]
            for _ in range(body["n"]):
                n_h += 1
                released.append(("h_lo_done", n_h))
        elif kind == "split":
            n_h += 4 if body == "nsa" else ND
        elif kind == "small_arrays":
            n_tile += 2
            released += [("rows_done", 1), ("rows_done", 2)]
        elif kind == "ffn":
            ffn_slots = n_unit % 2, (n_unit + 1) % 2
            ffn_ring = n_split % 2, (n_split + 1) % 2
            for _ in range(FFN_STEPS):
                for j in range(2):
                    ring_in[ffn_slots[j]] += 16
                    u = Unit("ffn", None, ND, 256)
                    n_tile += 2
                    n_split += 1
                    released += [("gsilu" if j == 0 else "act_done", 2 * _ + 1), ("gsilu" if j == 0 else "act_done", 2 * _ + 2)]
                    u.n, u.arrived, u.split, u.part, u.tile_end = n_unit, ring_in[ffn_slots[j]], n_split, n_part, n_tile
                    n_unit += 1
                    units.append(u)

    ctx = ExitStack()
    with ctx:
        def sb(name, shape, dt=F32):
            return ctx.enter_context(nc.sbuf_tensor(name, shape, dt))

        def sem(name):
            return ctx.enter_context(nc.semaphore(name))

        LRING = 7
        const = sb("const", [P, K_END])
        col = sb("col", [P, NROWS])
        relb = sb("relb", [BUCKETS, DSA_HEADS])
        lam_in = sb("lam_in", [P, 4, DH])
        gsub = sb("gsub", [P, P])
        cmp_w2 = sb("cmp_w2", [P, 2, 2, DH])
        raw = sb("raw", [P, 2, 2048])
        w_hi = sb("w_hi", [P, 2, 2048], F32R)
        w_lo = sb("w_lo", [P, 2, 2048], F32R)
        h_hi = sb("h_hi", [P, ND, T], F32R)
        h_lo = sb("h_lo", [P, ND, T], F32R)
        xres = sb("xres", [P, NT, D])
        zs = sb("zs", [P, NT, D])
        pool = sb("pool", [P, 16384])
        L = sb("L", [P, LRING, T])
        PT = sb("PT", [P, 3, T])
        st = sb("st", [P, 256])
        hid = sb("hid", [P, 2, 2, 2 * NCMP])
        kc = sb("kc", [P, 2 * NCMP])
        kc_t = sb("kc_t", [P, 2 * NCMP])
        vc = sb("vc", [P, KVH, DH])
        ngt = sb("ngt", [P, NT, 24])
        vec_rows = PT[0:NROWS, 0, 0:P]
        onehot = PT[:, :, :].rearrange("p a n -> p (a n)")[0:BUCKETS, P:P + BIASW]
        bias_row = L[0:DSA_HEADS, 4:6, :].rearrange("p a n -> p (a n)")

        ident = const[:, K_IDENT:K_IDENT + P]
        ones = const[:, K_ONES:K_ONES + P]
        mask = const[:, K_MASK:K_MASK + T]
        cmask = const[:, K_CMASK:K_CMASK + P].rearrange("p (i c) -> p i c", c=32)
        cvalid = const[:, K_CVALID:K_CVALID + P].rearrange("p (i c) -> p i c", c=32)

        def region(start, *shape):
            n = int(np.prod(shape))
            v = pool[:, start:start + n]
            if len(shape) == 2:
                v = v.rearrange("p (a b) -> p a b", b=shape[1])
            if len(shape) == 3:
                v = v.rearrange("p (a b c) -> p a b c", b=shape[1], c=shape[2])
            return v

        zflat = zs[:, :, :].rearrange("p a b -> p (a b)")
        dq = region(0, DIFF_HEADS, 2, T)
        dk, nq, dv = (region(4096 + 2048 * j, 4, T) for j in range(3))
        kd = region(10240, 2, T)
        vd = region(11264, 2, NT, P)
        oacc = region(12288, NT, 512)
        flat = region(12288, 2, NPAIR, 2 * NCMP)
        pc = region(14336, 2, 512)
        causal_distance = region(15360, T)
        shifted = zflat[:, 0:2048].rearrange("p (a b c) -> p a b c", a=2, b=KVH)
        zd = zflat[:, 0:2048].rearrange("p (i n) -> p i n", i=NT)
        nzt = zflat[:, 2048:4096].rearrange("p (m n) -> p m n", m=4)
        q2, k2, v2 = region(0, 4, T), region(2048, T), region(2560, NT, DH)
        pm = region(2816, 1280)
        bh = region(4096, DSA_HEADS, T)
        iq = region(8192, 4, 2, T)
        cc, cx = region(12288, 4, T), region(14336, 4, T)
        ot2 = zflat[:, 0:2048].rearrange("p (m n) -> p m n", m=4)
        ya = zflat[:, 2048:4096].rearrange("p (m n) -> p m n", m=4)
        ik2, work = zflat[:, 0:512], zflat[:, 512:1664]
        iw = zflat[:, 1664:1664 + 8 * NT].rearrange("p (i h) -> p i h", i=NT)

        def gate(j):
            return pool[:, 8192 + T * j:8192 + T * j + T]

        split_sources = dict(nsa=[(nzt[:, m, :], 4 + m) for m in range(4)],
                             branches=[(ya[:, m, :], m) for m in range(4)] + [(ot2[:, m, :], 4 + m) for m in range(4)],
                             merged=[(gate(m), m) for m in range(ND)])
        act = region(0, NFF, T)
        gfin = region(NFF * T, D)

        def causal_window(i):
            return slice(T - P - P * i, T)

        def work_of(i):
            o = {1: 0, 2: 256, 3: 640}[i]
            return work[:, o:o + P * (i + 1)]

        def pm_of(i):
            o = P * (i * (i + 1) // 2)
            return pm[:, o:o + P * (i + 1)]

        bank = [ctx.enter_context(nc.psum_tensor(f"bank{j}", [P, T], F32)) for j in range(8)]
        S_BANKS, O_BANKS = [4, 5, 3], [7, 2]

        ST_MN, ST_SM, ST_R, ST_C = 0, 16, 64, 72
        ST_EPS, ST_NEGLAM, ST_SS, ST_RS, ST_RR, ST_LAM = 80, 81, 84, 88, 92, 96
        ST_CMN, ST_CSM, ST_TOP, ST_DSS = 100, 116, 132, 160
        ST_C2 = 192
        ST_DR = 32
        eps = st[:, ST_EPS:ST_EPS + 1]
        neglam = st[:, ST_NEGLAM:ST_NEGLAM + 1]

        first_in, small_in = sem("first_in"), sem("small_in")
        x_in = [sem(f"x_in{i}") for i in range(NT)]
        raw_in = [sem("raw_in0"), sem("raw_in1")]
        hi_done, lo_done = sem("hi_done"), sem("lo_done")
        part_done, tile_done = sem("part_done"), sem("tile_done")
        sc_evac, ve_evac = sem("sc_evac"), sem("ve_evac")
        col_tr, col_done = sem("col_tr"), sem("col_done")
        setup_done, eps_done = sem("setup_done"), sem("eps_done")
        lam_dot, lam_exp, lam_done = sem("lam_dot"), sem("lam_exp"), sem("lam_done")
        squares, roots, recips, xn_done = sem("squares"), sem("roots"), sem("recips"), sem("xn_done")
        h_hi_done, h_lo_done = sem("h_hi_done"), sem("h_lo_done")
        aux_in, aux_done, aux_root, aux_free = sem("aux_in"), sem("aux_done"), sem("aux_root"), sem("aux_free")
        dve_step = sem("dve_step")
        s_done, lg_done, ex_done, p_done = sem("s_done"), sem("lg_done"), sem("ex_done"), sem("p_done")
        tr_done, pt_act, pt_dve = sem("tr_done"), sem("pt_act"), sem("pt_dve")
        pv_done, o_free = sem("pv_done"), sem("o_free")
        flat_done, hid_done, z_done = sem("flat_done"), sem("hid_done"), sem("z_done")
        epi_sq, epi_root, epi_done = sem("epi_sq"), sem("epi_root"), sem("epi_done")
        epi_rr, epi_zd = sem("epi_rr"), sem("epi_zd")
        kc_mm, kc_sq, kc_avg, kc_root, kc_done = sem("kc_mm"), sem("kc_sq"), sem("kc_avg"), sem("kc_root"), sem("kc_done")
        c_s, c_lg, c_ex, c_p = sem("c_s"), sem("c_lg"), sem("c_ex"), sem("c_p")
        c_tr, c_pt, c_pv, c_o = sem("c_tr"), sem("c_pt"), sem("c_pv"), sem("c_o")
        attn_done = sem("attn_done")
        hid_mm, zero_done, vc_zero = sem("hid_mm"), sem("zero_done"), sem("vc_zero")
        coef_done, scale_done = sem("coef_done"), sem("scale_done")
        alibi_done = sem("alibi_done")
        st_hi, st_lo = sem("st_hi"), sem("st_lo")
        res_done = sem("res_done")
        rows_done, scratch_in, bias_in = sem("rows_done"), sem("scratch_in"), sem("bias_in")
        iq_done, ik_done = sem("iq_done"), sem("ik_done")
        ix_s, ix_relu, ix_acc, topk_done = sem("ix_s"), sem("ix_relu"), sem("ix_acc"), sem("topk_done")
        q2_done, conv_in, conv_done, gate_done = sem("q2_done"), sem("conv_in"), sem("conv_done"), sem("gate_done")
        branch_done = sem("branch_done")
        gsilu, act_done = sem("gsilu"), sem("act_done")
        a_hi_done, a_lo_done = sem("a_hi_done"), sem("a_lo_done")
        gfin_in, y_done, out_done = sem("gfin_in"), sem("y_done"), sem("out_done")

        bias_dram = nc.dram_tensor("bias_dram", [DSA_HEADS, BIASW], F32, kind="Internal").ap()

        def used(n):
            u = units[n]
            if u.raw:
                return (hid_mm, u.hid) if u.last else (part_done, u.part)
            if u.name != "ffn" and not u.tiles and not u.last:
                return part_done, u.part
            return tile_done, u.tile_end

        frees = dict(aux_free=aux_free, aux_in=aux_in, ve_evac=ve_evac, res_done=res_done, branch_done=branch_done,
                     sc_evac=sc_evac, h_lo_done=h_lo_done, rows_done=rows_done, gsilu=gsilu, act_done=act_done)

        at_attention_1 = next(at for kind, _, at in plan if kind == "attention_1")
        split_units = [u for u in units if not u.raw]

        def slot(t, n, u):
            return t[:, n % 2, 0:u.nk * u.width].rearrange("p (k c) -> p k c", c=u.width)

        last_unit = len(units)
        down_units = [u for u in units if u.act]

        def q_stack(h):
            return h_hi[:, h, :]

        def k_stack(br, kv, part):
            return h_lo[:, 4 * br + 2 * kv + part, :]

        def jobs_of(which):
            jobs = []
            if which == "diff":
                for h in range(DIFF_HEADS):
                    for i in range(NT):
                        subs = [dict(q=[dq[:, h, c, P * i:P * i + P]], k=[dk[:, h, :]], bias=alibi(2 * h + 1))
                                for c in range(2)]
                        jobs.append(dict(g=h, i=i, subs=subs, v=[dv[:, j, P * h:P * h + P] for j in range(i + 1)]))
            if which == "nsa":
                for h in range(NSA_HEADS):
                    kv = h // GROUP
                    jobs.append(dict(g=h // 2, i=NT - 1, h=h, br=-1, subs=[], v=[vc[:, kv, :]]))
                    for br in range(2):
                        for i in range(NT):
                            q = q_stack(h)[:, P * i:P * i + P]
                            subs = [dict(q=[q, q], k=[k_stack(br, kv, 0), k_stack(br, kv, 1)], bias=alibi(h))]
                            jobs.append(dict(g=h // 2, i=i, subs=subs, h=h, br=br,
                                             v=[vd[:, br, j, DH * kv:DH * kv + DH] for j in range(i + 1)]))
            if which == "dsa":
                for h in range(DSA_HEADS):
                    for i in range(NT):
                        q = q_stack(h)[:, P * i:P * i + P]
                        subs = [dict(q=[q, q], k=[k_stack(0, 0, 0), k_stack(0, 0, 1)], bias=bh[:, h, :],
                                     select=pm_of(i))]
                        jobs.append(dict(g=h // 2, i=i, subs=subs, h=h, br=0, v=[v2[:, j, :] for j in range(i + 1)]))
            return jobs

        def alibi(m):
            z = (at_attention_1["unit"] + m) % 2
            return raw[:, z, T * (m // 2):T * (m // 2) + T]

        attention = {w: jobs_of(w) for w in ("diff", "nsa", "dsa")}
        sub_n = job_n = group_n = act_pt = dve_pt = scaled = 0
        for w in ("diff", "nsa", "dsa"):
            for m, j in enumerate(attention[w]):
                j["r"], j["n"], j["G"] = sub_n, job_n, group_n + j["g"]
                j["by_act"] = j["i"] in (3, 1) or w == "diff"
                j["last"] = m + 1 == len(attention[w]) or attention[w][m + 1]["g"] != j["g"]
                scaled += w != "diff" and j["subs"] != []
                j["scaled"] = scaled
                act_pt += j["by_act"]
                dve_pt += not j["by_act"]
                j["pt"] = (pt_act, act_pt) if j["by_act"] else (pt_dve, dve_pt)
                sub_n += len(j["subs"])
                job_n += 1
            group_n += attention[w][-1]["g"] + 1
        job_of_sub = [j for w in ("diff", "nsa", "dsa") for j in attention[w] for _ in j["subs"]]
        all_jobs = [j for w in ("diff", "nsa", "dsa") for j in attention[w]]
        def t_bank(n):
            return bank[(6, 1)[n % 2]] if n < len(attention["diff"]) else bank[(6, 1, 0)[n % 3]]

        GROUPS = {"diff": DIFF_HEADS, "nsa": NSA_HEADS // 2, "dsa": DSA_HEADS // 2}
        LAG = {"diff": 2, "nsa": 5, "dsa": 5}

        def stat(base, job, c):
            o = base + 2 * (job["n"] % 8) + c
            return st[:, o:o + 1]

        def sum_of(job, c):
            if len(job["subs"]) == 2 and c == 0:
                return st[:, ST_DR + job["n"]:ST_DR + job["n"] + 1]
            return stat(ST_SM, job, c)

        stack_items = {"nsa": [("k", br, kv) for br in range(2) for kv in range(KVH)] + [("q", h) for h in range(NSA_HEADS)],
                       "dsa": [("k", 0, 0)] + [("q", h) for h in range(DSA_HEADS)]}

        def stacked(which, m):
            items = (stack_items["nsa"] if which == "dsa" else []) + stack_items[which][:m]
            return sum(2 if item[0] == "k" else 1 for item in items)

        def stack_source(which, item):
            if item[0] == "q":
                h = item[1]
                r = DH * (h % 2)
                return (nq if which == "nsa" else q2)[r:r + DH, h // 2, :], r
            if which == "nsa":
                r = DH * item[2]
                return kd[r:r + DH, item[1], :], r
            return k2[0:DH, :], 0

        block = ctx.enter_context(nc.Block())

        @block.sync
        def _(sp):
            def load(u):
                if u.n >= 2:
                    before = units[u.n - 2]
                    if before.raw:
                        sp.wait_ge(*used(u.n - 2))
                    else:
                        sp.wait_ge(lo_done, before.split)
                if u.n == at_attention_1["unit"] + 1:
                    sp.wait_ge(attn_done, 1)
                for src, c0, width in u.parts:
                    sp.dma_start(slot(raw, u.n, u)[:, :, c0:c0 + width], src).then_inc(raw_in[u.n % 2], 16)

            def small_loads():
                rows = [(R_MIX, a["g_mix_2"][0].rearrange("(r c) -> r c", c=P)),
                        (R_FFN, a["g_ffn_2"][0].rearrange("(r c) -> r c", c=P)),
                        (R_BGATE, a["b_gate_2"][0].rearrange("(r c) -> r c", c=P)),
                        (R_CONV, a["conv_w_2"][0].rearrange("k (r c) -> (k r) c", c=P)),
                        (R_B1, a["cmp_b1"][0].rearrange("k (r c) -> (k r) c", c=P)),
                        (R_POS, a["cmp_pos"][0].rearrange("k (q b) d -> (k q) (b d)", b=2))]
                n_small = 0

                def small(dst, src):
                    nonlocal n_small
                    sp.dma_start(dst, src).then_inc(small_in, 16)
                    n_small += 1

                for r, src in rows:
                    small(vec_rows[r:r + src.shape[0], :], src)
                for half in range(2):
                    cols = slice(DH * half, DH * half + DH)
                    small(vec_rows[R_GDQ:R_GDQ + 1, cols], a["diff_q_norm_g"])
                    small(vec_rows[R_GDK:R_GDK + 1, cols], a["diff_k_norm_g"])
                    small(vec_rows[R_GNQ:R_GNQ + 1, cols], a["nsa_q_norm_g"])
                    small(vec_rows[R_GKC:R_GKC + 3, cols], a["nsa_k_norm_g"][0])
                for j, name in enumerate(("diff_lambda_q1", "diff_lambda_k1", "diff_lambda_q2", "diff_lambda_k2")):
                    small(lam_in[:, j, :], a[name].to_broadcast([P, DH]))
                small(gsub[:, :], a["diff_subln_g"].to_broadcast([P, P]))
                small(relb[:, :], a["rel_bias_2"])
                small(onehot[:, :], a["onehot"])
                small(cmp_w2[:, :, :, :], a["cmp_w2"][0].rearrange("k (h p) d -> p k h d", p=P))
                small(L[:, 0, :], a["distance"])
                assert n_small == N_SMALL

            for i in range(NT):
                sp.dma_start(xres[:, i, :], a["x"][0, P * i:P * i + P, :]).then_inc(x_in[i], 16)
            sp.dma_start(const[:, :], a["const"]).then_inc(first_in, 16)
            sp.dma_start(vec_rows[R_NORM:R_NORM + ND, :], a["norm_g"][0].rearrange("(r c) -> r c", c=P))\
              .then_inc(first_in, 16)
            for kind, body, at in plan:
                if kind == "unit":
                    load(body)
                    if body.n == 0:
                        small_loads()
                if kind == "ffn":
                    wg, wu = a["w_ffn_gate_2"][0], a["w_ffn_up_2"][0]
                    with sp.Fori(0, FFN_STEPS) as f:
                        for j, w in enumerate((wg, wu)):
                            sp.wait_ge(lo_done, f * 2 + (at["split"] - 1 + j))
                            sp.dma_start(raw[:, ffn_slots[j], :].rearrange("p (k c) -> p k c", c=256),
                                         w.rearrange("(k p) n -> p k n", p=P)[:, :, bass.ds(f * 256, 256)])\
                              .then_inc(raw_in[ffn_slots[j]], 16)
            sp.dma_start(gfin, a["g_final_2"].to_broadcast([P, D])).then_inc(gfin_in, 16)
            for i in range(NT):
                sp.wait_ge(y_done, i + 1)
                sp.dma_start(out[0, P * i:P * i + P, :], zs[:, i, :]).then_inc(out_done, 16)
            sp.wait_ge(out_done, 16 * NT)

        @block.gpsimd
        def _(pool_e):
            def split_lo(s):
                if s >= len(split_units):
                    return
                u = split_units[s]
                pool_e.wait_ge(hi_done, s + 1)
                size = u.nk * u.width
                nc.gpsimd.tensor_tensor(w_lo[:, s % 2, 0:size], raw[:, u.n % 2, 0:size],
                                        w_hi[:, s % 2, 0:size].bitcast(F32), ALU.subtract).then_inc(lo_done, 1)

            def scale(which):
                for k, job in enumerate(attention[which]):
                    if which == "dsa" and k % 4 == 0 and 3 + k // 4 < len(stack_items["dsa"]):
                        if k > 0:
                            pool_e.wait_ge(scale_done, job["scaled"] - 1)
                        stack_lo("dsa", 3 + k // 4)
                    if not job["subs"]:
                        continue
                    r, n = job["r"], P * (job["i"] + 1)
                    pool_e.wait_ge(coef_done, job["scaled"])
                    nc.gpsimd.tensor_tensor(L[:, r % LRING, 0:n], L[:, r % LRING, 0:n],
                                            stat(ST_C2, job, 0).to_broadcast([P, n]), ALU.mult).then_inc(scale_done, 1)

            def stack_lo(which, m):
                item = stack_items[which][m]
                src, r = stack_source(which, item)
                pool_e.wait_ge(st_hi, m + 1 + (len(stack_items["nsa"]) if which == "dsa" else 0))
                if item[0] == "q":
                    q = q_stack(item[1])
                    pieces = [(q[DH - r:P - r, :], q[r:r + DH, :])]
                else:
                    hi, lo = k_stack(item[1], item[2], 0), k_stack(item[1], item[2], 1)
                    pieces = [(lo[half:half + DH, :], hi[r:r + DH, :]) for half in (0, DH)]
                for j, (lo, hi) in enumerate(pieces):
                    nc.gpsimd.tensor_tensor(lo, src, hi.bitcast(F32), ALU.subtract).then_inc(st_lo, 1)
                    pool_e.wait_ge(st_lo, stacked(which, m) + j + 1)

            zeroed = 0

            def zero(x):
                nonlocal zeroed
                nc.gpsimd.memset(x, 0.0).then_inc(zero_done, 1)
                zeroed += 1
                pool_e.wait_ge(zero_done, zeroed)

            zero(vc[:, :, :])
            zero(dq[DH:P, :, 0, :])
            zero(dq[0:DH, :, 1, :])
            split_lo(0)
            for kind, body, at in plan:
                if kind == "unit" and not body.raw:
                    split_lo(body.split)
                if kind == "small_arrays":
                    pool_e.wait_ge(rows_done, 2)
                    pool_e.dma_start(bias_dram, bias_row[:, 0:BIASW]).then_inc(scratch_in, 16)
                if kind == "attention_1":
                    pool_e.wait_ge(lo_done, at["split"] + 1)
                    for m in (1, 3, 5, 7, 0, 2, 4, 6):
                        nc.gpsimd.tensor_scalar(alibi(m), causal_distance, 2.0 ** -(m + 1), None, ALU.mult)\
                            .then_inc(alibi_done, 1)
                    pool_e.wait_ge(alibi_done, 8)
                    for m in range(len(stack_items["nsa"])):
                        stack_lo("nsa", m)
                    scale("nsa")
                    pool_e.wait_ge(scratch_in, 16)
                    pool_e.wait_ge(attn_done, 1)
                    pool_e.dma_start(bh, bass.AP(bias_dram.tensor, 0, [[1, P], [BIASW, DSA_HEADS], [1, T]]))\
                          .then_inc(bias_in, 16)
                    zero(iq[DH:P, :, 0, :])
                    zero(iq[0:DH, :, 1, :])
                if kind == "attention_2":
                    pool_e.wait_ge(lo_done, at["split"] + 1)
                    for m in range(3):
                        stack_lo("dsa", m)
                    scale("dsa")
                if kind == "ffn":
                    def ffn_lo(j, value):
                        pool_e.wait_ge(hi_done, value)
                        z, w = ffn_slots[j], ffn_ring[j]
                        nc.gpsimd.tensor_tensor(w_lo[:, w, :], raw[:, z, :], w_hi[:, w, :].bitcast(F32),
                                                ALU.subtract).then_inc(lo_done, 1)

                    with pool_e.Fori(0, FFN_STEPS) as f:
                        ffn_lo(1, f * 2 + (at["split"] + 2))
                        ffn_lo(0, f * 2 + (at["split"] + 3))

        @block.scalar
        def _(sc):
            act_fn = nc.scalar.activation
            def split_hi(s):
                if s >= len(split_units):
                    return
                u = split_units[s]
                sc.wait_ge(raw_in[u.n % 2], u.arrived)
                if s >= 2:
                    sc.wait_ge(*used(split_units[s - 2].n))
                size = u.nk * u.width
                act_fn(w_hi[:, s % 2, 0:size], raw[:, u.n % 2, 0:size], ACT.Copy).then_inc(hi_done, 1)

            def split_act_hi(u):
                if u.act0 >= 2:
                    sc.wait_ge(*used(u.n - 2))
                o = 4 * (u.act0 % 2)
                act_fn(h_hi[:, o:o + u.nk, :], act[:, u.k0:u.k0 + u.nk, :], ACT.Copy).then_inc(a_hi_done, 1)

            def evacuate(u):
                if u.tiles is None:
                    if not u.last:
                        return
                    kind, arg = u.evac
                    if kind == "hidden":
                        for j in range(2):
                            sc.wait_ge(hid_mm, 2 * arg + j + 1)
                            act_fn(hid[:, arg, j, :], bank[6 + j][:, 0:2 * NCMP], ACT.Silu,
                                   bias=col[:, R_B1 + 2 * arg + j:R_B1 + 2 * arg + j + 1]).then_inc(hid_done, 1)
                    for j in range(u.ntiles):
                        t = u.tile + j
                        if kind == "z":
                            sc.wait_ge(tile_done, t + 1)
                            sc.wait_ge(flat_done, 4)
                            act_fn(zd[:, j, :], bank[t % 4][:, :], ACT.Silu).then_inc(sc_evac, 1)
                        if kind == "dv":
                            sc.wait_ge(tile_done, t + 1)
                            act_fn(dv[:, j, :], bank[t % 4][:, :], ACT.Copy).then_inc(sc_evac, 1)
                    return
                x = u.aux0
                for j, (c0, m, kind, idx) in enumerate(u.tiles):
                    t = u.tile + j
                    src = bank[t % 4][0:m, :]
                    if kind.startswith("norm") or kind in ("vd", "ng", "viw"):
                        sc.wait_ge(tile_done, t + 1)
                        if x == 0:
                            sc.wait_ge(setup_done, 1)
                        if x >= 4:
                            sc.wait_ge(aux_free, x - 3)
                        fn = ACT.Square if kind.startswith("norm") else ACT.Sigmoid if kind == "ng" else ACT.Copy
                        act_fn(L[0:m, x % 4, :], src, fn).then_inc(aux_in, 1)
                        x += 1
                    if kind == "iq":
                        sc.wait_ge(tile_done, t + 1)
                        if idx == 0:
                            sc.wait_ge(zero_done, 5)
                        act_fn(iq[0:DH, idx, 0, :], src[0:DH, :], ACT.Copy)
                        act_fn(iq[DH:P, idx, 1, :], src[DH:P, :], ACT.Copy).then_inc(sc_evac, 1)
                    if kind == "nz":
                        sc.wait_ge(tile_done, t + 1)
                        act_fn(nzt[:, idx, :], src, ACT.Silu).then_inc(sc_evac, 1)
                    if kind == "q2":
                        sc.wait_ge(tile_done, t + 1)
                        act_fn(q2[:, idx, :], src, ACT.Copy, scale=-(DH ** -0.5)).then_inc(sc_evac, 1)
                    if kind in ("cb", "cc", "cx"):
                        sc.wait_ge(tile_done, t + 1)
                        dst = dict(cb=ya, cc=cc, cx=cx)[kind][:, idx, :]
                        act_fn(dst, src, ACT.Copy).then_inc(sc_evac, 1)
                    if kind == "gate":
                        sc.wait_ge(tile_done, t + 1)
                        if idx == 0:
                            sc.wait_ge(ix_acc, 3 * DSA_HEADS)
                        if idx == 8:
                            sc.wait_ge(conv_done, 4)
                        act_fn(gate(idx), src, ACT.Sigmoid, bias=col[:, R_BGATE + idx:R_BGATE + idx + 1])\
                            .then_inc(sc_evac, 1)

            def roots_of(u):
                for j, (c0, m, kind, idx) in enumerate(u.tiles or []):
                    if kind.startswith("norm"):
                        x = u.aux0 + j
                        sc.wait_ge(aux_done, x + 1)
                        act_fn(L[:, x % 4, :], bank[4 + x % 2][:, :], ACT.Sqrt, bias=eps).then_inc(aux_root, 1)

            def row_norm(nth, junk):
                for i in range(NT):
                    if nth == 0:
                        sc.wait_ge(x_in[i], 16)
                    act_fn(junk[:, i, :], xres[:, i, :], ACT.Square, accum_out=st[:, ST_SS + i:ST_SS + i + 1])\
                        .then_inc(squares, 1)
                sc.wait_ge(squares, NT * (nth + 1))
                act_fn(st[:, ST_RS:ST_RS + NT], st[:, ST_SS:ST_SS + NT], ACT.Sqrt, scale=1.0 / D, bias=eps)\
                    .then_inc(roots, 1)

            def stack_hi(which, m):
                item = stack_items[which][m]
                src, r = stack_source(which, item)
                if item[0] == "q":
                    act_fn(q_stack(item[1])[r:r + DH, :], src, ACT.Copy).then_inc(st_hi, 1)
                else:
                    act_fn(k_stack(item[1], item[2], 0)[0:DH, :], src, ACT.Copy)
                    act_fn(k_stack(item[1], item[2], 0)[DH:P, :], src, ACT.Copy).then_inc(st_hi, 1)

            def attend(which, between):
                jobs, lag = attention[which], LAG[which]
                for k in range(len(jobs) + lag + 2):
                    between(k)
                    if 0 <= k - lag < len(jobs) and jobs[k - lag]["by_act"]:
                        job = jobs[k - lag]
                        n, w, rows = job["n"], P * (job["i"] + 1), P if job["subs"] else NCMP
                        sc.wait_ge(tr_done, n + 1)
                        if n >= 3:
                            sc.wait_ge(pv_done, n - 2)
                        act_fn(PT[0:rows, n % 3, 0:w], t_bank(n)[0:rows, 0:w], ACT.Copy).then_inc(pt_act, 1)
                    if k < len(jobs):
                        job = jobs[k]
                        for c in range(len(job["subs"])):
                            r = job["r"] + c
                            n = P * (job["i"] + 1)
                            sc.wait_ge(lg_done, r + 1)
                            act_fn(L[:, r % LRING, 0:n], L[:, r % LRING, 0:n], ACT.Exp, scale=-1.0, bias=stat(ST_MN, job, c),
                                   accum_out=sum_of(job, c)).then_inc(ex_done, 1)

            def compress_and_stack(k):
                if k == 0:
                    sc.wait_ge(kc_mm, 2)
                    act_fn(kc[:, :], bank[0][:, 0:2 * NCMP], ACT.Square).then_inc(kc_sq, 1)
                if k == 1:
                    sc.wait_ge(kc_avg, 1)
                    act_fn(kc[:, :], bank[0][:, P:P + 2 * NCMP], ACT.Sqrt, bias=eps).then_inc(kc_root, 1)
                if k == 3:
                    sc.wait_ge(kc_mm, 3)
                    act_fn(vc[0:NCMP, :, :].rearrange("p a b -> p (a b)"), bank[0][0:NCMP, 0:2 * DH], ACT.Copy)\
                        .then_inc(kc_sq, 1)
                if 4 <= k < 4 + len(stack_items["nsa"]):
                    stack_hi("nsa", k - 4)
                if k in (9, 14):
                    b = (9, 14).index(k)
                    sc.wait_ge(c_lg, b + 1)
                    lc = pc[:, b, :].rearrange("p (j c) -> p j c", c=32)[:, :, 0:NCMP]
                    act_fn(lc, lc, ACT.Exp, scale=-1.0).then_inc(c_ex, 1)

            def diff_norm(k):
                if k == 18:
                    sc.wait_ge(epi_sq, NT)
                    act_fn(st[:, ST_DSS + 16:ST_DSS + 32], st[:, ST_DSS:ST_DSS + 16], ACT.Sqrt, scale=1.0 / P,
                           bias=eps).then_inc(epi_root, 1)

            def dsa_stacks(k):
                m = 3 + k // 4
                if k % 4 == 0 and m < len(stack_items["dsa"]):
                    stack_hi("dsa", m)

            nth_norm = 0
            pending = None
            for at_step, (kind, body, at) in enumerate(plan):
                if kind == "unit":
                    if not body.raw:
                        split_hi(body.split)
                    if body.act and body.act0 + 1 < len(down_units):
                        split_act_hi(down_units[body.act0 + 1])
                    if pending is not None:
                        roots_of(pending)
                    evacuate(body)
                    pending = body
                    continue
                if pending is not None:
                    roots_of(pending)
                    pending = None
                if kind == "transpose":
                    if body["norm"]:
                        if nth_norm == 0:
                            sc.wait_ge(eps_done, 1)
                        else:
                            sc.wait_ge(res_done, at["res"])
                        row_norm(nth_norm, zs)
                        nth_norm += 1
                    if at["unit"] == 0:
                        split_hi(0)
                        sc.wait_ge(col_done, 1)
                    for k in range(body["n"]):
                        t = at["tile"] + k
                        sc.wait_ge(tile_done, t + 1)
                        if body["gain"] is None:
                            ins = act_fn(h_hi[:, k, :], bank[t % 4][:, :], ACT.Copy)
                        else:
                            ins = act_fn(h_hi[:, k, :], bank[t % 4][:, :], ACT.Copy,
                                         scale=col[:, body["gain"] + k:body["gain"] + k + 1])
                        ins.then_inc(h_hi_done, 1)
                if kind == "split":
                    for m, (src, k) in enumerate(split_sources[body]):
                        if body == "merged":
                            sc.wait_ge(branch_done, ND + m + 1)
                            sc.wait_ge(tile_done, at["tile"])
                        act_fn(h_hi[:, k, :], src, ACT.Copy).then_inc(h_hi_done, 1)
                if kind == "attention_1":
                    sc.wait_ge(tile_done, at["tile"])
                    attend("diff", compress_and_stack)
                    attend("nsa", diff_norm)
                    sc.wait_ge(attn_done, 1)
                if kind == "attention_2":
                    sc.wait_ge(tile_done, at["tile"])
                    for m in range(3):
                        stack_hi("dsa", m)
                    attend("dsa", dsa_stacks)
                    sc.wait_ge(attn_done, 2)
                if kind == "small_arrays":
                    for j in range(2):
                        t = at["tile"] + j
                        w = T if j == 0 else BIASW - T
                        sc.wait_ge(tile_done, t + 1)
                        act_fn(bias_row[:, T * j:T * j + w], bank[t % 4][0:DSA_HEADS, 0:w], ACT.Copy, scale=-1.0)\
                            .then_inc(rows_done, 1)
                    sc.wait_ge(col_done, 4)
                    sc.wait_ge(lam_dot, 2)
                    act_fn(st[:, ST_LAM + 2:ST_LAM + 4], st[:, ST_LAM:ST_LAM + 2], ACT.Exp).then_inc(lam_exp, 1)
                if kind == "index":
                    r = 0
                    for i in range(1, NT):
                        for h in range(DSA_HEADS):
                            w = P * (i + 1)
                            sc.wait_ge(ix_s, r + 1)
                            if r >= 4:
                                sc.wait_ge(ix_acc, r - 3)
                            act_fn(L[:, r % 4, 0:w], bank[4 + r % 3][:, 0:w], ACT.Relu).then_inc(ix_relu, 1)
                            r += 1
                if kind == "ffn":
                    n0, t0 = at["unit"], at["tile"]
                    (z0, z1), (g0, g1) = ffn_slots, ffn_ring

                    def ffn_step(f, first=False):
                        sc.wait_ge(raw_in[z1], f * 16 + units[n0 + 1].arrived)
                        sc.wait_ge(tile_done, f * 4 + t0)
                        act_fn(w_hi[:, g1, :], raw[:, z1, :], ACT.Copy).then_inc(hi_done, 1)
                        for j in range(2):
                            sc.wait_ge(tile_done, f * 4 + (t0 + j + 1))
                            if not first:
                                sc.wait_ge(act_done, f * 2)
                            act_fn(L[:, j, :], bank[(t0 + j) % 4][:, :], ACT.Silu).then_inc(gsilu, 1)
                        sc.wait_ge(raw_in[z0], f * 16 + (units[n0].arrived + 16))
                        sc.wait_ge(tile_done, f * 4 + (t0 + 2))
                        act_fn(w_hi[:, g0, :], raw[:, z0, :], ACT.Copy).then_inc(hi_done, 1)

                    ffn_step(0, first=True)
                    with sc.Fori(1, FFN_STEPS) as f:
                        ffn_step(f)
                    sc.wait_ge(act_done, NFF)
                    sc.wait_ge(tile_done, t0 + 4 * FFN_STEPS)
                    split_act_hi(down_units[0])
                if kind == "final":
                    sc.wait_ge(res_done, at["res"])
                    row_norm(nth_norm, zs)

        @block.vector
        def _(ve):
            v = nc.vector
            count = [0]

            def chain(ins):
                ins.then_inc(dve_step, 1)
                count[0] += 1
                ve.wait_ge(dve_step, count[0])

            def spread(x, *dims):
                return bass.AP(x.tensor, x.offset, [list(x.ap[0])] + [list(d) for d in dims])

            v.memset(eps, EPS).then_inc(eps_done, 1)
            ve.wait_ge(col_tr, 1)
            v.tensor_copy(col[:, 0:ND], bank[4][:, 0:ND]).then_inc(col_done, 1)

            def small_arrays():
                ve.wait_ge(small_in, 16 * N_SMALL)
                ve.wait_ge(col_tr, 2)
                v.tensor_copy(col[:, ND:NROWS], bank[4][:, ND:NROWS]).then_inc(col_done, 1)
                ve.wait_ge(col_done, 2)
                for r in (R_GDQ, R_GNQ):
                    v.tensor_scalar(col[:, r:r + 1], col[:, r:r + 1], -(DH ** -0.5), None, ALU.mult).then_inc(col_done, 1)
                for j in range(2):
                    v.tensor_tensor_reduce(out=lam_in[:, 2 * j, :], in0=lam_in[:, 2 * j, :], in1=lam_in[:, 2 * j + 1, :],
                                           scale=1.0, scalar=0.0, op0=ALU.mult, op1=ALU.add,
                                           accum_out=st[:, ST_LAM + j:ST_LAM + j + 1]).then_inc(lam_dot, 1)
                chain(v.tensor_scalar(gsub[:, :], gsub[:, :], 1.0 - LAM_INIT, None, ALU.mult))
                v.tensor_tensor(causal_distance, L[:, 0, :], mask, ALU.add).then_inc(setup_done, 1)
                ve.wait_ge(lam_exp, 1)
                chain(v.tensor_tensor(st[:, ST_LAM:ST_LAM + 1], st[:, ST_LAM + 3:ST_LAM + 4],
                                      st[:, ST_LAM + 2:ST_LAM + 3], ALU.subtract))
                v.tensor_scalar(neglam, st[:, ST_LAM:ST_LAM + 1], -LAM_INIT, None, ALU.add).then_inc(lam_done, 1)

            def evacuate(u):
                if u.tiles is None:
                    if not u.last:
                        return
                    kind, half = u.evac
                    if kind == "residual":
                        for i in range(NT):
                            t = u.tile + i
                            x = xres[:, i, 512 * half:512 * half + 512]
                            ve.wait_ge(tile_done, t + 1)
                            v.tensor_tensor(x, bank[t % 4][:, :], x, ALU.add).then_inc(res_done, 1)
                    return
                for j, (c0, m, kind, idx) in enumerate(u.tiles):
                    t = u.tile + j
                    src = bank[t % 4]
                    if kind == "cmp":
                        ve.wait_ge(tile_done, t + 1)
                        for kv in range(KVH):
                            half = slice(DH * kv, DH * kv + DH)
                            v.tensor_copy(shifted[0:DH, idx, kv, :], src[half, :])
                            ins = v.tensor_copy(shifted[DH:P, idx, kv, 0:T - 1], src[half, 1:T])
                        ins.then_inc(ve_evac, 1)
                        ve.wait_ge(ve_evac, u.ve0 + j + 1)
                        for s in range(2):
                            first = shifted[:, idx, 0, CMP_STRIDE * s:CMP_STRIDE * s + 1]
                            g = col[:, R_POS + NPAIR * idx + 8 * s:R_POS + NPAIR * idx + 8 * s + 1]
                            o = flat[:, idx, 8 * s, 0:1]
                            v.tensor_tensor(spread(o, [2 * NCMP, 8], [NCMP, KVH], [1, NCMP]),
                                            spread(first, [2, 8], [T, KVH], [CMP_STRIDE, NCMP]),
                                            spread(g, [1, 8], [0, KVH], [0, NCMP]), ALU.add).then_inc(flat_done, 1)
                    if kind == "kik":
                        ve.wait_ge(tile_done, t + 1)
                        v.tensor_copy(k2[0:DH, :], src[0:DH, :])
                        for r in range(2):
                            ins = v.tensor_copy(ik2[DH * r:DH * r + DH, :], src[DH:P, :])
                        ins.then_inc(ve_evac, 1)
                    if kind == "branch_a":
                        ve.wait_ge(tile_done, t + 1)
                        ve.wait_ge(sc_evac, u.sc0)
                        v.tensor_tensor(gate(idx), src[:, :], gate(idx), ALU.mult).then_inc(branch_done, 1)
                    if kind == "branch_b":
                        ve.wait_ge(tile_done, t + 1)
                        chain(v.tensor_tensor(gate(8 + idx), src[:, :], gate(8 + idx), ALU.mult))
                        v.tensor_tensor(gate(idx), gate(idx), gate(8 + idx), ALU.add).then_inc(branch_done, 1)

            def finish(u):
                x = u.aux0
                for j, (c0, m, kind, idx) in enumerate(u.tiles or []):
                    t = u.tile + j
                    aux = bank[4 + x % 2]
                    blocks = aux[:, :].rearrange("p (i c) -> p i c", c=P)
                    if kind.startswith("norm"):
                        ve.wait_ge(aux_root, x + 1)
                        chain(v.reciprocal(L[:, x % 4, :], L[:, x % 4, :]))
                        if kind != "norm_dq":
                            dst, g = {"norm_dk": (dk, R_GDK), "norm_nq": (nq, R_GNQ), "norm_kd": (kd, R_GKS + idx)}[kind]
                            v.scalar_tensor_tensor(dst[:, idx, :], bank[t % 4][:, :], col[:, g:g + 1], L[:, x % 4, :],
                                                   ALU.mult, ALU.mult).then_inc(aux_free, 1)
                        else:
                            if idx == 0:
                                ve.wait_ge(zero_done, 3)
                            for r in range(2):
                                rows = slice(DH * r, DH * r + DH)
                                ins = v.scalar_tensor_tensor(dq[rows, idx, r, :], bank[t % 4][rows, :],
                                                             col[rows, R_GDQ:R_GDQ + 1], L[rows, x % 4, :],
                                                             ALU.mult, ALU.mult)
                            ins.then_inc(aux_free, 1)
                    elif kind == "vd":
                        ve.wait_ge(aux_done, x + 1)
                        v.tensor_copy(vd[:, idx, :, :], blocks).then_inc(aux_free, 1)
                    elif kind == "ng":
                        ve.wait_ge(aux_done, x + 1)
                        v.tensor_copy(ngt[:, :, :], blocks[:, :, 96:120]).then_inc(aux_free, 1)
                    elif kind == "viw":
                        ve.wait_ge(aux_done, x + 1)
                        v.tensor_copy(v2, blocks[:, :, 0:DH])
                        v.tensor_scalar(iw, blocks[:, :, DH:DH + 8], 8 ** -0.5 * DH ** -0.5, None, ALU.mult)\
                            .then_inc(aux_free, 1)
                    else:
                        continue
                    x += 1

            def convolve():
                for m in range(4):
                    w = [col[:, R_CONV + 4 * k + m:R_CONV + 4 * k + m + 1] for k in range(3)]
                    u_, y_ = cc[:, m, :], cx[:, m, :]
                    chain(v.tensor_tensor(u_, u_, y_, ALU.mult))
                    chain(v.tensor_scalar(y_, u_, w[2], None, ALU.mult))
                    chain(v.scalar_tensor_tensor(y_[:, 1:T], u_[:, 0:T - 1], w[1], y_[:, 1:T], ALU.mult, ALU.add))
                    chain(v.scalar_tensor_tensor(y_[:, 2:T], u_[:, 0:T - 2], w[0], y_[:, 2:T], ALU.mult, ALU.add))
                    v.tensor_tensor(ya[:, m, :], ya[:, m, :], y_, ALU.mult).then_inc(conv_done, 1)

            def logits(job):
                n, i = P * (job["i"] + 1), job["i"]
                for c, s in enumerate(job["subs"]):
                    r = job["r"] + c
                    ve.wait_ge(s_done, r + 1)
                    if r >= LRING:
                        ve.wait_ge(tr_done, job_of_sub[r - LRING]["n"] + 1)
                    src, bias = bank[S_BANKS[r % 3]][:, 0:n], s["bias"][:, causal_window(i)]
                    if "select" in s:
                        bias = spread(s["bias"][:, n - 1:n], [-1, n])
                        chain(v.tensor_tensor(L[:, r % LRING, 0:n], src, bias, ALU.add))
                        src, bias = L[:, r % LRING, 0:n], s["select"]
                    v.tensor_tensor_reduce(out=L[:, r % LRING, 0:n], in0=src, in1=bias, scale=1.0, scalar=3e38,
                                           op0=ALU.add, op1=ALU.min, accum_out=stat(ST_MN, job, c))\
                        .then_inc(lg_done, 1)

            def combine(job):
                r, n = job["r"], P * (job["i"] + 1)
                ve.wait_ge(ex_done, r + 2)
                c = stat(ST_C2, job, 0)
                chain(v.reciprocal(c, sum_of(job, 1)))
                chain(v.tensor_scalar(c, c, sum_of(job, 0), neglam, ALU.mult, ALU.mult))
                v.scalar_tensor_tensor(L[:, r % LRING, 0:n], L[:, (r + 1) % LRING, 0:n], c, L[:, r % LRING, 0:n],
                                       ALU.mult, ALU.add).then_inc(p_done, 1)

            def coefficient(job):
                c = stat(ST_C2, job, 0)
                ve.wait_ge(ex_done, job["r"] + 1)
                if job["G"] < GROUPS["diff"] + GROUPS["nsa"]:
                    g = 8 * (1 + job["br"]) + job["h"]
                    chain(v.reciprocal(c, sum_of(job, 0)))
                    v.tensor_tensor(c, c, ngt[:, job["i"], g:g + 1], ALU.mult).then_inc(coef_done, 1)
                else:
                    v.reciprocal(c, sum_of(job, 0)).then_inc(coef_done, 1)

            def group_out(which, job):
                G = job["G"]
                O = bank[O_BANKS[G % 2]]
                ve.wait_ge(pv_done, job["n"] + 1)
                if which == "diff":
                    sums = st[:, ST_DR + NT * G:ST_DR + NT * G + NT]
                    chain(v.reciprocal(sums, sums))
                    for i in range(NT):
                        ins = v.tensor_scalar(oacc[:, i, P * G:P * G + P], O[:, P * i:P * i + P], sums[:, i:i + 1],
                                              None, ALU.mult)
                    ins.then_inc(o_free, 1)
                elif which == "nsa":
                    z = nzt[:, job["g"], :]
                    v.tensor_tensor(z, O[:, :], z, ALU.mult).then_inc(o_free, 1)
                else:
                    v.tensor_copy(ot2[:, job["g"], :], O[:, :]).then_inc(o_free, 1)

            def attend(which, between):
                jobs, lag = attention[which], LAG[which]
                for k in range(len(jobs) + lag + 2):
                    between(k)
                    if k < len(jobs):
                        logits(jobs[k])
                    if 1 <= k <= len(jobs) and jobs[k - 1]["subs"]:
                        (combine if which == "diff" else coefficient)(jobs[k - 1])
                    if 0 <= k - lag < len(jobs) and not jobs[k - lag]["by_act"]:
                        job = jobs[k - lag]
                        n, w = job["n"], P * (job["i"] + 1)
                        ve.wait_ge(tr_done, n + 1)
                        ve.wait_ge(pv_done, n - 2)
                        v.tensor_copy(PT[:, n % 3, 0:w], t_bank(n)[:, 0:w]).then_inc(pt_dve, 1)
                    if 0 <= k - lag - 2 and jobs[k - lag - 2]["last"]:
                        group_out(which, jobs[k - lag - 2])

            def grid(x):
                return spread(x, [P, GROUP], [32, NT], [1, NCMP])

            def compress_and_stack(k):
                cmn, csm = st[:, ST_CMN:ST_CMN + 16], st[:, ST_CSM:ST_CSM + 16]
                if k % NT == 0:
                    ve.wait_ge(alibi_done, min(k // NT + 1, 8))
                if k == 2:
                    ve.wait_ge(kc_root, 1)
                    chain(v.reciprocal(kc[:, :], kc[:, :]))
                    v.scalar_tensor_tensor(kc_t[:, :], bank[0][:, 0:2 * NCMP], col[:, R_GKC:R_GKC + 1], kc[:, :],
                                           ALU.mult, ALU.mult).then_inc(kc_done, 1)
                if k in (7, 12):
                    b = (7, 12).index(k)
                    lc = grid(pc[:, b, 0:1])
                    l3 = pc[:, b, :].rearrange("p (j c) -> p j c", c=32)[:, :, 0:NCMP]
                    ve.wait_ge(c_s, b + 1)
                    chain(v.tensor_tensor(lc, grid(bank[0][:, 0:1]),
                                          spread(cmask[:, 0, 0:1], [0, GROUP], [32, NT], [1, NCMP]), ALU.add))
                    chain(v.tensor_reduce(out=cmn, in_=l3, axis=AX.X, op=ALU.min))
                    v.tensor_tensor(l3, l3, spread(cmn[:, 0:1], [1, 16], [0, NCMP]), ALU.subtract).then_inc(c_lg, 1)
                if k in (10, 15):
                    b = (10, 15).index(k)
                    lc = grid(pc[:, b, 0:1])
                    l3 = pc[:, b, :].rearrange("p (j c) -> p j c", c=32)[:, :, 0:NCMP]
                    ve.wait_ge(c_ex, b + 1)
                    chain(v.tensor_reduce(out=csm, in_=l3, axis=AX.X, op=ALU.add))
                    chain(v.reciprocal(csm, csm))
                    chain(v.tensor_tensor(spread(csm[:, 0:1], [NT, GROUP], [1, NT]), spread(csm[:, 0:1], [NT, GROUP], [1, NT]),
                                          spread(ngt[:, 0, b:b + 1], [2, GROUP], [24, NT]), ALU.mult))
                    chain(v.tensor_tensor(lc, lc, spread(cvalid[:, 0, 0:1], [0, GROUP], [32, NT], [1, NCMP]), ALU.mult))
                    v.tensor_tensor(l3, l3, spread(csm[:, 0:1], [1, 16], [0, NCMP]), ALU.mult).then_inc(c_p, 1)

            def diff_norm(k):
                rr = st[:, ST_DSS + 16:ST_DSS + 32]
                i, part = divmod(k - 2, 4)
                if 0 <= i < NT and part == 0:
                    ve.wait_ge(o_free, DIFF_HEADS)
                    v.tensor_tensor(dk[:, i, :], oacc[:, i, :], oacc[:, i, :], ALU.mult).then_inc(epi_done, 1)
                if 0 <= i < NT and part == 2:
                    ve.wait_ge(epi_done, i + 1)
                    v.tensor_reduce(out=st[:, ST_DSS + 4 * i:ST_DSS + 4 * i + 4],
                                    in_=dk[:, i, :].rearrange("p (h d) -> p h d", d=P), axis=AX.X, op=ALU.add)\
                        .then_inc(epi_sq, 1)
                if k == 22:
                    ve.wait_ge(epi_root, 1)
                    v.reciprocal(rr, rr).then_inc(epi_rr, 1)
                i, part = divmod(k - 24, 4)
                if 0 <= i < NT:
                    heads = lambda x: x[:, i, :].rearrange("p (h d) -> p h d", d=P)
                    if part == 0:
                        ve.wait_ge(epi_rr, 1)
                        v.tensor_tensor(heads(oacc), heads(oacc), spread(rr[:, 4 * i:4 * i + 1], [1, 4], [0, P]), ALU.mult)\
                            .then_inc(epi_zd, 1)
                    if part == 1:
                        v.tensor_tensor(heads(zd), heads(zd), spread(gsub[:, 0:1], [0, 4], [1, P]), ALU.mult)\
                            .then_inc(epi_zd, 1)
                    if part == 2:
                        ve.wait_ge(epi_zd, 3 * i + 2)
                        v.tensor_tensor(zd[:, i, :], zd[:, i, :], oacc[:, i, :], ALU.mult).then_inc(epi_zd, 1)

            def split_act_lo(u):
                ve.wait_ge(a_hi_done, u.act0 + 1)
                o = 4 * (u.act0 % 2)
                v.tensor_tensor(h_lo[:, o:o + u.nk, :], act[:, u.k0:u.k0 + u.nk, :],
                                h_hi[:, o:o + u.nk, :].bitcast(F32), ALU.subtract).then_inc(a_lo_done, 1)

            nth_norm, pending = 0, None
            for kind, body, at in plan:
                if kind == "unit":
                    if body.act and body.act0 + 1 < len(down_units):
                        split_act_lo(down_units[body.act0 + 1])
                    if pending is not None:
                        finish(pending)
                    evacuate(body)
                    pending = body
                    if body.name == "conv_x" and body.tiles[1][3] == 3:
                        ve.wait_ge(sc_evac, body.sc0 + 2)
                        convolve()
                    continue
                if pending is not None:
                    finish(pending)
                    pending = None
                if kind in ("transpose", "final") and (kind == "final" or body["norm"]):
                    ve.wait_ge(roots, nth_norm + 1)
                    nth_norm += 1
                    chain(v.reciprocal(st[:, ST_RR:ST_RR + NT], st[:, ST_RS:ST_RS + NT]))
                    for i in range(NT):
                        r = st[:, ST_RR + i:ST_RR + i + 1]
                        if kind == "transpose":
                            v.tensor_scalar(zs[:, i, :], xres[:, i, :], r, None, ALU.mult).then_inc(xn_done, 1)
                        else:
                            ve.wait_ge(gfin_in, 16)
                            v.scalar_tensor_tensor(zs[:, i, :], xres[:, i, :], r, gfin, ALU.mult, ALU.mult)\
                                .then_inc(y_done, 1)
                if kind == "transpose":
                    h0 = at["h"]
                    for k in range(body["n"]):
                        g = 1.0 if body["gain"] is None else col[:, body["gain"] + k:body["gain"] + k + 1]
                        ve.wait_ge(h_hi_done, h0 + k + 1)
                        v.scalar_tensor_tensor(h_lo[:, k, :], bank[(at["tile"] + k) % 4][:, :], g,
                                               h_hi[:, k, :].bitcast(F32), ALU.mult, ALU.subtract)\
                            .then_inc(h_lo_done, 1)
                if kind == "small_arrays":
                    small_arrays()
                if kind == "attention_1":
                    ve.wait_ge(sc_evac, at["sc"])
                    ve.wait_ge(scratch_in, 16)
                    attend("diff", compress_and_stack)
                    ve.wait_ge(alibi_done, 8)
                    attend("nsa", diff_norm)
                    ve.wait_ge(o_free, GROUPS["diff"] + GROUPS["nsa"])
                    ve.wait_ge(epi_zd, 3 * NT)
                    v.tensor_copy(st[:, ST_C:ST_C + 1], eps).then_inc(attn_done, 1)
                if kind == "index":
                    ve.wait_ge(aux_free, at["aux"])
                    r = 0
                    for i in range(1, NT):
                        for h in range(DSA_HEADS):
                            w = P * (i + 1)
                            ve.wait_ge(ix_relu, r + 1)
                            src = L[:, r % 4, 0:w]
                            if h == 0:
                                v.scalar_tensor_tensor(work_of(i), src, iw[:, i, h:h + 1], mask[:, causal_window(i)],
                                                       ALU.mult, ALU.subtract).then_inc(ix_acc, 1)
                            else:
                                ve.wait_ge(ix_acc, r)
                                v.scalar_tensor_tensor(work_of(i), src, iw[:, i, h:h + 1], work_of(i),
                                                       ALU.mult, ALU.add).then_inc(ix_acc, 1)
                            r += 1
                    ve.wait_ge(ix_acc, r)
                    v.tensor_copy(pm_of(0), mask[:, causal_window(0)])
                    for _ in range(TOPK // 8):
                        for i in range(1, NT):
                            ins = v.max(st[:, ST_TOP + 8 * (i - 1):ST_TOP + 8 * i], work_of(i))
                        chain(ins)
                        for i in range(1, NT):
                            ins = v.match_replace(work_of(i), st[:, ST_TOP + 8 * (i - 1):ST_TOP + 8 * i], work_of(i), TAKEN)
                        chain(ins)
                    for i in range(1, NT):
                        ins = v.tensor_scalar(pm_of(i), work_of(i), TAKEN / 2, BIG, ALU.is_gt, ALU.mult)
                    ins.then_inc(topk_done, 1)
                if kind == "attention_2":
                    ve.wait_ge(topk_done, 1)
                    ve.wait_ge(bias_in, 16)
                    attend("dsa", lambda k: None)
                    ve.wait_ge(o_free, sum(GROUPS.values()))
                    v.tensor_copy(st[:, ST_C:ST_C + 1], eps).then_inc(attn_done, 1)
                if kind == "split":
                    for m, (src, k) in enumerate(split_sources[body]):
                        ve.wait_ge(h_hi_done, at["h"] + m + 1)
                        v.tensor_tensor(h_lo[:, k, :], src, h_hi[:, k, :].bitcast(F32), ALU.subtract)\
                            .then_inc(h_lo_done, 1)
                if kind == "ffn":
                    t0 = at["tile"]

                    def ffn_step(f, tile):
                        for j in range(2):
                            ve.wait_ge(tile_done, f * 4 + (t0 + j + 3))
                            ve.wait_ge(gsilu, f * 2 + (j + 1))
                            v.tensor_tensor(tile(j), bank[(t0 + 2 + j) % 4][:, :], L[:, j, :], ALU.mult).then_inc(act_done, 1)

                    with ve.Fori(0, FFN_STEPS) as f:
                        ffn_step(f, lambda j: pool[:, bass.ds(f * (2 * T) + T * j, T)])
                    split_act_lo(down_units[0])

        @block.tensor
        def _(pe):
            mm = nc.tensor.matmul

            def free_bank(t):
                if t >= 4:
                    name, value = released[t - 4]
                    pe.wait_ge(frees[name], value)

            def three(dst, w_pair, h_pair, start, stop):
                for p, (w, h) in enumerate(((0, 0), (0, 1), (1, 0))):
                    ins = mm(dst, w_pair[w], h_pair[h], start=start and p == 0, stop=stop and p == 2)
                return ins

            fresh = [None]

            def main(u, between):
                n = u.n
                if u.raw:
                    between()
                    pe.wait_ge(raw_in[n % 2], u.arrived)
                    w, kv = slot(raw, n, u), u.evac[1]
                    pe.wait_ge(flat_done, 2 * kv + 2)
                    if u.first and kv == 1:
                        pe.wait_ge(hid_done, 2)
                    for j in range(2):
                        for q in range(u.nk):
                            ins = mm(bank[6 + j][:, 0:2 * NCMP], w[:, q, P * j:P * j + P],
                                     flat[:, kv, u.k0 + q, :], start=u.first and q == 0, stop=u.last and q == u.nk - 1,
                                     skip_group_check=True)
                        if u.last:
                            ins.then_inc(hid_mm, 1)
                    if not u.last:
                        ins.then_inc(part_done, 1)
                    return
                pe.wait_ge(lo_done, u.split)
                hi, lo = slot(w_hi, u.split - 1, u), slot(w_lo, u.split - 1, u)
                if u.tiles:
                    for j, (c0, m, kind, idx) in enumerate(u.tiles):
                        t = u.tile + j
                        free_bank(t)
                        for k in range(u.nk):
                            if j == 0 and fresh[0] is not None:
                                pe.wait_ge(h_lo_done, fresh[0] + u.k0 + k + 1)
                            h = u.k0 + k
                            ins = three(bank[t % 4][0:m, :], (hi[:, k, c0:c0 + m], lo[:, k, c0:c0 + m]),
                                        (h_hi[:, h, :], h_lo[:, h, :]), k == 0, k == u.nk - 1)
                        ins.then_inc(tile_done, 1)
                        if j == 0:
                            between()
                    fresh[0] = None
                    return
                tile = u.tile
                if u.act:
                    pe.wait_ge(a_lo_done, u.act0 + 1)
                for i in range(NT):
                    if u.first:
                        free_bank(tile + i)
                    for k in range(u.nk):
                        h = 4 * (u.act0 % 2) + k if u.act else u.k0 + k
                        if i == 0 and fresh[0] is not None:
                            pe.wait_ge(h_lo_done, fresh[0] + u.k0 + k + 1)
                        cols = slice(P * i, P * i + P)
                        s, e = u.first and k == 0, u.last and k == u.nk - 1
                        for p, (x, w) in enumerate(((h_hi, hi), (h_lo, hi), (h_hi, lo))):
                            ins = mm(bank[(tile + i) % 4][:, :], x[:, h, cols], w[:, k, :],
                                     start=s and p == 0, stop=e and p == 2, skip_group_check=True)
                    if u.last:
                        ins.then_inc(tile_done, 1)
                    if i == 0:
                        between()
                if not u.last:
                    ins.then_inc(part_done, 1)
                if u.last:
                    fresh[0] = None

            def second(u):
                x = u.aux0
                for j, (c0, m, kind, idx) in enumerate(u.tiles or []):
                    if not (kind.startswith("norm") or kind in ("vd", "ng", "viw")):
                        continue
                    pe.wait_ge(aux_in, x + 1)
                    if x >= 2:
                        pe.wait_ge(aux_free, x - 1)
                    else:
                        pe.wait_ge(col_done, 2)
                    dst = bank[4 + x % 2]
                    if kind.startswith("norm"):
                        mm(dst[:, :], ones, L[:, x % 4, :], start=True, stop=True).then_inc(aux_done, 1)
                    else:
                        for i in range(NT):
                            ins = nc.tensor.transpose(dst[:, P * i:P * i + m], L[0:m, x % 4, P * i:P * i + P],
                                                      ident[0:m, 0:m])
                        ins.then_inc(aux_done, 1)
                    x += 1

            def attend(which, between):
                jobs, lag = attention[which], LAG[which]
                for k in range(len(jobs) + lag + 2):
                    between(k)
                    if k < len(jobs):
                        job = jobs[k]
                        n = P * (job["i"] + 1)
                        for c, s in enumerate(job["subs"]):
                            r = job["r"] + c
                            if r >= 3:
                                pe.wait_ge(lg_done, r - 2)
                            wide = n if len(s["q"]) == 1 else max(n, 256)
                            for p, (q, kk) in enumerate(zip(s["q"], s["k"])):
                                ins = mm(bank[S_BANKS[r % 3]][:, 0:wide], q, kk[:, 0:wide], start=p == 0,
                                         stop=p == len(s["q"]) - 1)
                            ins.then_inc(s_done, 1)
                    if 0 <= k - lag < len(jobs):
                        job = jobs[k - lag]
                        dst = t_bank(job["n"])
                        n = job["n"]
                        back = 2 if which == "diff" else 1 if n < len(attention["diff"]) + 3 else 3
                        if n >= back:
                            pe.wait_ge(*all_jobs[n - back]["pt"])
                        if not job["subs"]:
                            o = P * (job["h"] // 2)
                            for j in range(NT):
                                ins = nc.tensor.transpose(dst[0:NCMP, P * j:P * j + P],
                                                          pc[:, job["h"] % 2, o + 32 * j:o + 32 * j + NCMP], ident)
                        else:
                            if which == "diff":
                                pe.wait_ge(p_done, job["n"] + 1)
                            else:
                                pe.wait_ge(scale_done, job["scaled"])
                            for j in range(job["i"] + 1):
                                ins = nc.tensor.transpose(dst[:, P * j:P * j + P], L[:, job["r"] % LRING, P * j:P * j + P],
                                                          ident)
                        ins.then_inc(tr_done, 1)
                    if 0 <= k - lag - 2:
                        job = jobs[k - lag - 2]
                        i, G, pt = job["i"], job["G"], PT[:, job["n"] % 3, :]
                        O = bank[O_BANKS[G % 2]]
                        pe.wait_ge(*job["pt"])
                        if G >= 2 and (k - lag - 2 == 0 or jobs[k - lag - 3]["last"]):
                            pe.wait_ge(o_free, G - 1)
                        if which == "diff":
                            for j in range(i + 1):
                                ins = mm(O[:, P * i:P * i + P], pt[:, P * j:P * j + P], job["v"][j], start=j == 0,
                                         stop=j == i)
                        else:
                            rows = slice(DH * (job["h"] % 2), DH * (job["h"] % 2) + DH)
                            if not job["subs"]:
                                ins = mm(O[rows, :], job["v"][0], pt, start=True, stop=False, skip_group_check=True)
                            for j in range(i + 1 if job["subs"] else 0):
                                ins = mm(O[rows, P * i:P * i + P], job["v"][j], pt[:, P * j:P * j + P],
                                         start=which == "dsa" and j == 0, stop=j == i and (which == "dsa" or job["br"] == 1),
                                         skip_group_check=True)
                        ins.then_inc(pv_done, 1)

            def compress(k):
                if k == 0:
                    for r in range(2):
                        for hh in range(2):
                            ins = mm(bank[0][DH * r:DH * r + DH, 0:2 * NCMP], cmp_w2[:, 0, hh, :], hid[:, 0, hh, :],
                                     start=hh == 0, stop=hh == 1)
                        ins.then_inc(kc_mm, 1)
                if k == 1:
                    pe.wait_ge(kc_sq, 1)
                    mm(bank[0][:, P:P + 2 * NCMP], ones, kc[:, :], start=True, stop=True).then_inc(kc_avg, 1)
                if k == 3:
                    pe.wait_ge(kc_done, 1)
                    for kv in range(KVH):
                        for hh in range(2):
                            ins = mm(bank[0][0:NCMP, DH * kv:DH * kv + DH],
                                     hid[:, 1, hh, NCMP * kv:NCMP * kv + NCMP], cmp_w2[:, 1, hh, :],
                                     start=hh == 0, stop=hh == 1)
                    ins.then_inc(kc_mm, 1)
                if k in (6, 11):
                    b = (6, 11).index(k)
                    if b == 0:
                        pe.wait_ge(kc_sq, 2)
                    else:
                        pe.wait_ge(c_lg, 1)
                    for g in range(GROUP):
                        h, r = 2 * g + b, DH * b
                        kv = h // GROUP
                        for i in range(NT):
                            o = P * g + 32 * i
                            ins = mm(bank[0][:, o:o + NCMP], nq[r:r + DH, h // 2, P * i:P * i + P],
                                     kc_t[r:r + DH, NCMP * kv:NCMP * kv + NCMP], start=True, stop=True)
                    ins.then_inc(c_s, 1)

            def nothing(k):
                pass

            def dsa_stacks(k):
                if k % 4 == 0 and k < len(attention["dsa"]):
                    pe.wait_ge(st_lo, stacked("dsa", 2 + k // 4))

            pe.wait_ge(first_in, 32)
            nc.tensor.transpose(bank[4][:, 0:ND], vec_rows[0:ND, :], ident[0:ND, 0:ND]).then_inc(col_tr, 1)
            nth_norm = n_attn = 0
            pending = None
            for kind, body, at in plan:
                if kind == "unit":
                    before = pending
                    main(body, lambda: before is not None and second(before))
                    pending = body
                    continue
                if pending is not None:
                    second(pending)
                    pending = None
                if kind == "transpose":
                    src = zs if body["norm"] else zd
                    if not body["norm"]:
                        pe.wait_ge(attn_done, n_attn)
                    for k in range(body["n"]):
                        t = at["tile"] + k
                        free_bank(t)
                        for i in range(NT):
                            if body["norm"] and k == 0:
                                pe.wait_ge(xn_done, NT * nth_norm + i + 1)
                            ins = nc.tensor.transpose(bank[t % 4][:, P * i:P * i + P], src[:, i, P * k:P * k + P], ident)
                        ins.then_inc(tile_done, 1)
                    nth_norm += body["norm"]
                    fresh[0] = at["h"]
                if kind == "split" and body != "nsa":
                    fresh[0] = at["h"]
                if kind == "small_arrays":
                    pe.wait_ge(small_in, 16 * N_SMALL)
                    pe.wait_ge(col_done, 1)
                    nc.tensor.transpose(bank[4][:, 0:NROWS], vec_rows[:, :], ident[0:NROWS, 0:NROWS]).then_inc(col_tr, 1)
                    for j in range(2):
                        t, w = at["tile"] + j, (T, BIASW - T)[j]
                        free_bank(t)
                        mm(bank[t % 4][0:DSA_HEADS, 0:w], relb[:, :], onehot[:, T * j:T * j + w], start=True, stop=True)\
                            .then_inc(tile_done, 1)
                if kind == "attention_1":
                    n_attn += 1
                    for j in range(4):
                        free_bank(at["tile"] + j)
                    pe.wait_ge(aux_free, at["aux"])
                    pe.wait_ge(lam_done, 1)
                    pe.wait_ge(hid_done, 4)
                    attend("diff", compress)
                    pe.wait_ge(st_lo, stacked("dsa", 0))
                    pe.wait_ge(c_p, 2)
                    attend("nsa", nothing)
                if kind == "index":
                    pe.wait_ge(aux_free, at["aux"])
                    pe.wait_ge(sc_evac, at["sc"])
                    pe.wait_ge(ve_evac, at["ve"])
                    r = 0
                    for i in range(1, NT):
                        for h in range(DSA_HEADS):
                            w = P * (i + 1)
                            if r >= 3:
                                pe.wait_ge(ix_relu, r - 2)
                            mm(bank[4 + r % 3][:, 0:w], iq[:, h // 2, h % 2, P * i:P * i + P], ik2[:, 0:w],
                               start=True, stop=True).then_inc(ix_s, 1)
                            r += 1
                if kind == "attention_2":
                    n_attn += 1
                    for j in range(4):
                        free_bank(at["tile"] + j)
                    pe.wait_ge(ix_relu, 3 * DSA_HEADS)
                    attend("dsa", dsa_stacks)
                if kind == "ffn":
                    n0, t0, s0 = at["unit"], at["tile"], at["split"]

                    def ffn_step(f, first=False):
                        for j in range(2):
                            pe.wait_ge(lo_done, f * 2 + (s0 + j + 1))
                            hi = w_hi[:, ffn_ring[j], :].rearrange("p (k c) -> p k c", c=256)
                            lo = w_lo[:, ffn_ring[j], :].rearrange("p (k c) -> p k c", c=256)
                            for m in range(2):
                                if first:
                                    free_bank(t0 + 2 * j + m)
                                else:
                                    pe.wait_ge((gsilu, act_done)[j], f * 2 + (m - 1))
                                for k in range(ND):
                                    if first and j == 0 and m == 0:
                                        pe.wait_ge(h_lo_done, at["h"] - ND + k + 1)
                                    ins = three(bank[(t0 + 2 * j + m) % 4][:, :],
                                                (hi[:, k, P * m:P * m + P], lo[:, k, P * m:P * m + P]),
                                                (h_hi[:, k, :], h_lo[:, k, :]), k == 0, k == ND - 1)
                                ins.then_inc(tile_done, 1)

                    ffn_step(0, first=True)
                    with pe.Fori(1, FFN_STEPS) as f:
                        ffn_step(f)
                    fresh[0] = None


_INS = ["x", "norm_g", "w_in", "diff_q_norm_g", "diff_k_norm_g", "diff_lambda_q1", "diff_lambda_k1",
        "diff_lambda_q2", "diff_lambda_k2", "diff_subln_g", "nsa_q_norm_g", "nsa_k_norm_g", "cmp_pos", "cmp_w1",
        "cmp_b1", "cmp_w2", "w_out", "g_mix_2", "w_in_2", "b_gate_2", "conv_w_2", "w_branch_a_2", "w_branch_b_2",
        "w_out_2", "rel_bias_2", "g_ffn_2", "w_ffn_gate_2", "w_ffn_up_2", "w_ffn_down_2", "g_final_2"]


def kernel(**inputs):
    import concourse.bacc as bacc
    from concourse.bass_utils import run_bass_kernel_spmd

    nc = bacc.Bacc("TRN2", target_bir_lowering=False, num_devices=1)
    arrays = {name: np.ascontiguousarray(inputs[name]) for name in _INS}
    arrays["g_final_2"] = arrays["g_final_2"].reshape(1, D)
    arrays["const"], arrays["distance"], arrays["onehot"] = shape_constants()
    ins = {name: nc.dram_tensor(f"in_{name}", x.shape, mybir.dt.from_np(x.dtype), kind="ExternalInput").ap()
           for name, x in arrays.items()}
    out = nc.dram_tensor("out_0", (1, T, D), mybir.dt.float32, kind="ExternalOutput").ap()
    build(nc, ins, out)
    r = run_bass_kernel_spmd(nc, [{f"in_{name}": x for name, x in arrays.items()}], core_ids=[0])
    return r.results[0]["out_0"]
```

```python
import math
from contextlib import ExitStack

import concourse.bass as bass
import numpy as np
from concourse import mybir

P = 128
T = 512
D = 1024
NT = T // P
ND = D // P
DH = 64
DIFF_HEADS = 4
NSA_HEADS = 8
KVH = 2
GROUP = NSA_HEADS // KVH
CMP_BLOCK, CMP_STRIDE, CMP_HIDDEN = 32, 16, 256
NCMP = (T - CMP_BLOCK) // CMP_STRIDE + 1
NPAIR = CMP_BLOCK // 2
SEL_BLOCK, SEL_TOPK, WINDOW = 64, 8, 512
assert SEL_TOPK * SEL_BLOCK >= T and WINDOW >= T
DSA_HEADS = 8
TOPK = min(256, T // 4)
BUCKETS, MAX_EXACT, MAX_DISTANCE = 32, 16, 128
DFF = 2816
NFF = DFF // P
LRING = 7
EPS = 1e-6
LAM_INIT = 0.8 - 0.6 * math.exp(0.0)
BIG = 1e30
TAKEN = -3e38
BIASW = 640

C_DQ, C_DK, C_DV, C_DZ, C_NQ, C_KV, C_NZ, C_NG = 0, 512, 1024, 1536, 2048, 2560, 3328, 3840
C_CB, C_CC, C_CX, C_Q, C_K, C_V, C_IQ, C_IK, C_IW, C_GA, C_GB = (
    0, 512, 1024, 1536, 2048, 2112, 2176, 2688, 2752, 2760, 3784)

R_NORM, R_MIX, R_FFN, R_BGATE, R_CONV, R_B1, R_POS = 0, 8, 16, 24, 40, 52, 56
R_GDQ, R_GDK, R_GNQ, R_GKC, R_GKS, R_GKW = 88, 89, 90, 91, 92, 93
NROWS = 94
N_SMALL = 23
K_IDENT, K_ONES, K_MASK, K_CMASK, K_CVALID, K_END = 0, 128, 256, 768, 896, 1024


def shape_constants():
    p = np.arange(P)[:, None]
    x = np.arange(T)[None, :]
    dist = (T - P) + p - x
    mask = np.where(dist < 0, BIG, 0.0)
    ones = np.kron(np.eye(2), np.ones((DH, DH)) / DH)
    c = np.arange(32)[None, None, :]
    t = np.arange(P)[:, None, None] + P * np.arange(NT)[None, :, None]
    ok = (c * CMP_STRIDE + CMP_BLOCK - 1 <= t) & (c < NCMP)
    const = np.concatenate([np.eye(P), ones, mask, np.where(ok, 0.0, BIG).reshape(P, -1),
                            np.where(ok, 1.0, 0.0).reshape(P, -1)], 1).astype(np.float32)
    distance = np.maximum(dist, 0).astype(np.float32)
    n = np.arange(BIASW) - (P - 1)
    large = MAX_EXACT + np.floor(np.log(np.maximum(n, 1) / MAX_EXACT) / math.log(MAX_DISTANCE / MAX_EXACT)
                                 * (BUCKETS - MAX_EXACT) + 1e-9).astype(np.int64)
    bucket = np.where(n < MAX_EXACT, n, np.minimum(large, BUCKETS - 1))
    onehot = ((np.arange(BUCKETS)[:, None] == bucket[None, :]) & ((n >= 0) & (n < T))[None, :]).astype(np.float32)
    return const, distance, onehot


class Unit:

    def __init__(self, name, parts, nk, width, tiles=None, k0=0, evac=None, first=True, last=True, raw=False,
                 aux=0, act=False):
        self.name, self.parts, self.nk, self.width = name, parts, nk, width
        self.tiles, self.k0, self.evac = tiles, k0, evac
        self.first, self.last, self.raw, self.aux, self.act = first, last, raw, aux, act


def build(nc, a, out):
    F32, F32R = mybir.dt.float32, mybir.dt.float32r
    ACT, ALU, AX = mybir.ActivationFunctionType, mybir.AluOpType, mybir.AxisListType

    def rows_of(w, r0, nk, c0, width):
        return w[r0 * P:(r0 + nk) * P, c0:c0 + width].rearrange("(k p) n -> p k n", p=P)

    steps = []

    def feature_units(name, w, c0, n, evac, aux=0, first_index=0):
        for j in range(n):
            steps.append(("unit", Unit(name, [(rows_of(w, 0, ND, c0 + 256 * j, 256), 0, 256)], ND, 256,
                                       tiles=[(0, P, evac, first_index + 2 * j), (P, P, evac, first_index + 2 * j + 1)],
                                       aux=aux)))

    def token_units(name, w, c0, evac, half, ktiles=ND, act=False):
        n = -(-ktiles // 4)
        starts = [0]
        for j in range(n - 1):
            starts.append(starts[-1] + (4 if j < n - (4 * n - ktiles) else 3))
        for s, end in zip(starts, starts[1:] + [ktiles]):
            nk = end - s
            steps.append(("unit", Unit(name, [(rows_of(w, s, nk, c0, 512), 0, 512)], nk, 512, k0=s,
                                       evac=(evac, half), first=s == 0, last=s == starts[-1], act=act)))

    w1in, w2in = a["w_in"][0], a["w_in_2"][0]

    def cmp_unit(kv, half):
        w1 = a["cmp_w1"][0, kv].rearrange("(q p) n -> p q n", p=P)
        steps.append(("unit", Unit("cmp_w1", [(w1[:, 8 * half:8 * half + 8, :], 0, CMP_HIDDEN)], 8, CMP_HIDDEN,
                                   k0=8 * half, evac=("hidden", kv), first=half == 0, last=half == 1, raw=True)))

    steps.append(("transpose", dict(norm=True, gain=R_NORM, n=ND)))
    steps.append(("small_arrays", None))
    feature_units("diff_q", w1in, C_DQ, 2, "norm_dq", aux=2)
    steps.append(("unit", Unit("cmp_kv", [(rows_of(w1in, 0, ND, C_KV, 256), 0, 256)], ND, 256,
                               tiles=[(0, P, "cmp", 0), (P, P, "cmp", 1)])))
    feature_units("diff_k", w1in, C_DK, 1, "norm_dk", aux=2)
    cmp_unit(0, 0)
    feature_units("diff_k", w1in, C_DK + 256, 1, "norm_dk", aux=2, first_index=2)
    cmp_unit(0, 1)
    feature_units("nsa_q", w1in, C_NQ, 1, "norm_nq", aux=2)
    cmp_unit(1, 0)
    feature_units("nsa_q", w1in, C_NQ + 256, 1, "norm_nq", aux=2, first_index=2)
    cmp_unit(1, 1)
    steps.append(("unit", Unit("nsa_k", [(rows_of(w1in, 0, ND, C_KV + 256, 128), 0, 128),
                                         (rows_of(w1in, 0, ND, C_KV + 512, 128), 128, 128)], ND, 256,
                               tiles=[(0, P, "norm_kd", 0), (P, P, "norm_kd", 1)], aux=2)))
    steps.append(("unit", Unit("nsa_v", [(rows_of(w1in, 0, ND, C_KV + 384, 128), 0, 128),
                                         (rows_of(w1in, 0, ND, C_KV + 640, 128), 128, 128)], ND, 256,
                               tiles=[(0, P, "vd", 0), (P, P, "vd", 1)], aux=2)))
    steps.append(("unit", Unit("nsa_gate", [(rows_of(w1in, 0, ND, C_NG - 96, 120), 0, 120)], ND, 120,
                               tiles=[(0, 120, "ng", 0)], aux=1)))
    token_units("diff_z", w1in, C_DZ, "z", 0)
    feature_units("nsa_z", w1in, C_NZ, 2, "nz")
    token_units("diff_v", w1in, C_DV, "dv", 0)
    steps.append(("attention_1", None))
    steps.append(("transpose", dict(norm=False, gain=None, n=DIFF_HEADS)))
    steps.append(("split", "nsa"))
    token_units("out_1", a["w_out"][0], 0, "residual", 0)
    token_units("out_1", a["w_out"][0], 512, "residual", 1)
    steps.append(("transpose", dict(norm=True, gain=R_MIX, n=ND)))
    feature_units("index_q", w2in, C_IQ, 2, "iq")
    steps.append(("unit", Unit("k_ik_v_iw", [(rows_of(w2in, 0, ND, C_K, 64), 0, 64),
                                             (rows_of(w2in, 0, ND, C_IK, 64), 64, 64),
                                             (rows_of(w2in, 0, ND, C_V, 64), 128, 64),
                                             (rows_of(w2in, 0, ND, C_IW, 8), 192, 8)], ND, 200,
                               tiles=[(0, P, "kik", 0), (P, 72, "viw", 0)], aux=1)))
    steps.append(("index", None))
    feature_units("q", w2in, C_Q, 2, "q2")
    feature_units("conv_b", w2in, C_CB, 2, "cb")
    feature_units("conv_c", w2in, C_CC, 2, "cc")
    feature_units("conv_x", w2in, C_CX, 2, "cx")
    feature_units("gates_a", w2in, C_GA, 4, "gate", first_index=0)
    feature_units("gates_b", w2in, C_GB, 4, "gate", first_index=8)
    steps.append(("attention_2", None))
    steps.append(("split", "branches"))
    for name, w, k0 in (("branch_a", a["w_branch_a_2"][0], 0), ("branch_b", a["w_branch_b_2"][0], 4)):
        for half in range(2):
            steps.append(("unit", Unit(name, [(rows_of(w, 0, 4, 512 * half, 512), 0, 512)], 4, 512, k0=k0,
                                       tiles=[(P * j, P, name, 4 * half + j) for j in range(4)])))
    steps.append(("split", "merged"))
    token_units("out_2", a["w_out_2"][0], 0, "residual", 0)
    token_units("out_2", a["w_out_2"][0], 512, "residual", 1)
    steps.append(("transpose", dict(norm=True, gain=R_FFN, n=ND)))
    steps.append(("ffn", None))
    FFN_STEPS = DFF // 256
    token_units("down", a["w_ffn_down_2"][0], 0, "residual", 0, ktiles=NFF, act=True)
    token_units("down", a["w_ffn_down_2"][0], 512, "residual", 1, ktiles=NFF, act=True)
    steps.append(("final", None))

    n_unit = n_split = n_tile = n_part = n_aux = n_h = n_act = n_res = n_sc = n_ve = n_branch = n_hid = 0
    ring_in = [0, 0]
    plan = []
    released = []
    units = []
    for kind, body in steps:
        at = dict(unit=n_unit, split=n_split, tile=n_tile, part=n_part, aux=n_aux, h=n_h, act=n_act, res=n_res,
                  sc=n_sc, ve=n_ve)
        plan.append((kind, body, at))
        if kind == "unit":
            ntiles = len(body.tiles) if body.tiles else (NT if body.last and not body.raw else 0)
            body.n, body.tile, body.ntiles = n_unit, n_tile, ntiles
            ring_in[n_unit % 2] += 16 * len(body.parts)
            body.arrived = ring_in[n_unit % 2]
            n_unit += 1
            n_split += not body.raw
            body.split = n_split
            n_tile += ntiles
            if not body.tiles and not body.last:
                n_part += 1
            elif body.raw:
                n_hid += 2
            body.part, body.hid = n_part, n_hid
            body.tile_end = n_tile
            body.aux0 = n_aux
            n_aux += body.aux
            body.act0 = n_act
            n_act += body.act
            body.sc0, body.ve0, body.res0, body.branch0, x = n_sc, n_ve, n_res, n_branch, body.aux0
            for tile_kind in ([t[2] for t in body.tiles] if body.tiles else [body.evac[0]] * ntiles):
                if tile_kind.startswith("norm"):
                    x += 1
                    released.append(("aux_free", x))
                elif tile_kind in ("vd", "ng", "viw"):
                    x += 1
                    released.append(("aux_in", x))
                elif tile_kind in ("cmp", "kik"):
                    n_ve += 1
                    released.append(("ve_evac", n_ve))
                elif tile_kind == "residual":
                    n_res += 1
                    released.append(("res_done", n_res))
                elif tile_kind.startswith("branch"):
                    n_branch += 1
                    released.append(("branch_done", n_branch))
                else:
                    n_sc += 1
                    released.append(("sc_evac", n_sc))
            units.append(body)
        elif kind == "transpose":
            n_tile += body["n"]
            for _ in range(body["n"]):
                n_h += 1
                released.append(("h_lo_done", n_h))
        elif kind == "split":
            n_h += 4 if body == "nsa" else ND
        elif kind == "small_arrays":
            n_tile += 2
            released += [("rows_done", 1), ("rows_done", 2)]
        elif kind == "ffn":
            ffn_slots = n_unit % 2, (n_unit + 1) % 2
            ffn_ring = n_split % 2, (n_split + 1) % 2
            for _ in range(FFN_STEPS):
                for j in range(2):
                    ring_in[ffn_slots[j]] += 16
                    u = Unit("ffn", None, ND, 256)
                    n_tile += 2
                    n_split += 1
                    released += [("gsilu" if j == 0 else "act_done", 2 * _ + 1), ("gsilu" if j == 0 else "act_done", 2 * _ + 2)]
                    u.n, u.arrived, u.split, u.part, u.tile_end = n_unit, ring_in[ffn_slots[j]], n_split, n_part, n_tile
                    n_unit += 1
                    units.append(u)

    ctx = ExitStack()
    with ctx:
        def sb(name, shape, dt=F32):
            return ctx.enter_context(nc.sbuf_tensor(name, shape, dt))

        def sem(name):
            return ctx.enter_context(nc.semaphore(name))

        const = sb("const", [P, K_END])
        col = sb("col", [P, NROWS])
        relb = sb("relb", [BUCKETS, DSA_HEADS])
        lam_in = sb("lam_in", [P, 4, DH])
        gsub = sb("gsub", [P, P])
        cmp_w2 = sb("cmp_w2", [P, 2, 2, DH])
        raw = sb("raw", [P, 2, 2048])
        w_hi = sb("w_hi", [P, 2, 2048], F32R)
        w_lo = sb("w_lo", [P, 2, 2048], F32R)
        h_hi = sb("h_hi", [P, ND, T], F32R)
        h_lo = sb("h_lo", [P, ND, T], F32R)
        xres = sb("xres", [P, NT, D])
        zs = sb("zs", [P, NT, D])
        pool = sb("pool", [P, 16384])
        L = sb("L", [P, LRING, T])
        PT = sb("PT", [P, 3, T])
        st = sb("st", [P, 256])
        hid = sb("hid", [P, 2, 2, 2 * NCMP])
        kc = sb("kc", [P, 2 * NCMP])
        kc_t = sb("kc_t", [P, 2 * NCMP])
        vc = sb("vc", [P, KVH, DH])
        ngt = sb("ngt", [P, NT, 24])
        vec_rows = PT[0:NROWS, 0, 0:P]
        onehot = PT[:, :, :].rearrange("p a n -> p (a n)")[0:BUCKETS, P:P + BIASW]
        bias_row = L[0:DSA_HEADS, 4:6, :].rearrange("p a n -> p (a n)")

        ident = const[:, K_IDENT:K_IDENT + P]
        ones = const[:, K_ONES:K_ONES + P]
        mask = const[:, K_MASK:K_MASK + T]
        cmask = const[:, K_CMASK:K_CMASK + P].rearrange("p (i c) -> p i c", c=32)
        cvalid = const[:, K_CVALID:K_CVALID + P].rearrange("p (i c) -> p i c", c=32)

        def region(start, *shape):
            n = int(np.prod(shape))
            v = pool[:, start:start + n]
            if len(shape) == 2:
                v = v.rearrange("p (a b) -> p a b", b=shape[1])
            if len(shape) == 3:
                v = v.rearrange("p (a b c) -> p a b c", b=shape[1], c=shape[2])
            return v

        zflat = zs[:, :, :].rearrange("p a b -> p (a b)")
        dq = region(0, DIFF_HEADS, 2, T)
        dk, nq, dv = (region(4096 + 2048 * j, 4, T) for j in range(3))
        kd = region(10240, 2, T)
        vd = region(11264, 2, NT, P)
        oacc = region(12288, NT, 512)
        flat = region(12288, 2, NPAIR, 2 * NCMP)
        pc = region(14336, 2, 512)
        causal_distance = region(15360, T)
        shifted = zflat[:, 0:2048].rearrange("p (a b c) -> p a b c", a=2, b=KVH)
        zd = zflat[:, 0:2048].rearrange("p (i n) -> p i n", i=NT)
        nzt = zflat[:, 2048:4096].rearrange("p (m n) -> p m n", m=4)
        q2, k2, v2 = region(0, 4, T), region(2048, T), region(2560, NT, DH)
        pm = region(2816, 1280)
        bh = region(4096, DSA_HEADS, T)
        iq = region(8192, 4, 2, T)
        cc, cx = region(12288, 4, T), region(14336, 4, T)
        ot2 = zflat[:, 0:2048].rearrange("p (m n) -> p m n", m=4)
        ya = zflat[:, 2048:4096].rearrange("p (m n) -> p m n", m=4)
        ik2, work = zflat[:, 0:512], zflat[:, 512:1664]
        iw = zflat[:, 1664:1664 + 8 * NT].rearrange("p (i h) -> p i h", i=NT)

        def gate(j):
            return pool[:, 8192 + T * j:8192 + T * j + T]

        split_sources = dict(nsa=[(nzt[:, m, :], 4 + m) for m in range(4)],
                             branches=[(ya[:, m, :], m) for m in range(4)] + [(ot2[:, m, :], 4 + m) for m in range(4)],
                             merged=[(gate(m), m) for m in range(ND)])
        act = region(0, NFF, T)
        gfin = region(NFF * T, D)

        def causal_window(i):
            return slice(T - P - P * i, T)

        def work_of(i):
            o = {1: 0, 2: 256, 3: 640}[i]
            return work[:, o:o + P * (i + 1)]

        def pm_of(i):
            o = P * (i * (i + 1) // 2)
            return pm[:, o:o + P * (i + 1)]

        bank = [ctx.enter_context(nc.psum_tensor(f"bank{j}", [P, T], F32)) for j in range(8)]
        S_BANKS, O_BANKS = [4, 5, 3], [2, 7]

        ST_MN, ST_SM, ST_C = 0, 16, 72
        ST_EPS, ST_NEGLAM, ST_SS, ST_RS, ST_RR, ST_LAM = 80, 81, 84, 64, 92, 96
        ST_CMN, ST_CSM, ST_TOP, ST_DSS = 100, 116, 132, 160
        ST_C2 = 192
        ST_DR = 32
        eps = st[:, ST_EPS:ST_EPS + 1]
        neglam = st[:, ST_NEGLAM:ST_NEGLAM + 1]

        first_in, small_in = sem("first_in"), sem("small_in")
        x_in = [sem(f"x_in{i}") for i in range(NT)]
        raw_in = [sem("raw_in0"), sem("raw_in1")]
        hi_done, lo_done, part_done, tile_done = sem("hi_done"), sem("lo_done"), sem("part_done"), sem("tile_done")
        sc_evac, ve_evac, res_done, branch_done = sem("sc_evac"), sem("ve_evac"), sem("res_done"), sem("branch_done")
        col_tr, col_done, setup_done, eps_done = sem("col_tr"), sem("col_done"), sem("setup_done"), sem("eps_done")
        lam_dot, lam_exp, lam_done, zero_done = sem("lam_dot"), sem("lam_exp"), sem("lam_done"), sem("zero_done")
        squares, roots, xn_done, h_hi_done = sem("squares"), sem("roots"), sem("xn_done"), sem("h_hi_done")
        h_lo_done = sem("h_lo_done")
        aux_in, aux_done, aux_root, aux_free = sem("aux_in"), sem("aux_done"), sem("aux_root"), sem("aux_free")
        dve_step = sem("dve_step")
        s_done, lg_done, ex_done = sem("s_done"), sem("lg_done"), sem("ex_done")
        p_done, coef_done, scale_done, tr_done = sem("p_done"), sem("coef_done"), sem("scale_done"), sem("tr_done")
        pt_done, pv_done = sem("pt_done"), sem("pv_done")
        o_free, attn_done, sums_done, stack_hi_done = sem("o_free"), sem("attn_done"), sem("sums_done"), sem("stack_hi_done")
        stack_lo_done, first_stacks_done, alibi_done = sem("stack_lo_done"), sem("first_stacks_done"), sem("alibi_done")
        flat_done, hid_mm, hid_done, kc_mm = sem("flat_done"), sem("hid_mm"), sem("hid_done"), sem("kc_mm")
        kc_squares, kc_avg, kc_root, kc_done = sem("kc_squares"), sem("kc_avg"), sem("kc_root"), sem("kc_done")
        cmp_s_done, cmp_lg_done, cmp_ex_done, cmp_p_done = sem("cmp_s_done"), sem("cmp_lg_done"), sem("cmp_ex_done"), sem("cmp_p_done")
        diff_squares, diff_sums, diff_root, diff_recip = sem("diff_squares"), sem("diff_sums"), sem("diff_root"), sem("diff_recip")
        diff_out = sem("diff_out")
        rows_done, scratch_in, bias_in = sem("rows_done"), sem("scratch_in"), sem("bias_in")
        ix_s, ix_relu, ix_acc, topk_done = sem("ix_s"), sem("ix_relu"), sem("ix_acc"), sem("topk_done")
        conv_done = sem("conv_done")
        gsilu, act_done, a_hi_done, a_lo_done = sem("gsilu"), sem("act_done"), sem("a_hi_done"), sem("a_lo_done")
        gfin_in, y_done, out_done = sem("gfin_in"), sem("y_done"), sem("out_done")

        bias_dram = nc.dram_tensor("bias_dram", [DSA_HEADS, BIASW], F32, kind="Internal").ap()

        def used(n):
            u = units[n]
            if u.raw:
                return (hid_mm, u.hid) if u.last else (part_done, u.part)
            if u.name != "ffn" and not u.tiles and not u.last:
                return part_done, u.part
            return tile_done, u.tile_end

        frees = dict(aux_free=aux_free, aux_in=aux_in, ve_evac=ve_evac, res_done=res_done, branch_done=branch_done,
                     sc_evac=sc_evac, h_lo_done=h_lo_done, rows_done=rows_done, gsilu=gsilu, act_done=act_done)

        at_attention_1 = next(at for kind, _, at in plan if kind == "attention_1")
        at_attention_2 = next(at for kind, _, at in plan if kind == "attention_2")
        split_units = [u for u in units if not u.raw]

        def slot(t, n, u):
            return t[:, n % 2, 0:u.nk * u.width].rearrange("p (k c) -> p k c", c=u.width)

        down_units = [u for u in units if u.act]
        early_splits = dict(nsa=0, branches=4, merged=4)
        at_split = {body: at for kind, body, at in plan if kind == "split"}
        last_branch_unit = [u for u in split_units if u.name == "branch_b"][-1]
        branch_a_end = max(u.tile_end for u in split_units if u.name == "branch_a")

        def act_pieces(u):
            o = 4 * (u.act0 % 2)
            return [(o + k, u.k0 + k, 1) for k in range(u.nk)] if u.act0 == 0 else [(o, u.k0, u.nk)]

        def act_done_at(u, j):
            return j + 1 if u.act0 == 0 else down_units[0].nk + u.act0

        def q_stack(h):
            return h_hi[:, h, :]

        def k_stack(br, kv, part):
            return h_lo[:, 4 * br + 2 * kv + part, :]

        def jobs_of(which):
            jobs = []
            if which == "diff":
                for h in range(DIFF_HEADS):
                    for i in range(NT):
                        subs = [dict(q=[dq[:, h, c, P * i:P * i + P]], k=[dk[:, h, :]], bias=alibi(2 * h + 1))
                                for c in range(2)]
                        jobs.append(dict(g=h, i=i, subs=subs, v=[dv[:, j, P * h:P * h + P] for j in range(i + 1)]))
            if which == "nsa":
                for h in range(NSA_HEADS):
                    kv = h // GROUP
                    jobs.append(dict(g=h // 2, i=NT - 1, h=h, br=-1, subs=[], v=[vc[:, kv, :]]))
                    for br in range(2):
                        for i in range(NT):
                            q = q_stack(h)[:, P * i:P * i + P]
                            subs = [dict(q=[q, q], k=[k_stack(br, kv, 0), k_stack(br, kv, 1)], bias=alibi(h))]
                            jobs.append(dict(g=h // 2, i=i, subs=subs, h=h, br=br,
                                             v=[vd[:, br, j, DH * kv:DH * kv + DH] for j in range(i + 1)]))
            if which == "dsa":
                for h in range(DSA_HEADS):
                    for i in range(NT):
                        q = q_stack(h)[:, P * i:P * i + P]
                        subs = [dict(q=[q, q], k=[k_stack(1, 1, 0), k_stack(1, 1, 1)], bias=bh[:, h, :],
                                     select=pm_of(i))]
                        jobs.append(dict(g=h // 2, i=i, subs=subs, h=h, br=0, v=[v2[:, j, :] for j in range(i + 1)]))
            return jobs

        def alibi(m):
            z = (at_attention_1["unit"] + m) % 2
            return raw[:, z, T * (m // 2):T * (m // 2) + T]

        attention = {w: jobs_of(w) for w in ("diff", "nsa", "dsa")}
        sub_n = job_n = group_n = scaled = 0
        for w in ("diff", "nsa", "dsa"):
            for m, j in enumerate(attention[w]):
                j["r"], j["n"], j["G"] = sub_n, job_n, group_n + j["g"]
                j["last"] = m + 1 == len(attention[w]) or attention[w][m + 1]["g"] != j["g"]
                scaled += w != "diff" and j["subs"] != []
                j["scaled"] = scaled
                sub_n += len(j["subs"])
                job_n += 1
            group_n += attention[w][-1]["g"] + 1
        job_of_sub = [j for w in ("diff", "nsa", "dsa") for j in attention[w] for _ in j["subs"]]
        def t_bank(n):
            return bank[(6, 1)[n % 2]] if n < len(attention["diff"]) else bank[(6, 1, 0)[(n + 1) % 3]]

        GROUPS = {"diff": DIFF_HEADS, "nsa": NSA_HEADS // 2, "dsa": DSA_HEADS // 2}
        LAG = {"diff": 3, "nsa": 5, "dsa": 4}

        def stat(base, job, c):
            o = base + 2 * (job["n"] % 8) + c
            return st[:, o:o + 1]

        def sum_of(job, c):
            if len(job["subs"]) == 2 and c == 0:
                return st[:, ST_DR + job["n"]:ST_DR + job["n"] + 1]
            return stat(ST_SM, job, c)

        stack_items = {"nsa": [("k", br, kv) for br in range(2) for kv in range(KVH)] + [("q", h) for h in range(NSA_HEADS)],
                       "dsa": [("k", 1, 1)] + [("q", h) for h in range(DSA_HEADS)]}

        def stacked(which, m):
            items = stack_items["nsa"] + stack_items["dsa"][3:m] if which == "dsa" else stack_items["nsa"][:m]
            return sum(2 if item[0] == "k" else 1 for item in items)

        def stack_source(which, item):
            if item[0] == "q":
                h = item[1]
                r = DH * (h % 2)
                return (nq if which == "nsa" else q2)[r:r + DH, h // 2, :], r
            if which == "nsa":
                r = DH * item[2]
                return kd[r:r + DH, item[1], :], r
            return k2, 0

        def lower_pieces(which, m):
            item = stack_items[which][m]
            src, r = stack_source(which, item)
            if item[0] == "q":
                q = q_stack(item[1])
                return [(q[DH - r:P - r, :], src, q[r:r + DH, :].bitcast(F32))]
            hi, lo = k_stack(item[1], item[2], 0), k_stack(item[1], item[2], 1)
            if which == "dsa":
                return [(lo, src, hi.bitcast(F32))]
            return [(lo[half:half + DH, :], src, hi[r:r + DH, :].bitcast(F32)) for half in (0, DH)]

        block = ctx.enter_context(nc.Block())

        @block.sync
        def _(sp):
            def load(u):
                if u.n >= 2:
                    before = units[u.n - 2]
                    if before.raw:
                        sp.wait_ge(*used(u.n - 2))
                    else:
                        sp.wait_ge(lo_done, before.split)
                if u.n == at_attention_1["unit"] + 1:
                    sp.wait_ge(attn_done, 1)
                for src, c0, width in u.parts:
                    sp.dma_start(slot(raw, u.n, u)[:, :, c0:c0 + width], src).then_inc(raw_in[u.n % 2], 16)

            def small_loads():
                rows = [(R_MIX, a["g_mix_2"][0].rearrange("(r c) -> r c", c=P)),
                        (R_FFN, a["g_ffn_2"][0].rearrange("(r c) -> r c", c=P)),
                        (R_BGATE, a["b_gate_2"][0].rearrange("(r c) -> r c", c=P)),
                        (R_CONV, a["conv_w_2"][0].rearrange("k (r c) -> (k r) c", c=P)),
                        (R_B1, a["cmp_b1"][0].rearrange("k (r c) -> (k r) c", c=P)),
                        (R_POS, a["cmp_pos"][0].rearrange("k (q b) d -> (k q) (b d)", b=2))]
                n_small = 0

                def small(dst, src):
                    nonlocal n_small
                    sp.dma_start(dst, src).then_inc(small_in, 16)
                    n_small += 1

                for r, src in rows:
                    small(vec_rows[r:r + src.shape[0], :], src)
                for half in range(2):
                    cols = slice(DH * half, DH * half + DH)
                    small(vec_rows[R_GDQ:R_GDQ + 1, cols], a["diff_q_norm_g"])
                    small(vec_rows[R_GDK:R_GDK + 1, cols], a["diff_k_norm_g"])
                    small(vec_rows[R_GNQ:R_GNQ + 1, cols], a["nsa_q_norm_g"])
                    small(vec_rows[R_GKC:R_GKC + 3, cols], a["nsa_k_norm_g"][0])
                for j, name in enumerate(("diff_lambda_q1", "diff_lambda_k1", "diff_lambda_q2", "diff_lambda_k2")):
                    small(lam_in[:, j, :], a[name].to_broadcast([P, DH]))
                small(gsub[:, :], a["diff_subln_g"].to_broadcast([P, P]))
                small(relb[:, :], a["rel_bias_2"])
                small(onehot[:, :], a["onehot"])
                small(cmp_w2[:, :, :, :], a["cmp_w2"][0].rearrange("k (h p) d -> p k h d", p=P))
                small(L[:, 0, :], a["distance"])
                assert n_small == N_SMALL

            for i in range(NT):
                sp.dma_start(xres[:, i, :], a["x"][0, P * i:P * i + P, :]).then_inc(x_in[i], 16)
            sp.dma_start(const[:, :], a["const"]).then_inc(first_in, 16)
            sp.dma_start(vec_rows[R_NORM:R_NORM + ND, :], a["norm_g"][0].rearrange("(r c) -> r c", c=P))\
              .then_inc(first_in, 16)
            for kind, body, at in plan:
                if kind == "unit":
                    load(body)
                    if body.n == 0:
                        small_loads()
                if kind == "ffn":
                    wg, wu = a["w_ffn_gate_2"][0], a["w_ffn_up_2"][0]
                    with sp.Fori(0, FFN_STEPS) as f:
                        for j, w in enumerate((wg, wu)):
                            sp.wait_ge(lo_done, f * 2 + (at["split"] - 1 + j))
                            sp.dma_start(raw[:, ffn_slots[j], :].rearrange("p (k c) -> p k c", c=256),
                                         w.rearrange("(k p) n -> p k n", p=P)[:, :, bass.ds(f * 256, 256)])\
                              .then_inc(raw_in[ffn_slots[j]], 16)
            sp.dma_start(gfin, a["g_final_2"].to_broadcast([P, D])).then_inc(gfin_in, 16)
            for i in range(NT):
                sp.wait_ge(y_done, i + 1)
                sp.dma_start(out[0, P * i:P * i + P, :], zs[:, i, :]).then_inc(out_done, 16)
            sp.wait_ge(out_done, 16 * NT)

        @block.gpsimd
        def _(pool_e):
            def split_lo(s):
                if s >= len(split_units):
                    return
                u = split_units[s]
                pool_e.wait_ge(hi_done, s + 1)
                size = u.nk * u.width
                nc.gpsimd.tensor_tensor(w_lo[:, s % 2, 0:size], raw[:, u.n % 2, 0:size],
                                        w_hi[:, s % 2, 0:size].bitcast(F32), ALU.subtract).then_inc(lo_done, 1)

            def scale(which):
                for k, job in enumerate(attention[which]):
                    if which == "dsa" and k % 4 == 0 and 3 + k // 4 < len(stack_items["dsa"]):
                        if k > 0:
                            pool_e.wait_ge(scale_done, job["scaled"] - 1)
                        else:
                            pool_e.wait_ge(lo_done, at_attention_2["split"] + 1)
                        stack_lo("dsa", 3 + k // 4)
                    if not job["subs"]:
                        continue
                    m = k // 4 - 2
                    if which == "dsa" and k % 4 == 2 and 0 <= m < early_splits["branches"]:
                        src, t = split_sources["branches"][m]
                        pool_e.wait_ge(h_hi_done, at_split["branches"]["h"] + m + 1)
                        nc.gpsimd.tensor_tensor(h_lo[:, t, :], src, h_hi[:, t, :].bitcast(F32), ALU.subtract)\
                            .then_inc(h_lo_done, 1)
                    r, n = job["r"], P * (job["i"] + 1)
                    pool_e.wait_ge(coef_done, job["scaled"])
                    nc.gpsimd.tensor_tensor(L[:, r % LRING, 0:n], L[:, r % LRING, 0:n],
                                            stat(ST_C2, job, 0).to_broadcast([P, n]), ALU.mult).then_inc(scale_done, 1)

            def stack_lo(which, m):
                pool_e.wait_ge(stack_hi_done, m + 1 + (len(stack_items["nsa"]) if which == "dsa" else 0))
                for j, (lo, src, hi) in enumerate(lower_pieces(which, m)):
                    nc.gpsimd.tensor_tensor(lo, src, hi, ALU.subtract).then_inc(stack_lo_done, 1)
                    pool_e.wait_ge(stack_lo_done, stacked(which, m) + j + 1)

            zeroed = 0

            def zero(x):
                nonlocal zeroed
                nc.gpsimd.memset(x, 0.0).then_inc(zero_done, 1)
                zeroed += 1
                pool_e.wait_ge(zero_done, zeroed)

            zero(vc[:, :, :])
            zero(dq[DH:P, :, 0, :])
            zero(dq[0:DH, :, 1, :])
            split_lo(0)
            for kind, body, at in plan:
                if kind == "unit" and not body.raw:
                    split_lo(body.split)
                if kind == "small_arrays":
                    pool_e.wait_ge(rows_done, 2)
                    pool_e.dma_start(bias_dram, bias_row[:, 0:BIASW]).then_inc(scratch_in, 16)
                if kind == "attention_1":
                    pool_e.wait_ge(lo_done, at["split"] + 1)
                    for m in (1, 3, 5, 7, 0, 2, 4, 6):
                        nc.gpsimd.tensor_scalar(alibi(m), causal_distance, 2.0 ** -(m + 1), None, ALU.mult)\
                            .then_inc(alibi_done, 1)
                    pool_e.wait_ge(alibi_done, 8)
                    for m in range(len(stack_items["nsa"])):
                        stack_lo("nsa", m)
                    scale("nsa")
                    pool_e.wait_ge(scratch_in, 16)
                    pool_e.wait_ge(attn_done, 1)
                    pool_e.dma_start(bh, bass.AP(bias_dram.tensor, 0, [[1, P], [BIASW, DSA_HEADS], [1, T]]))\
                          .then_inc(bias_in, 16)
                    zero(iq[DH:P, :, 0, :])
                    zero(iq[0:DH, :, 1, :])
                if kind == "attention_2":
                    scale("dsa")
                if kind == "ffn":
                    def ffn_lo(j, value):
                        pool_e.wait_ge(hi_done, value)
                        z, w = ffn_slots[j], ffn_ring[j]
                        nc.gpsimd.tensor_tensor(w_lo[:, w, :], raw[:, z, :], w_hi[:, w, :].bitcast(F32),
                                                ALU.subtract).then_inc(lo_done, 1)

                    with pool_e.Fori(0, FFN_STEPS) as f:
                        ffn_lo(1, f * 2 + (at["split"] + 2))
                        ffn_lo(0, f * 2 + (at["split"] + 3))

        @block.scalar
        def _(sc):
            act_fn = nc.scalar.activation
            def split_hi(s):
                if s >= len(split_units):
                    return
                u = split_units[s]
                sc.wait_ge(raw_in[u.n % 2], u.arrived)
                if s >= 2:
                    sc.wait_ge(*used(split_units[s - 2].n))
                size = u.nk * u.width
                act_fn(w_hi[:, s % 2, 0:size], raw[:, u.n % 2, 0:size], ACT.Copy).then_inc(hi_done, 1)

            def split_act_hi(u):
                if u.act0 >= 2:
                    sc.wait_ge(*used(u.n - 2))
                for o, k, nk in act_pieces(u):
                    act_fn(h_hi[:, o:o + nk, :], act[:, k:k + nk, :], ACT.Copy).then_inc(a_hi_done, 1)

            def evacuate(u):
                if u.tiles is None:
                    if not u.last:
                        return
                    kind, arg = u.evac
                    if kind == "hidden":
                        for j in range(2):
                            sc.wait_ge(hid_mm, 2 * arg + j + 1)
                            act_fn(hid[:, arg, j, :], bank[6 + j][:, 0:2 * NCMP], ACT.Silu,
                                   bias=col[:, R_B1 + 2 * arg + j:R_B1 + 2 * arg + j + 1]).then_inc(hid_done, 1)
                    for j in range(u.ntiles):
                        t = u.tile + j
                        if kind == "z":
                            sc.wait_ge(tile_done, t + 1)
                            sc.wait_ge(flat_done, 4)
                            act_fn(zd[:, j, :], bank[t % 4][:, :], ACT.Silu).then_inc(sc_evac, 1)
                        if kind == "dv":
                            sc.wait_ge(tile_done, t + 1)
                            act_fn(dv[:, j, :], bank[t % 4][:, :], ACT.Copy).then_inc(sc_evac, 1)
                    return
                x = u.aux0
                for j, (c0, m, kind, idx) in enumerate(u.tiles):
                    t = u.tile + j
                    src = bank[t % 4][0:m, :]
                    if kind.startswith("norm") or kind in ("vd", "ng", "viw"):
                        sc.wait_ge(tile_done, t + 1)
                        if x == 0:
                            sc.wait_ge(setup_done, 1)
                        if x >= 4:
                            sc.wait_ge(aux_free, x - 3)
                        fn = ACT.Square if kind.startswith("norm") else ACT.Sigmoid if kind == "ng" else ACT.Copy
                        act_fn(L[0:m, x % 4, :], src, fn).then_inc(aux_in, 1)
                        x += 1
                    if kind == "iq":
                        sc.wait_ge(tile_done, t + 1)
                        if idx == 0:
                            sc.wait_ge(zero_done, 5)
                        act_fn(iq[0:DH, idx, 0, :], src[0:DH, :], ACT.Copy)
                        act_fn(iq[DH:P, idx, 1, :], src[DH:P, :], ACT.Copy).then_inc(sc_evac, 1)
                    if kind == "nz":
                        sc.wait_ge(tile_done, t + 1)
                        act_fn(nzt[:, idx, :], src, ACT.Silu).then_inc(sc_evac, 1)
                    if kind == "q2":
                        sc.wait_ge(tile_done, t + 1)
                        act_fn(q2[:, idx, :], src, ACT.Copy, scale=-(DH ** -0.5)).then_inc(sc_evac, 1)
                    if kind in ("cb", "cc", "cx"):
                        sc.wait_ge(tile_done, t + 1)
                        dst = dict(cb=ya, cc=cc, cx=cx)[kind][:, idx, :]
                        act_fn(dst, src, ACT.Copy).then_inc(sc_evac, 1)
                    if kind == "gate":
                        sc.wait_ge(tile_done, t + 1)
                        if idx == 0:
                            sc.wait_ge(ix_acc, 3 * DSA_HEADS)
                        if idx == 8:
                            sc.wait_ge(conv_done, 4)
                        act_fn(gate(idx), src, ACT.Sigmoid, bias=col[:, R_BGATE + idx:R_BGATE + idx + 1])\
                            .then_inc(sc_evac, 1)

            def roots_of(u):
                for j, (c0, m, kind, idx) in enumerate(u.tiles or []):
                    if kind.startswith("norm"):
                        x = u.aux0 + j
                        sc.wait_ge(aux_done, x + 1)
                        act_fn(L[:, x % 4, :], bank[4 + x % 2][:, :], ACT.Sqrt, bias=eps).then_inc(aux_root, 1)

            def row_norm(nth, junk, res):
                if nth == 0:
                    sc.wait_ge(eps_done, 1)
                act_fn(st[:, ST_RS + NT:ST_RS + NT + 1], eps, ACT.Sqrt)
                for i in range(NT):
                    if nth == 0:
                        sc.wait_ge(x_in[i], 16)
                    else:
                        sc.wait_ge(res_done, res - NT + i + 1)
                    act_fn(junk[:, i, :], xres[:, i, :], ACT.Square, accum_out=st[:, ST_SS + i:ST_SS + i + 1])\
                        .then_inc(squares, 1)
                    sc.wait_ge(squares, NT * nth + i + 1)
                    act_fn(st[:, ST_RS + i:ST_RS + i + 1], st[:, ST_SS + i:ST_SS + i + 1], ACT.Sqrt, scale=1.0 / D,
                           bias=eps).then_inc(roots, 1)

            def stack_hi(which, m):
                item = stack_items[which][m]
                src, r = stack_source(which, item)
                if item[0] == "q":
                    act_fn(q_stack(item[1])[r:r + DH, :], src, ACT.Copy).then_inc(stack_hi_done, 1)
                elif which == "dsa":
                    act_fn(k_stack(item[1], item[2], 0), src, ACT.Copy).then_inc(stack_hi_done, 1)
                else:
                    act_fn(k_stack(item[1], item[2], 0)[0:DH, :], src, ACT.Copy)
                    act_fn(k_stack(item[1], item[2], 0)[DH:P, :], src, ACT.Copy).then_inc(stack_hi_done, 1)

            def attend(which, between):
                jobs, lag = attention[which], LAG[which]
                for k in range(len(jobs) + lag + 2):
                    between(k)
                    if 0 <= k - lag < len(jobs):
                        job = jobs[k - lag]
                        n, w, rows = job["n"], P * (job["i"] + 1), P if job["subs"] else NCMP
                        sc.wait_ge(tr_done, n + 1)
                        if n >= 3:
                            sc.wait_ge(pv_done, n - 2)
                        act_fn(PT[0:rows, n % 3, 0:w], t_bank(n)[0:rows, 0:w], ACT.Copy).then_inc(pt_done, 1)
                    if which == "diff" and 0 <= k - lag - 2 and jobs[k - lag - 2]["last"]:
                        job = jobs[k - lag - 2]
                        G = job["G"]
                        sc.wait_ge(pv_done, job["n"] + 1)
                        sc.wait_ge(sums_done, G + 1)
                        for i in range(NT):
                            ins = act_fn(oacc[:, i, P * G:P * G + P], bank[O_BANKS[G % 2]][:, P * i:P * i + P], ACT.Copy,
                                         scale=st[:, ST_DR + NT * G + i:ST_DR + NT * G + i + 1])
                        ins.then_inc(o_free, 1)
                    if k < len(jobs):
                        job = jobs[k]
                        for c in range(len(job["subs"])):
                            r = job["r"] + c
                            n = P * (job["i"] + 1)
                            sc.wait_ge(lg_done, r + 1)
                            act_fn(L[:, r % LRING, 0:n], L[:, r % LRING, 0:n], ACT.Exp, scale=-1.0, bias=stat(ST_MN, job, c),
                                   accum_out=sum_of(job, c)).then_inc(ex_done, 1)

            def compress_and_stack(k):
                if k == 0:
                    sc.wait_ge(kc_mm, 2)
                    act_fn(kc[:, :], bank[0][:, 0:2 * NCMP], ACT.Square).then_inc(kc_squares, 1)
                if k == 1:
                    sc.wait_ge(kc_avg, 1)
                    act_fn(kc[:, :], bank[0][:, P:P + 2 * NCMP], ACT.Sqrt, bias=eps).then_inc(kc_root, 1)
                if k == 5:
                    sc.wait_ge(kc_mm, 3)
                    act_fn(vc[0:NCMP, :, :].rearrange("p a b -> p (a b)"), bank[0][0:NCMP, 0:2 * DH], ACT.Copy)\
                        .then_inc(kc_squares, 1)
                if 4 <= k < 4 + len(stack_items["nsa"]):
                    stack_hi("nsa", k - 4)
                if k in (11, 16):
                    b = (11, 16).index(k)
                    sc.wait_ge(cmp_lg_done, b + 1)
                    lc = pc[:, b, :].rearrange("p (j c) -> p j c", c=32)[:, :, 0:NCMP]
                    act_fn(lc, lc, ACT.Exp, scale=-1.0).then_inc(cmp_ex_done, 1)

            def diff_norm(k):
                if k == 18:
                    sc.wait_ge(diff_sums, NT)
                    act_fn(st[:, ST_DSS + 16:ST_DSS + 32], st[:, ST_DSS:ST_DSS + 16], ACT.Sqrt, scale=1.0 / P,
                           bias=eps).then_inc(diff_root, 1)

            def dsa_stacks(k):
                m = 3 + k // 4
                if k % 4 == 0 and m < len(stack_items["dsa"]):
                    stack_hi("dsa", m)
                m = k // 4 - 2
                if k % 4 == 0 and 0 <= m < early_splits["branches"]:
                    sc.wait_ge(s_done, attention["dsa"][NT * m + NT - 1]["r"] + 1)
                    split_source_hi("branches", m)

            def split_source_hi(what, m):
                src, k = split_sources[what][m]
                if what == "merged":
                    sc.wait_ge(branch_done, ND + m + 1)
                act_fn(h_hi[:, k, :], src, ACT.Copy).then_inc(h_hi_done, 1)

            nth_norm = 0
            pending = None
            for at_step, (kind, body, at) in enumerate(plan):
                if kind == "unit":
                    if not body.raw:
                        split_hi(body.split)
                    if body.act and body.act0 + 1 < len(down_units):
                        split_act_hi(down_units[body.act0 + 1])
                    if pending is not None:
                        roots_of(pending)
                    evacuate(body)
                    if body is last_branch_unit:
                        sc.wait_ge(tile_done, branch_a_end)
                        for m in range(early_splits["merged"]):
                            split_source_hi("merged", m)
                    pending = body
                    continue
                if pending is not None:
                    roots_of(pending)
                    pending = None
                if kind == "transpose":
                    if body["norm"]:
                        row_norm(nth_norm, zs, at["res"])
                        nth_norm += 1
                    if at["unit"] == 0:
                        split_hi(0)
                        sc.wait_ge(col_done, 1)
                    for k in range(body["n"]):
                        t = at["tile"] + k
                        sc.wait_ge(tile_done, t + 1)
                        if body["gain"] is None:
                            ins = act_fn(h_hi[:, k, :], bank[t % 4][:, :], ACT.Copy)
                        else:
                            ins = act_fn(h_hi[:, k, :], bank[t % 4][:, :], ACT.Copy,
                                         scale=col[:, body["gain"] + k:body["gain"] + k + 1])
                        ins.then_inc(h_hi_done, 1)
                if kind == "split":
                    if body == "merged":
                        sc.wait_ge(tile_done, at["tile"])
                    for m in range(early_splits[body], len(split_sources[body])):
                        split_source_hi(body, m)
                if kind == "attention_1":
                    sc.wait_ge(tile_done, at["tile"])
                    attend("diff", compress_and_stack)
                    attend("nsa", diff_norm)
                    sc.wait_ge(attn_done, 1)
                if kind == "attention_2":
                    sc.wait_ge(tile_done, at["tile"])
                    for m in range(3):
                        stack_hi("dsa", m)
                    attend("dsa", dsa_stacks)
                    sc.wait_ge(attn_done, 2)
                if kind == "small_arrays":
                    for j in range(2):
                        t = at["tile"] + j
                        w = T if j == 0 else BIASW - T
                        sc.wait_ge(tile_done, t + 1)
                        act_fn(bias_row[:, T * j:T * j + w], bank[t % 4][0:DSA_HEADS, 0:w], ACT.Copy, scale=-1.0)\
                            .then_inc(rows_done, 1)
                    sc.wait_ge(col_done, 4)
                    sc.wait_ge(lam_dot, 2)
                    act_fn(st[:, ST_LAM + 2:ST_LAM + 4], st[:, ST_LAM:ST_LAM + 2], ACT.Exp).then_inc(lam_exp, 1)
                if kind == "index":
                    r = 0
                    for i in range(1, NT):
                        for h in range(DSA_HEADS):
                            w = P * (i + 1)
                            sc.wait_ge(ix_s, r + 1)
                            if r >= 4:
                                sc.wait_ge(ix_acc, r - 3)
                            act_fn(L[:, r % 4, 0:w], bank[4 + r % 3][:, 0:w], ACT.Relu).then_inc(ix_relu, 1)
                            r += 1
                if kind == "ffn":
                    n0, t0 = at["unit"], at["tile"]
                    (z0, z1), (g0, g1) = ffn_slots, ffn_ring

                    def ffn_step(f, first=False):
                        sc.wait_ge(raw_in[z1], f * 16 + units[n0 + 1].arrived)
                        sc.wait_ge(tile_done, f * 4 + t0)
                        act_fn(w_hi[:, g1, :], raw[:, z1, :], ACT.Copy).then_inc(hi_done, 1)
                        for j in range(2):
                            sc.wait_ge(tile_done, f * 4 + (t0 + j + 1))
                            if not first:
                                sc.wait_ge(act_done, f * 2)
                            act_fn(L[:, j, :], bank[(t0 + j) % 4][:, :], ACT.Silu).then_inc(gsilu, 1)
                        sc.wait_ge(raw_in[z0], f * 16 + (units[n0].arrived + 16))
                        sc.wait_ge(tile_done, f * 4 + (t0 + 2))
                        act_fn(w_hi[:, g0, :], raw[:, z0, :], ACT.Copy).then_inc(hi_done, 1)

                    ffn_step(0, first=True)
                    with sc.Fori(1, FFN_STEPS) as f:
                        ffn_step(f)
                    sc.wait_ge(act_done, NFF)
                    sc.wait_ge(tile_done, t0 + 4 * FFN_STEPS)
                    split_act_hi(down_units[0])
                if kind == "final":
                    row_norm(nth_norm, zs, at["res"])

        @block.vector
        def _(ve):
            v = nc.vector
            count = [0]

            def chain(ins):
                ins.then_inc(dve_step, 1)
                count[0] += 1
                ve.wait_ge(dve_step, count[0])

            def spread(x, *dims):
                return bass.AP(x.tensor, x.offset, [list(x.ap[0])] + [list(d) for d in dims])

            v.memset(eps, EPS).then_inc(eps_done, 1)
            ve.wait_ge(col_tr, 1)
            v.tensor_copy(col[:, 0:ND], bank[4][:, 0:ND]).then_inc(col_done, 1)

            def small_arrays():
                ve.wait_ge(small_in, 16 * N_SMALL)
                ve.wait_ge(col_tr, 2)
                v.tensor_copy(col[:, ND:NROWS], bank[4][:, ND:NROWS]).then_inc(col_done, 1)
                ve.wait_ge(col_done, 2)
                for r in (R_GDQ, R_GNQ):
                    v.tensor_scalar(col[:, r:r + 1], col[:, r:r + 1], -(DH ** -0.5), None, ALU.mult).then_inc(col_done, 1)
                for j in range(2):
                    v.tensor_tensor_reduce(out=lam_in[:, 2 * j, :], in0=lam_in[:, 2 * j, :], in1=lam_in[:, 2 * j + 1, :],
                                           scale=1.0, scalar=0.0, op0=ALU.mult, op1=ALU.add,
                                           accum_out=st[:, ST_LAM + j:ST_LAM + j + 1]).then_inc(lam_dot, 1)
                chain(v.tensor_scalar(gsub[:, :], gsub[:, :], 1.0 - LAM_INIT, None, ALU.mult))
                v.tensor_tensor(causal_distance, L[:, 0, :], mask, ALU.add).then_inc(setup_done, 1)
                ve.wait_ge(lam_exp, 1)
                chain(v.tensor_tensor(st[:, ST_LAM:ST_LAM + 1], st[:, ST_LAM + 3:ST_LAM + 4],
                                      st[:, ST_LAM + 2:ST_LAM + 3], ALU.subtract))
                v.tensor_scalar(neglam, st[:, ST_LAM:ST_LAM + 1], -LAM_INIT, None, ALU.add).then_inc(lam_done, 1)

            def evacuate(u):
                if u.tiles is None:
                    if not u.last:
                        return
                    kind, half = u.evac
                    if kind == "residual":
                        for i in range(NT):
                            t = u.tile + i
                            x = xres[:, i, 512 * half:512 * half + 512]
                            ve.wait_ge(tile_done, t + 1)
                            v.tensor_tensor(x, bank[t % 4][:, :], x, ALU.add).then_inc(res_done, 1)
                    return
                for j, (c0, m, kind, idx) in enumerate(u.tiles):
                    t = u.tile + j
                    src = bank[t % 4]
                    if kind == "cmp":
                        ve.wait_ge(tile_done, t + 1)
                        for kv in range(KVH):
                            half = slice(DH * kv, DH * kv + DH)
                            v.tensor_copy(shifted[0:DH, idx, kv, :], src[half, :])
                            ins = v.tensor_copy(shifted[DH:P, idx, kv, 0:T - 1], src[half, 1:T])
                        ins.then_inc(ve_evac, 1)
                        ve.wait_ge(ve_evac, u.ve0 + j + 1)
                        for s in range(2):
                            first = shifted[:, idx, 0, CMP_STRIDE * s:CMP_STRIDE * s + 1]
                            g = col[:, R_POS + NPAIR * idx + 8 * s:R_POS + NPAIR * idx + 8 * s + 1]
                            o = flat[:, idx, 8 * s, 0:1]
                            v.tensor_tensor(spread(o, [2 * NCMP, 8], [NCMP, KVH], [1, NCMP]),
                                            spread(first, [2, 8], [T, KVH], [CMP_STRIDE, NCMP]),
                                            spread(g, [1, 8], [0, KVH], [0, NCMP]), ALU.add).then_inc(flat_done, 1)
                    if kind == "kik":
                        ve.wait_ge(tile_done, t + 1)
                        for r in range(2):
                            v.tensor_copy(k2[DH * r:DH * r + DH, :], src[0:DH, :])
                            ins = v.tensor_copy(ik2[DH * r:DH * r + DH, :], src[DH:P, :])
                        ins.then_inc(ve_evac, 1)
                    if kind == "branch_a":
                        ve.wait_ge(tile_done, t + 1)
                        ve.wait_ge(sc_evac, u.sc0)
                        v.tensor_tensor(gate(idx), src[:, :], gate(idx), ALU.mult).then_inc(branch_done, 1)
                    if kind == "branch_b":
                        ve.wait_ge(tile_done, t + 1)
                        chain(v.tensor_tensor(gate(8 + idx), src[:, :], gate(8 + idx), ALU.mult))
                        v.tensor_tensor(gate(idx), gate(idx), gate(8 + idx), ALU.add).then_inc(branch_done, 1)

            def finish(u):
                x = u.aux0
                for j, (c0, m, kind, idx) in enumerate(u.tiles or []):
                    t = u.tile + j
                    aux = bank[4 + x % 2]
                    blocks = aux[:, :].rearrange("p (i c) -> p i c", c=P)
                    if kind.startswith("norm"):
                        ve.wait_ge(aux_root, x + 1)
                        chain(v.reciprocal(L[:, x % 4, :], L[:, x % 4, :]))
                        if kind != "norm_dq":
                            dst, g = {"norm_dk": (dk, R_GDK), "norm_nq": (nq, R_GNQ), "norm_kd": (kd, R_GKS + idx)}[kind]
                            v.scalar_tensor_tensor(dst[:, idx, :], bank[t % 4][:, :], col[:, g:g + 1], L[:, x % 4, :],
                                                   ALU.mult, ALU.mult).then_inc(aux_free, 1)
                        else:
                            if idx == 0:
                                ve.wait_ge(zero_done, 3)
                            for r in range(2):
                                rows = slice(DH * r, DH * r + DH)
                                ins = v.scalar_tensor_tensor(dq[rows, idx, r, :], bank[t % 4][rows, :],
                                                             col[rows, R_GDQ:R_GDQ + 1], L[rows, x % 4, :],
                                                             ALU.mult, ALU.mult)
                            ins.then_inc(aux_free, 1)
                    elif kind == "vd":
                        ve.wait_ge(aux_done, x + 1)
                        v.tensor_copy(vd[:, idx, :, :], blocks).then_inc(aux_free, 1)
                    elif kind == "ng":
                        ve.wait_ge(aux_done, x + 1)
                        v.tensor_copy(ngt[:, :, :], blocks[:, :, 96:120]).then_inc(aux_free, 1)
                    elif kind == "viw":
                        ve.wait_ge(aux_done, x + 1)
                        v.tensor_copy(v2, blocks[:, :, 0:DH])
                        v.tensor_scalar(iw, blocks[:, :, DH:DH + 8], 8 ** -0.5 * DH ** -0.5, None, ALU.mult)\
                            .then_inc(aux_free, 1)
                    else:
                        continue
                    x += 1

            def convolve():
                for m in range(4):
                    w = [col[:, R_CONV + 4 * k + m:R_CONV + 4 * k + m + 1] for k in range(3)]
                    u_, y_ = cc[:, m, :], cx[:, m, :]
                    chain(v.tensor_tensor(u_, u_, y_, ALU.mult))
                    chain(v.tensor_scalar(y_, u_, w[2], None, ALU.mult))
                    chain(v.scalar_tensor_tensor(y_[:, 1:T], u_[:, 0:T - 1], w[1], y_[:, 1:T], ALU.mult, ALU.add))
                    chain(v.scalar_tensor_tensor(y_[:, 2:T], u_[:, 0:T - 2], w[0], y_[:, 2:T], ALU.mult, ALU.add))
                    v.tensor_tensor(ya[:, m, :], ya[:, m, :], y_, ALU.mult).then_inc(conv_done, 1)

            def logits(job):
                n, i = P * (job["i"] + 1), job["i"]
                for c, s in enumerate(job["subs"]):
                    r = job["r"] + c
                    ve.wait_ge(s_done, r + 1)
                    if r >= LRING:
                        ve.wait_ge(tr_done, job_of_sub[r - LRING]["n"] + 1)
                    src, bias = bank[S_BANKS[r % 3]][:, 0:n], s["bias"][:, causal_window(i)]
                    if "select" in s:
                        bias = spread(s["bias"][:, n - 1:n], [-1, n])
                        chain(v.tensor_tensor(L[:, r % LRING, 0:n], src, bias, ALU.add))
                        src, bias = L[:, r % LRING, 0:n], s["select"]
                    v.tensor_tensor_reduce(out=L[:, r % LRING, 0:n], in0=src, in1=bias, scale=1.0, scalar=3e38,
                                           op0=ALU.add, op1=ALU.min, accum_out=stat(ST_MN, job, c))\
                        .then_inc(lg_done, 1)

            def combine(job):
                r, n = job["r"], P * (job["i"] + 1)
                ve.wait_ge(ex_done, r + 2)
                c = stat(ST_C2, job, 0)
                chain(v.reciprocal(c, sum_of(job, 1)))
                chain(v.tensor_scalar(c, c, sum_of(job, 0), neglam, ALU.mult, ALU.mult))
                v.scalar_tensor_tensor(L[:, r % LRING, 0:n], L[:, (r + 1) % LRING, 0:n], c, L[:, r % LRING, 0:n],
                                       ALU.mult, ALU.add).then_inc(p_done, 1)
                if job["last"]:
                    sums = st[:, ST_DR + NT * job["G"]:ST_DR + NT * job["G"] + NT]
                    v.reciprocal(sums, sums).then_inc(sums_done, 1)

            def coefficient(job):
                c = stat(ST_C2, job, 0)
                ve.wait_ge(ex_done, job["r"] + 1)
                if job["G"] < GROUPS["diff"] + GROUPS["nsa"]:
                    g = 8 * (1 + job["br"]) + job["h"]
                    chain(v.reciprocal(c, sum_of(job, 0)))
                    v.tensor_tensor(c, c, ngt[:, job["i"], g:g + 1], ALU.mult).then_inc(coef_done, 1)
                else:
                    v.reciprocal(c, sum_of(job, 0)).then_inc(coef_done, 1)

            def group_out(which, job):
                G = job["G"]
                O = bank[O_BANKS[G % 2]]
                ve.wait_ge(pv_done, job["n"] + 1)
                if which == "nsa":
                    z = nzt[:, job["g"], :]
                    v.tensor_tensor(z, O[:, :], z, ALU.mult).then_inc(o_free, 1)
                else:
                    v.tensor_copy(ot2[:, job["g"], :], O[:, :]).then_inc(o_free, 1)

            def attend(which, between):
                jobs, lag = attention[which], LAG[which]
                for k in range(len(jobs) + lag + 2):
                    between(k)
                    if k < len(jobs):
                        logits(jobs[k])
                    if 1 <= k <= len(jobs) and jobs[k - 1]["subs"]:
                        (combine if which == "diff" else coefficient)(jobs[k - 1])
                    if which != "diff" and 0 <= k - lag - 2 and jobs[k - lag - 2]["last"]:
                        group_out(which, jobs[k - lag - 2])

            def grid(x):
                return spread(x, [P, GROUP], [32, NT], [1, NCMP])

            def compress_and_stack(k):
                cmn, csm = st[:, ST_CMN:ST_CMN + 16], st[:, ST_CSM:ST_CSM + 16]
                if k % NT == 0:
                    ve.wait_ge(alibi_done, min(k // NT + 1, 8))
                if k == 2:
                    ve.wait_ge(kc_root, 1)
                    chain(v.reciprocal(kc[:, :], kc[:, :]))
                    v.scalar_tensor_tensor(kc_t[:, :], bank[0][:, 0:2 * NCMP], col[:, R_GKC:R_GKC + 1], kc[:, :],
                                           ALU.mult, ALU.mult).then_inc(kc_done, 1)
                if k in (9, 14):
                    b = (9, 14).index(k)
                    lc = grid(pc[:, b, 0:1])
                    l3 = pc[:, b, :].rearrange("p (j c) -> p j c", c=32)[:, :, 0:NCMP]
                    ve.wait_ge(cmp_s_done, b + 1)
                    chain(v.tensor_tensor(lc, grid(bank[0][:, 0:1]),
                                          spread(cmask[:, 0, 0:1], [0, GROUP], [32, NT], [1, NCMP]), ALU.add))
                    chain(v.tensor_reduce(out=cmn, in_=l3, axis=AX.X, op=ALU.min))
                    v.tensor_tensor(l3, l3, spread(cmn[:, 0:1], [1, 16], [0, NCMP]), ALU.subtract).then_inc(cmp_lg_done, 1)
                if k in (12, 17):
                    b = (12, 17).index(k)
                    lc = grid(pc[:, b, 0:1])
                    l3 = pc[:, b, :].rearrange("p (j c) -> p j c", c=32)[:, :, 0:NCMP]
                    ve.wait_ge(cmp_ex_done, b + 1)
                    chain(v.tensor_reduce(out=csm, in_=l3, axis=AX.X, op=ALU.add))
                    chain(v.reciprocal(csm, csm))
                    chain(v.tensor_tensor(spread(csm[:, 0:1], [NT, GROUP], [1, NT]), spread(csm[:, 0:1], [NT, GROUP], [1, NT]),
                                          spread(ngt[:, 0, b:b + 1], [2, GROUP], [24, NT]), ALU.mult))
                    chain(v.tensor_tensor(lc, lc, spread(cvalid[:, 0, 0:1], [0, GROUP], [32, NT], [1, NCMP]), ALU.mult))
                    v.tensor_tensor(l3, l3, spread(csm[:, 0:1], [1, 16], [0, NCMP]), ALU.mult).then_inc(cmp_p_done, 1)

            def diff_norm(k):
                rr = st[:, ST_DSS + 16:ST_DSS + 32]
                i, part = divmod(k - 2, 4)
                if 0 <= i < NT and part == 0:
                    ve.wait_ge(o_free, DIFF_HEADS)
                    v.tensor_tensor(dk[:, i, :], oacc[:, i, :], oacc[:, i, :], ALU.mult).then_inc(diff_squares, 1)
                if 0 <= i < NT and part == 2:
                    ve.wait_ge(diff_squares, i + 1)
                    v.tensor_reduce(out=st[:, ST_DSS + 4 * i:ST_DSS + 4 * i + 4],
                                    in_=dk[:, i, :].rearrange("p (h d) -> p h d", d=P), axis=AX.X, op=ALU.add)\
                        .then_inc(diff_sums, 1)
                if k == 22:
                    ve.wait_ge(diff_root, 1)
                    v.reciprocal(rr, rr).then_inc(diff_recip, 1)
                i, part = divmod(k - 24, 4)
                if 0 <= i < NT:
                    heads = lambda x: x[:, i, :].rearrange("p (h d) -> p h d", d=P)
                    if part == 0:
                        ve.wait_ge(diff_recip, 1)
                        v.tensor_tensor(heads(oacc), heads(oacc), spread(rr[:, 4 * i:4 * i + 1], [1, 4], [0, P]), ALU.mult)\
                            .then_inc(diff_out, 1)
                    if part == 1:
                        v.tensor_tensor(heads(zd), heads(zd), spread(gsub[:, 0:1], [0, 4], [1, P]), ALU.mult)\
                            .then_inc(diff_out, 1)
                    if part == 2:
                        ve.wait_ge(diff_out, 3 * i + 2)
                        v.tensor_tensor(zd[:, i, :], zd[:, i, :], oacc[:, i, :], ALU.mult).then_inc(diff_out, 1)

            def split_act_lo(u):
                for j, (o, k, nk) in enumerate(act_pieces(u)):
                    ve.wait_ge(a_hi_done, act_done_at(u, j))
                    v.tensor_tensor(h_lo[:, o:o + nk, :], act[:, k:k + nk, :], h_hi[:, o:o + nk, :].bitcast(F32),
                                    ALU.subtract).then_inc(a_lo_done, 1)

            def split_source_lo(what, m):
                src, k = split_sources[what][m]
                ve.wait_ge(h_hi_done, at_split[what]["h"] + m + 1)
                v.tensor_tensor(h_lo[:, k, :], src, h_hi[:, k, :].bitcast(F32), ALU.subtract).then_inc(h_lo_done, 1)

            nth_norm, pending = 0, None
            for kind, body, at in plan:
                if kind == "unit":
                    if body.act and body.act0 + 1 < len(down_units):
                        split_act_lo(down_units[body.act0 + 1])
                    if pending is not None:
                        finish(pending)
                    if body is last_branch_unit:
                        for m in range(early_splits["merged"]):
                            split_source_lo("merged", m)
                    evacuate(body)
                    pending = body
                    if body.name == "conv_x" and body.tiles[1][3] == 3:
                        ve.wait_ge(sc_evac, body.sc0 + 2)
                        convolve()
                    continue
                if pending is not None:
                    finish(pending)
                    pending = None
                if kind in ("transpose", "final") and (kind == "final" or body["norm"]):
                    nth_norm += 1
                    for i in range(NT):
                        r = st[:, ST_RR + i:ST_RR + i + 1]
                        ve.wait_ge(roots, NT * (nth_norm - 1) + i + 1)
                        chain(v.reciprocal(r, st[:, ST_RS + i:ST_RS + i + 1]))
                        if kind == "transpose":
                            v.tensor_scalar(zs[:, i, :], xres[:, i, :], r, None, ALU.mult).then_inc(xn_done, 1)
                        else:
                            ve.wait_ge(gfin_in, 16)
                            v.scalar_tensor_tensor(zs[:, i, :], xres[:, i, :], r, gfin, ALU.mult, ALU.mult)\
                                .then_inc(y_done, 1)
                if kind == "transpose":
                    h0 = at["h"]
                    for k in range(body["n"]):
                        g = 1.0 if body["gain"] is None else col[:, body["gain"] + k:body["gain"] + k + 1]
                        ve.wait_ge(h_hi_done, h0 + k + 1)
                        v.scalar_tensor_tensor(h_lo[:, k, :], bank[(at["tile"] + k) % 4][:, :], g,
                                               h_hi[:, k, :].bitcast(F32), ALU.mult, ALU.subtract)\
                            .then_inc(h_lo_done, 1)
                if kind == "small_arrays":
                    small_arrays()
                if kind == "attention_1":
                    ve.wait_ge(sc_evac, at["sc"])
                    ve.wait_ge(scratch_in, 16)
                    attend("diff", compress_and_stack)
                    ve.wait_ge(alibi_done, 8)
                    attend("nsa", diff_norm)
                    ve.wait_ge(o_free, GROUPS["diff"] + GROUPS["nsa"])
                    ve.wait_ge(diff_out, 3 * NT)
                    v.tensor_copy(st[:, ST_C:ST_C + 1], eps).then_inc(attn_done, 1)
                if kind == "index":
                    ve.wait_ge(aux_free, at["aux"])
                    r = 0
                    for i in range(1, NT):
                        for h in range(DSA_HEADS):
                            w = P * (i + 1)
                            ve.wait_ge(ix_relu, r + 1)
                            src = L[:, r % 4, 0:w]
                            if h == 0:
                                v.scalar_tensor_tensor(work_of(i), src, iw[:, i, h:h + 1], mask[:, causal_window(i)],
                                                       ALU.mult, ALU.subtract).then_inc(ix_acc, 1)
                            else:
                                ve.wait_ge(ix_acc, r)
                                v.scalar_tensor_tensor(work_of(i), src, iw[:, i, h:h + 1], work_of(i),
                                                       ALU.mult, ALU.add).then_inc(ix_acc, 1)
                            r += 1
                    ve.wait_ge(ix_acc, r)
                    v.tensor_copy(pm_of(0), mask[:, causal_window(0)])
                    for _ in range(TOPK // 8):
                        for i in range(1, NT):
                            ins = v.max(st[:, ST_TOP + 8 * (i - 1):ST_TOP + 8 * i], work_of(i))
                        chain(ins)
                        for i in range(1, NT):
                            ins = v.match_replace(work_of(i), st[:, ST_TOP + 8 * (i - 1):ST_TOP + 8 * i], work_of(i), TAKEN)
                        chain(ins)
                    for i in range(1, NT):
                        ins = v.tensor_scalar(pm_of(i), work_of(i), TAKEN / 2, BIG, ALU.is_gt, ALU.mult)
                    ins.then_inc(topk_done, 1)
                if kind == "attention_2":
                    for m in range(3):
                        ve.wait_ge(stack_hi_done, len(stack_items["nsa"]) + m + 1)
                        for lo, src, hi in lower_pieces("dsa", m):
                            v.tensor_tensor(lo, src, hi, ALU.subtract).then_inc(first_stacks_done, 1)
                    ve.wait_ge(topk_done, 1)
                    ve.wait_ge(bias_in, 16)
                    attend("dsa", lambda k: None)
                    ve.wait_ge(o_free, sum(GROUPS.values()))
                    v.tensor_copy(st[:, ST_C:ST_C + 1], eps).then_inc(attn_done, 1)
                if kind == "split":
                    ve.wait_ge(h_lo_done, at["h"] + early_splits[body])
                    for m in range(early_splits[body], len(split_sources[body])):
                        split_source_lo(body, m)
                if kind == "ffn":
                    t0 = at["tile"]

                    def ffn_step(f, tile):
                        for j in range(2):
                            ve.wait_ge(tile_done, f * 4 + (t0 + j + 3))
                            ve.wait_ge(gsilu, f * 2 + (j + 1))
                            v.tensor_tensor(tile(j), bank[(t0 + 2 + j) % 4][:, :], L[:, j, :], ALU.mult).then_inc(act_done, 1)

                    with ve.Fori(0, FFN_STEPS) as f:
                        ffn_step(f, lambda j: pool[:, bass.ds(f * (2 * T) + T * j, T)])
                    split_act_lo(down_units[0])

        @block.tensor
        def _(pe):
            mm = nc.tensor.matmul

            def free_bank(t):
                if t >= 4:
                    name, value = released[t - 4]
                    pe.wait_ge(frees[name], value)

            def three(dst, w_pair, h_pair, start, stop):
                for p, (w, h) in enumerate(((0, 0), (0, 1), (1, 0))):
                    ins = mm(dst, w_pair[w], h_pair[h], start=start and p == 0, stop=stop and p == 2)
                return ins

            fresh = [None]

            def main(u, between):
                n = u.n
                if u.raw:
                    between()
                    pe.wait_ge(raw_in[n % 2], u.arrived)
                    w, kv = slot(raw, n, u), u.evac[1]
                    pe.wait_ge(flat_done, 2 * kv + 2)
                    if u.first and kv == 1:
                        pe.wait_ge(hid_done, 2)
                    for j in range(2):
                        for q in range(u.nk):
                            ins = mm(bank[6 + j][:, 0:2 * NCMP], w[:, q, P * j:P * j + P],
                                     flat[:, kv, u.k0 + q, :], start=u.first and q == 0, stop=u.last and q == u.nk - 1,
                                     skip_group_check=True)
                        if u.last:
                            ins.then_inc(hid_mm, 1)
                    if not u.last:
                        ins.then_inc(part_done, 1)
                    return
                pe.wait_ge(lo_done, u.split)
                hi, lo = slot(w_hi, u.split - 1, u), slot(w_lo, u.split - 1, u)
                if u.tiles:
                    for j, (c0, m, kind, idx) in enumerate(u.tiles):
                        t = u.tile + j
                        free_bank(t)
                        for k in range(u.nk):
                            if j == 0 and fresh[0] is not None:
                                pe.wait_ge(h_lo_done, fresh[0] + u.k0 + k + 1)
                            h = u.k0 + k
                            ins = three(bank[t % 4][0:m, :], (hi[:, k, c0:c0 + m], lo[:, k, c0:c0 + m]),
                                        (h_hi[:, h, :], h_lo[:, h, :]), k == 0, k == u.nk - 1)
                        ins.then_inc(tile_done, 1)
                        if j == 0:
                            between()
                    fresh[0] = None
                    return
                tile = u.tile
                if u.act and u.act0 > 0:
                    pe.wait_ge(a_lo_done, act_done_at(u, 0))
                for i in range(NT):
                    if u.first:
                        free_bank(tile + i)
                    for k in range(u.nk):
                        h = 4 * (u.act0 % 2) + k if u.act else u.k0 + k
                        if i == 0 and u.act and u.act0 == 0:
                            pe.wait_ge(a_lo_done, act_done_at(u, k))
                        if i == 0 and fresh[0] is not None:
                            pe.wait_ge(h_lo_done, fresh[0] + u.k0 + k + 1)
                        cols = slice(P * i, P * i + P)
                        s, e = u.first and k == 0, u.last and k == u.nk - 1
                        for p, (x, w) in enumerate(((h_hi, hi), (h_lo, hi), (h_hi, lo))):
                            ins = mm(bank[(tile + i) % 4][:, :], x[:, h, cols], w[:, k, :],
                                     start=s and p == 0, stop=e and p == 2, skip_group_check=True)
                    if u.last:
                        ins.then_inc(tile_done, 1)
                    if i == 0:
                        between()
                if not u.last:
                    ins.then_inc(part_done, 1)
                if u.last:
                    fresh[0] = None

            def second(u):
                x = u.aux0
                for j, (c0, m, kind, idx) in enumerate(u.tiles or []):
                    if not (kind.startswith("norm") or kind in ("vd", "ng", "viw")):
                        continue
                    pe.wait_ge(aux_in, x + 1)
                    if x >= 2:
                        pe.wait_ge(aux_free, x - 1)
                    else:
                        pe.wait_ge(col_done, 2)
                    dst = bank[4 + x % 2]
                    if kind.startswith("norm"):
                        mm(dst[:, :], ones, L[:, x % 4, :], start=True, stop=True).then_inc(aux_done, 1)
                    else:
                        for i in range(NT):
                            ins = nc.tensor.transpose(dst[:, P * i:P * i + m], L[0:m, x % 4, P * i:P * i + P],
                                                      ident[0:m, 0:m])
                        ins.then_inc(aux_done, 1)
                    x += 1

            def attend(which, between):
                jobs, lag = attention[which], LAG[which]
                for k in range(len(jobs) + lag + 2):
                    between(k)
                    if k < len(jobs):
                        job = jobs[k]
                        n = P * (job["i"] + 1)
                        for c, s in enumerate(job["subs"]):
                            r = job["r"] + c
                            if r >= 3:
                                pe.wait_ge(lg_done, r - 2)
                            wide = n if len(s["q"]) == 1 else max(n, 256)
                            for p, (q, kk) in enumerate(zip(s["q"], s["k"])):
                                ins = mm(bank[S_BANKS[r % 3]][:, 0:wide], q, kk[:, 0:wide], start=p == 0,
                                         stop=p == len(s["q"]) - 1)
                            ins.then_inc(s_done, 1)
                    if 0 <= k - lag < len(jobs):
                        job = jobs[k - lag]
                        dst = t_bank(job["n"])
                        n = job["n"]
                        back = 2 if which == "diff" else 3
                        if n >= back:
                            pe.wait_ge(pt_done, n - back + 1)
                        if not job["subs"]:
                            o = P * (job["h"] // 2)
                            for j in range(NT):
                                ins = nc.tensor.transpose(dst[0:NCMP, P * j:P * j + P],
                                                          pc[:, job["h"] % 2, o + 32 * j:o + 32 * j + NCMP], ident)
                        else:
                            if which == "diff":
                                pe.wait_ge(p_done, job["n"] + 1)
                            else:
                                pe.wait_ge(scale_done, job["scaled"])
                            for j in range(job["i"] + 1):
                                ins = nc.tensor.transpose(dst[:, P * j:P * j + P], L[:, job["r"] % LRING, P * j:P * j + P],
                                                          ident)
                        ins.then_inc(tr_done, 1)
                    if 0 <= k - lag - 2:
                        job = jobs[k - lag - 2]
                        i, G, pt = job["i"], job["G"], PT[:, job["n"] % 3, :]
                        O = bank[O_BANKS[G % 2]]
                        pe.wait_ge(pt_done, job["n"] + 1)
                        if G >= 2 and (k - lag - 2 == 0 or jobs[k - lag - 3]["last"]):
                            pe.wait_ge(o_free, G - 1)
                        if which == "diff":
                            for j in range(i + 1):
                                ins = mm(O[:, P * i:P * i + P], pt[:, P * j:P * j + P], job["v"][j], start=j == 0,
                                         stop=j == i)
                        else:
                            rows = slice(DH * (job["h"] % 2), DH * (job["h"] % 2) + DH)
                            if not job["subs"]:
                                ins = mm(O[rows, :], job["v"][0], pt, start=True, stop=False, skip_group_check=True)
                            for j in range(i + 1 if job["subs"] else 0):
                                ins = mm(O[rows, P * i:P * i + P], job["v"][j], pt[:, P * j:P * j + P],
                                         start=which == "dsa" and j == 0, stop=j == i and (which == "dsa" or job["br"] == 1),
                                         skip_group_check=True)
                        ins.then_inc(pv_done, 1)

            def compress(k):
                if k == 0:
                    for r in range(2):
                        for hh in range(2):
                            ins = mm(bank[0][DH * r:DH * r + DH, 0:2 * NCMP], cmp_w2[:, 0, hh, :], hid[:, 0, hh, :],
                                     start=hh == 0, stop=hh == 1)
                        ins.then_inc(kc_mm, 1)
                if k == 1:
                    pe.wait_ge(kc_squares, 1)
                    mm(bank[0][:, P:P + 2 * NCMP], ones, kc[:, :], start=True, stop=True).then_inc(kc_avg, 1)
                if k == 5:
                    pe.wait_ge(kc_done, 1)
                    for kv in range(KVH):
                        for hh in range(2):
                            ins = mm(bank[0][0:NCMP, DH * kv:DH * kv + DH],
                                     hid[:, 1, hh, NCMP * kv:NCMP * kv + NCMP], cmp_w2[:, 1, hh, :],
                                     start=hh == 0, stop=hh == 1)
                    ins.then_inc(kc_mm, 1)
                if k in (8, 13):
                    b = (8, 13).index(k)
                    if b == 0:
                        pe.wait_ge(kc_squares, 2)
                    else:
                        pe.wait_ge(cmp_lg_done, 1)
                    for g in range(GROUP):
                        h, r = 2 * g + b, DH * b
                        kv = h // GROUP
                        for i in range(NT):
                            o = P * g + 32 * i
                            ins = mm(bank[0][:, o:o + NCMP], nq[r:r + DH, h // 2, P * i:P * i + P],
                                     kc_t[r:r + DH, NCMP * kv:NCMP * kv + NCMP], start=True, stop=True)
                    ins.then_inc(cmp_s_done, 1)

            def compressed_ready(k):
                if k == LAG["nsa"]:
                    pe.wait_ge(cmp_p_done, 2)

            def dsa_stacks(k):
                if k in (0, 4):
                    pe.wait_ge(first_stacks_done, 2 + k // 4)
                elif k % 4 == 0 and k < len(attention["dsa"]):
                    pe.wait_ge(stack_lo_done, stacked("dsa", 2 + k // 4))

            pe.wait_ge(first_in, 32)
            nc.tensor.transpose(bank[4][:, 0:ND], vec_rows[0:ND, :], ident[0:ND, 0:ND]).then_inc(col_tr, 1)
            nth_norm = n_attn = 0
            pending = None
            for kind, body, at in plan:
                if kind == "unit":
                    before = pending
                    main(body, lambda: before is not None and second(before))
                    pending = body
                    continue
                if pending is not None:
                    second(pending)
                    pending = None
                if kind == "transpose":
                    src = zs if body["norm"] else zd
                    if not body["norm"]:
                        pe.wait_ge(attn_done, n_attn)
                    for k in range(body["n"]):
                        t = at["tile"] + k
                        free_bank(t)
                        for i in range(NT):
                            if body["norm"] and k == 0:
                                pe.wait_ge(xn_done, NT * nth_norm + i + 1)
                            ins = nc.tensor.transpose(bank[t % 4][:, P * i:P * i + P], src[:, i, P * k:P * k + P], ident)
                        ins.then_inc(tile_done, 1)
                    nth_norm += body["norm"]
                    fresh[0] = at["h"]
                if kind == "split" and body == "branches":
                    pe.wait_ge(o_free, sum(GROUPS.values()) - 1)
                if kind == "split" and body != "nsa":
                    fresh[0] = at["h"]
                if kind == "small_arrays":
                    pe.wait_ge(small_in, 16 * N_SMALL)
                    pe.wait_ge(col_done, 1)
                    nc.tensor.transpose(bank[4][:, 0:NROWS], vec_rows[:, :], ident[0:NROWS, 0:NROWS]).then_inc(col_tr, 1)
                    for j in range(2):
                        t, w = at["tile"] + j, (T, BIASW - T)[j]
                        free_bank(t)
                        mm(bank[t % 4][0:DSA_HEADS, 0:w], relb[:, :], onehot[:, T * j:T * j + w], start=True, stop=True)\
                            .then_inc(tile_done, 1)
                if kind == "attention_1":
                    n_attn += 1
                    for j in range(4):
                        free_bank(at["tile"] + j)
                    pe.wait_ge(aux_free, at["aux"])
                    pe.wait_ge(lam_done, 1)
                    pe.wait_ge(hid_done, 4)
                    attend("diff", compress)
                    pe.wait_ge(stack_lo_done, stacked("dsa", 0))
                    attend("nsa", compressed_ready)
                if kind == "index":
                    pe.wait_ge(aux_free, at["aux"])
                    pe.wait_ge(sc_evac, at["sc"])
                    pe.wait_ge(ve_evac, at["ve"])
                    r = 0
                    for i in range(1, NT):
                        for h in range(DSA_HEADS):
                            w = P * (i + 1)
                            if r >= 3:
                                pe.wait_ge(ix_relu, r - 2)
                            mm(bank[4 + r % 3][:, 0:w], iq[:, h // 2, h % 2, P * i:P * i + P], ik2[:, 0:w],
                               start=True, stop=True).then_inc(ix_s, 1)
                            r += 1
                if kind == "attention_2":
                    n_attn += 1
                    for j in range(4):
                        free_bank(at["tile"] + j)
                    pe.wait_ge(ix_relu, 3 * DSA_HEADS)
                    attend("dsa", dsa_stacks)
                if kind == "ffn":
                    t0, s0 = at["tile"], at["split"]

                    def ffn_step(f, first=False):
                        for j in range(2):
                            pe.wait_ge(lo_done, f * 2 + (s0 + j + 1))
                            hi = w_hi[:, ffn_ring[j], :].rearrange("p (k c) -> p k c", c=256)
                            lo = w_lo[:, ffn_ring[j], :].rearrange("p (k c) -> p k c", c=256)
                            for m in range(2):
                                if first:
                                    free_bank(t0 + 2 * j + m)
                                else:
                                    pe.wait_ge((gsilu, act_done)[j], f * 2 + (m - 1))
                                for k in range(ND):
                                    if first and j == 0 and m == 0:
                                        pe.wait_ge(h_lo_done, at["h"] - ND + k + 1)
                                    ins = three(bank[(t0 + 2 * j + m) % 4][:, :],
                                                (hi[:, k, P * m:P * m + P], lo[:, k, P * m:P * m + P]),
                                                (h_hi[:, k, :], h_lo[:, k, :]), k == 0, k == ND - 1)
                                ins.then_inc(tile_done, 1)

                    ffn_step(0, first=True)
                    with pe.Fori(1, FFN_STEPS) as f:
                        ffn_step(f)
                    fresh[0] = None


_INS = ["x", "norm_g", "w_in", "diff_q_norm_g", "diff_k_norm_g", "diff_lambda_q1", "diff_lambda_k1",
        "diff_lambda_q2", "diff_lambda_k2", "diff_subln_g", "nsa_q_norm_g", "nsa_k_norm_g", "cmp_pos", "cmp_w1",
        "cmp_b1", "cmp_w2", "w_out", "g_mix_2", "w_in_2", "b_gate_2", "conv_w_2", "w_branch_a_2", "w_branch_b_2",
        "w_out_2", "rel_bias_2", "g_ffn_2", "w_ffn_gate_2", "w_ffn_up_2", "w_ffn_down_2", "g_final_2"]


def kernel(**inputs):
    import concourse.bacc as bacc
    from concourse.bass_utils import run_bass_kernel_spmd

    nc = bacc.Bacc("TRN2", target_bir_lowering=False, num_devices=1)
    arrays = {name: np.ascontiguousarray(inputs[name]) for name in _INS}
    arrays["g_final_2"] = arrays["g_final_2"].reshape(1, D)
    arrays["const"], arrays["distance"], arrays["onehot"] = shape_constants()
    ins = {name: nc.dram_tensor(f"in_{name}", x.shape, mybir.dt.from_np(x.dtype), kind="ExternalInput").ap()
           for name, x in arrays.items()}
    out = nc.dram_tensor("out_0", (1, T, D), mybir.dt.float32, kind="ExternalOutput").ap()
    build(nc, ins, out)
    r = run_bass_kernel_spmd(nc, [{f"in_{name}": x for name, x in arrays.items()}], core_ids=[0])
    return r.results[0]["out_0"]
```
